# Optimizing a Trainium2 kernel written in Bass

```python
import math
import jax, jax.numpy as jnp
from jax import lax
import numpy as np

D_MODEL = 1024
BATCH = 1
SEQ = 256
DEPTH = 2

EPS = 1e-6
A_GROUPS = 4
A_GROUP_DIM = 128
A_CHUNK = 128
A_WIDTH = A_GROUPS * A_GROUP_DIM
B_WINDOWS = (2, 4, 8, 16)
B_GROUPS = 4
B_GROUP_DIM = 128
B_WIDTH = B_GROUPS * B_GROUP_DIM
C_HEADS = 8
C_HEAD = 64
C_WIDTH = C_HEADS * C_HEAD
C_DECAY_LORA = 64
C_AAA_LORA = 64
C_GATE_LORA = 128
C_LORA = C_DECAY_LORA + C_AAA_LORA + C_GATE_LORA
C_PROJ = 3 * C_WIDTH + C_LORA
C_GN_EPS = 64e-5
D_HEADS = 8
D_HEAD = 64
D_WIDTH = D_HEADS * D_HEAD
D_GROUPS = 2
D_STATE = 128
D_CONV = 4
D_CHUNK = 128
D_CONV_DIM = D_WIDTH + 2 * D_GROUPS * D_STATE
N_BRANCH = 4
BRANCH_WIDTH = 512
IN_SPLITS = (2 * A_WIDTH, B_WIDTH, C_PROJ, D_WIDTH, D_CONV_DIM, D_HEADS, N_BRANCH * D_MODEL)
IN_DIM = sum(IN_SPLITS)
D_FF = 3584
N_EXPERTS = 8
TOP_K = 2
N_DENSE = (DEPTH + 1) // 2
N_MOE = DEPTH // 2

kernel_name = 'hybrid_gated_4mixer_moe_trunk'

F32 = jnp.float32

def split_cols(z, sizes):
    out, start = [], 0
    for s in sizes:
        out.append(z[..., start:start + s])
        start += s
    return out

def rmsnorm(x, g):
    xf = x.astype(F32)
    y = xf * lax.rsqrt(jnp.mean(xf * xf, axis=-1, keepdims=True) + EPS)
    return (y * g).astype(x.dtype)

def token_shift(x):
    return jnp.pad(x, ((0, 0), (1, 0), (0, 0)))[:, :-1]

def causal_depthwise_conv(x, w, b):
    k_w, ch = w.shape
    y = lax.conv_general_dilated(x, w[:, None, :], window_strides=(1,), padding=[(k_w - 1, 0)],
                                 dimension_numbers=('NWC', 'WIO', 'NWC'), feature_group_count=ch)
    return y + b

def mixer_spatial_gating(uv, ln_g, ln_b, w_s, b_s):
    bsz, t_len, _ = uv.shape
    u, v = jnp.split(jax.nn.gelu(uv), 2, axis=-1)
    vf = v.astype(F32)
    mu = jnp.mean(vf, axis=-1, keepdims=True)
    var = jnp.mean(jnp.square(vf - mu), axis=-1, keepdims=True)
    v = ((vf - mu) * lax.rsqrt(var + EPS) * ln_g + ln_b).astype(uv.dtype)
    v = v.reshape(bsz, t_len // A_CHUNK, A_CHUNK, A_GROUPS, A_GROUP_DIM)
    causal = jnp.tril(jnp.ones((A_CHUNK, A_CHUNK), dtype=bool))
    w = jnp.where(causal, w_s, jnp.zeros_like(w_s))
    v = jnp.einsum('gts,bcsge->bctge', w, v) + b_s.T[None, None, :, :, None]
    return u * v.reshape(bsz, t_len, A_WIDTH)

def mixer_pool(p, w_pool, scale):
    bsz, t_len, _ = p.shape
    pf = p.astype(F32)
    cs = jnp.pad(jnp.cumsum(pf, axis=1), ((0, 0), (1, 0), (0, 0)))
    count = jnp.arange(1, t_len + 1, dtype=F32)[None, :, None]
    outs = []
    for gi, win in enumerate(B_WINDOWS):
        sl = slice(gi * B_GROUP_DIM, (gi + 1) * B_GROUP_DIM)
        c = cs[:, :, sl]
        hi = c[:, 1:]
        lo = jnp.pad(c[:, :t_len + 1 - win], ((0, 0), (win - 1, 0), (0, 0)))
        mean = (hi - lo) / jnp.minimum(count, float(win))
        outs.append(mean - pf[:, :, sl])
    pooled = jnp.stack(outs, axis=2).astype(p.dtype)
    y = jnp.einsum('btge,gef->btgf', pooled, w_pool).reshape(bsz, t_len, B_WIDTH)
    return y * scale

def rwkv7_step(state, inp):
    r_t, w_t, k_t, v_t, kk_t, b_t = inp
    s_kk = jnp.einsum('bhvk,bhk->bhv', state, kk_t)
    state = state * w_t[:, :, None, :] - s_kk[..., None] * b_t[:, :, None, :] + v_t[..., None] * k_t[:, :, None, :]
    return state, jnp.einsum('bhvk,bhk->bhv', state, r_t)

def mixer_rwkv7(zc, mix, w0, w2, a0, a2, g2, k_k, k_a, r_k, ln_g, ln_b):
    bsz, t_len, _ = zc.shape
    zc = zc + (token_shift(zc) - zc) * mix
    r, k, v, lw, la, lg = split_cols(zc, (C_WIDTH, C_WIDTH, C_WIDTH, C_DECAY_LORA, C_AAA_LORA, C_GATE_LORA))
    w_log = -jax.nn.softplus(-(w0 + jnp.tanh(lw) @ w2).astype(F32)) - 0.5
    decay = jnp.exp(-jnp.exp(w_log))
    a = jax.nn.sigmoid((a0 + la @ a2).astype(F32))
    g = jax.nn.sigmoid(lg) @ g2
    heads = lambda t: t.astype(F32).reshape(bsz, t_len, C_HEADS, C_HEAD)
    r, k, v, a, decay = heads(r), heads(k), heads(v), heads(a), heads(decay)
    kk = k * k_k.astype(F32).reshape(C_HEADS, C_HEAD)
    kk = kk / jnp.maximum(jnp.linalg.norm(kk, axis=-1, keepdims=True), 1e-12)
    k = k * (1.0 + (a - 1.0) * k_a.astype(F32).reshape(C_HEADS, C_HEAD))
    tm = lambda t: jnp.moveaxis(t, 1, 0)
    s0 = jnp.zeros((bsz, C_HEADS, C_HEAD, C_HEAD), F32)
    _, o = lax.scan(rwkv7_step, s0, (tm(r), tm(decay), tm(k), tm(v), tm(kk), tm(kk * a)))
    o = jnp.moveaxis(o, 0, 1)
    mu = jnp.mean(o, axis=-1, keepdims=True)
    var = jnp.mean(jnp.square(o - mu), axis=-1, keepdims=True)
    o = ((o - mu) * lax.rsqrt(var + C_GN_EPS)).reshape(bsz, t_len, C_WIDTH) * ln_g + ln_b
    bonus = jnp.sum(r * k * r_k.astype(F32), axis=-1, keepdims=True) * v
    o = o + bonus.reshape(bsz, t_len, C_WIDTH)
    return (o * g).astype(zc.dtype)

def ssd_chunked(xh, dt, a_head, bm, cm):
    bsz, t_len, n_h, p_dim = xh.shape
    nc, lc, ng, ne, ns = t_len // D_CHUNK, D_CHUNK, D_GROUPS, n_h // D_GROUPS, D_STATE
    xd = (xh * dt[..., None]).reshape(bsz, nc, lc, ng, ne, p_dim)
    a = (dt * a_head).reshape(bsz, nc, lc, ng, ne).transpose(0, 3, 4, 1, 2)
    bc = bm.reshape(bsz, nc, lc, ng, ns)
    cc = cm.reshape(bsz, nc, lc, ng, ns)
    a_cs = jnp.cumsum(a, axis=-1)
    causal = jnp.tril(jnp.ones((lc, lc), dtype=bool))
    seg = a_cs[..., :, None] - a_cs[..., None, :]
    decay_in = jnp.exp(jnp.where(causal, seg, -jnp.inf))
    cb = jnp.einsum('bclgn,bcsgn->bgcls', cc, bc)
    y_diag = jnp.einsum('bgcls,bgecls,bcsgep->bclgep', cb, decay_in, xd)
    decay_to_end = jnp.exp(a_cs[..., -1:] - a_cs)
    states = jnp.einsum('bclgn,bgecl,bclgep->cbgepn', bc, decay_to_end, xd)
    chunk_decay = jnp.exp(a_cs[..., -1]).transpose(3, 0, 1, 2)

    def carry_step(h, inp):
        s_c, d_c = inp
        return h * d_c[..., None, None] + s_c, h

    h0 = jnp.zeros(states.shape[1:], states.dtype)
    _, prev = lax.scan(carry_step, h0, (states, chunk_decay))
    y_off = jnp.einsum('bclgn,cbgepn,bgecl->bclgep', cc, prev, jnp.exp(a_cs))
    return (y_diag + y_off).reshape(bsz, t_len, n_h, p_dim)

def mixer_ssd(zg, xbc, dt_raw, conv_w, conv_b, dt_bias, a_log, d_skip, norm_g):
    bsz, t_len, _ = xbc.shape
    xbc = jax.nn.silu(causal_depthwise_conv(xbc, conv_w, conv_b))
    xs, bm, cm = split_cols(xbc, (D_WIDTH, D_GROUPS * D_STATE, D_GROUPS * D_STATE))
    xh = xs.astype(F32).reshape(bsz, t_len, D_HEADS, D_HEAD)
    dt = jax.nn.softplus(dt_raw.astype(F32) + dt_bias)
    a_head = -jnp.exp(a_log.astype(F32))
    y = ssd_chunked(xh, dt, a_head,
                    bm.astype(F32).reshape(bsz, t_len, D_GROUPS, D_STATE),
                    cm.astype(F32).reshape(bsz, t_len, D_GROUPS, D_STATE))
    y = y + d_skip[:, None] * xh
    y = y.reshape(bsz, t_len, D_WIDTH) * jax.nn.silu(zg.astype(F32))
    return rmsnorm(y, norm_g).astype(zg.dtype)

def swiglu(h, wg, wu, wd):
    return (jax.nn.silu(h @ wg) * (h @ wu)) @ wd

def moe_swiglu(h, router, wg, wu, wd):
    logits = jnp.einsum('btd,de->bte', h, router).astype(F32)
    top_v, top_i = lax.top_k(logits, TOP_K)
    probs = jax.nn.softmax(top_v, axis=-1)
    combine = jnp.sum(jax.nn.one_hot(top_i, N_EXPERTS, dtype=F32) * probs[..., None], axis=-2)
    out = jnp.zeros_like(h)
    for e in range(N_EXPERTS):
        out = out + swiglu(h, wg[e], wu[e], wd[e]) * combine[..., e:e + 1].astype(h.dtype)
    return out

def setup_inputs(seed: int = 0) -> dict:
    key = jax.random.key(seed)
    ks = iter(jax.random.split(key, 48))
    nrm = lambda shape, s: jax.random.normal(next(ks), shape, F32) * s
    L = DEPTH
    x = nrm((BATCH, SEQ, D_MODEL), 1.0)
    norm_mix_g = 1.0 + nrm((L, D_MODEL), 0.02)
    w_in = nrm((L, D_MODEL, IN_DIM), D_MODEL ** -0.5)
    a_ln_g = 1.0 + nrm((L, A_WIDTH), 0.02)
    a_ln_b = nrm((L, A_WIDTH), 0.02)
    a_w_s = nrm((L, A_GROUPS, A_CHUNK, A_CHUNK), A_CHUNK ** -0.5)
    a_b_s = 1.0 + nrm((L, A_GROUPS, A_CHUNK), 0.1)
    b_w_pool = nrm((L, B_GROUPS, B_GROUP_DIM, B_GROUP_DIM), B_GROUP_DIM ** -0.5)
    b_scale = 1.0 + nrm((L, B_WIDTH), 0.1)
    c_mix = jax.random.uniform(next(ks), (L, C_PROJ), F32)
    c_w0 = jax.random.uniform(next(ks), (L, C_WIDTH), F32, -6.5, -1.5)
    c_w2 = nrm((L, C_DECAY_LORA, C_WIDTH), 0.1)
    c_a0 = nrm((L, C_WIDTH), 0.1)
    c_a2 = nrm((L, C_AAA_LORA, C_WIDTH), 0.1)
    c_g2 = nrm((L, C_GATE_LORA, C_WIDTH), C_GATE_LORA ** -0.5)
    c_k_k = 0.85 + nrm((L, C_WIDTH), 0.02)
    c_k_a = 1.0 + nrm((L, C_WIDTH), 0.02)
    c_r_k = nrm((L, C_HEADS, C_HEAD), 0.1)
    c_ln_g = 1.0 + nrm((L, C_WIDTH), 0.02)
    c_ln_b = nrm((L, C_WIDTH), 0.02)
    d_conv_w = nrm((L, D_CONV, D_CONV_DIM), D_CONV ** -0.5)
    d_conv_b = nrm((L, D_CONV_DIM), 0.02)
    dt0 = jnp.exp(jax.random.uniform(next(ks), (L, D_HEADS), F32, math.log(1e-3), math.log(1e-1)))
    d_dt_bias = dt0 + jnp.log(-jnp.expm1(-dt0))
    d_a_log = jnp.log(jax.random.uniform(next(ks), (L, D_HEADS), F32, 1.0, 16.0))
    d_skip = 1.0 + nrm((L, D_HEADS), 0.1)
    d_norm_g = 1.0 + nrm((L, D_WIDTH), 0.02)
    w_branch = nrm((L, N_BRANCH, BRANCH_WIDTH, D_MODEL), BRANCH_WIDTH ** -0.5)
    w_out = nrm((L, D_MODEL, D_MODEL), D_MODEL ** -0.5)
    norm_ffn_g = 1.0 + nrm((L, D_MODEL), 0.02)
    ffn_w_gate = nrm((N_DENSE, D_MODEL, D_FF), D_MODEL ** -0.5)
    ffn_w_up = nrm((N_DENSE, D_MODEL, D_FF), D_MODEL ** -0.5)
    ffn_w_down = nrm((N_DENSE, D_FF, D_MODEL), D_FF ** -0.5)
    moe_router = nrm((N_MOE, D_MODEL, N_EXPERTS), D_MODEL ** -0.5)
    moe_w_gate = nrm((N_MOE, N_EXPERTS, D_MODEL, D_FF), D_MODEL ** -0.5)
    moe_w_up = nrm((N_MOE, N_EXPERTS, D_MODEL, D_FF), D_MODEL ** -0.5)
    moe_w_down = nrm((N_MOE, N_EXPERTS, D_FF, D_MODEL), D_FF ** -0.5)
    norm_final_g = 1.0 + nrm((D_MODEL,), 0.02)
    return {'x': x, 'norm_mix_g': norm_mix_g, 'w_in': w_in,
            'a_ln_g': a_ln_g, 'a_ln_b': a_ln_b, 'a_w_s': a_w_s, 'a_b_s': a_b_s,
            'b_w_pool': b_w_pool, 'b_scale': b_scale,
            'c_mix': c_mix, 'c_w0': c_w0, 'c_w2': c_w2, 'c_a0': c_a0, 'c_a2': c_a2, 'c_g2': c_g2,
            'c_k_k': c_k_k, 'c_k_a': c_k_a, 'c_r_k': c_r_k, 'c_ln_g': c_ln_g, 'c_ln_b': c_ln_b,
            'd_conv_w': d_conv_w, 'd_conv_b': d_conv_b, 'd_dt_bias': d_dt_bias, 'd_a_log': d_a_log,
            'd_skip': d_skip, 'd_norm_g': d_norm_g,
            'w_branch': w_branch, 'w_out': w_out, 'norm_ffn_g': norm_ffn_g,
            'ffn_w_gate': ffn_w_gate, 'ffn_w_up': ffn_w_up, 'ffn_w_down': ffn_w_down,
            'moe_router': moe_router, 'moe_w_gate': moe_w_gate, 'moe_w_up': moe_w_up, 'moe_w_down': moe_w_down,
            'norm_final_g': norm_final_g}

def reference(x, norm_mix_g, w_in, a_ln_g, a_ln_b, a_w_s, a_b_s, b_w_pool, b_scale,
              c_mix, c_w0, c_w2, c_a0, c_a2, c_g2, c_k_k, c_k_a, c_r_k, c_ln_g, c_ln_b,
              d_conv_w, d_conv_b, d_dt_bias, d_a_log, d_skip, d_norm_g,
              w_branch, w_out, norm_ffn_g, ffn_w_gate, ffn_w_up, ffn_w_down,
              moe_router, moe_w_gate, moe_w_up, moe_w_down, norm_final_g):
    bsz, t_len, _ = x.shape
    for l in range(DEPTH):
        h = rmsnorm(x, norm_mix_g[l])
        z = h @ w_in[l]
        z_a, z_b, z_c, z_dz, z_dxbc, z_ddt, z_g = split_cols(z, IN_SPLITS)
        y_a = mixer_spatial_gating(z_a, a_ln_g[l], a_ln_b[l], a_w_s[l], a_b_s[l])
        y_b = mixer_pool(z_b, b_w_pool[l], b_scale[l])
        y_c = mixer_rwkv7(z_c, c_mix[l], c_w0[l], c_w2[l], c_a0[l], c_a2[l], c_g2[l],
                          c_k_k[l], c_k_a[l], c_r_k[l], c_ln_g[l], c_ln_b[l])
        y_d = mixer_ssd(z_dz, z_dxbc, z_ddt, d_conv_w[l], d_conv_b[l], d_dt_bias[l],
                        d_a_log[l], d_skip[l], d_norm_g[l])
        branches = jnp.stack([y_a, y_b, y_c, y_d], axis=2)
        proj = jnp.einsum('btkc,kcd->btkd', branches, w_branch[l])
        gates = jax.nn.sigmoid(z_g.astype(F32)).reshape(bsz, t_len, N_BRANCH, D_MODEL).astype(x.dtype)
        merged = jnp.sum(gates * proj, axis=2)
        x = x + merged @ w_out[l]
        h = rmsnorm(x, norm_ffn_g[l])
        if l % 2 == 0:
            i = l // 2
            x = x + swiglu(h, ffn_w_gate[i], ffn_w_up[i], ffn_w_down[i])
        else:
            i = l // 2
            x = x + moe_swiglu(h, moe_router[i], moe_w_gate[i], moe_w_up[i], moe_w_down[i])
    return rmsnorm(x, norm_final_g)


_drawn_inputs = setup_inputs


def setup_inputs(seed=0):
    import zlib

    import numpy as np

    out = dict(_drawn_inputs(seed))
    spreads = {}
    factors = {'a_ln_g': 7.618,
     'a_ln_b': 19.559,
     'c_w2': 3.808,
     'c_k_k': 17.387,
     'c_k_a': 7.959,
     'c_ln_g': 13.368,
     'c_ln_b': 11.775,
     'norm_final_g': 7.176,
     'd_conv_b': 5.29,
     'd_norm_g': 5.83,
     'norm_ffn_g': 4.179}
    for name, (base, spread) in spreads.items():
        noise = np.random.default_rng([zlib.crc32(name.encode()), seed]).standard_normal(out[name].shape)
        drawn = base * np.exp(spread * noise) if base else spread * noise
        out[name] = __import__('jax').numpy.asarray(drawn.astype(out[name].dtype))
    for name, factor in factors.items():
        out[name] = (out[name] * factor).astype(out[name].dtype)
    return out
```

```python
from contextlib import ExitStack

import concourse.bass as bass
from concourse import mybir

F32 = mybir.dt.float32
ALU = mybir.AluOpType
ACT = mybir.ActivationFunctionType
AX_X = mybir.AxisListType.X

P = 128
T = 256
D = 1024
DT = D // P
L = 2
NCH = T // P
FF = 3584
FT = FF // P
E = 8
H = 8
HEADS = [0, 2, 4, 6, 1, 3, 5, 7]
CT = 14
BLK = 16
CW = BLK * P
RING = 7
EPS = 1e-6
GN_EPS = 64e-5
DECAY = 0.6065306597126334
FLOOR = 1e-24

Z_UNITS = [("zg", 0), ("zg", 1), ("xbc", 0), ("xbc", 1), ("xbc", 2), ("xbc", 3), ("v", 0), ("v", 1), ("u", 0), ("u", 1),
           ("b", 0), ("b", 1)] + [("c", i) for i in range(CT // 2)]
NZ = len(Z_UNITS)
N_MERGE = 3 * DT
N_OUT = DT // 2
N_MIX = NZ + N_MERGE + N_OUT
N_GU = FT
N_DOWN = DT * FT // BLK
N_FFN = N_GU + N_DOWN
FFN0 = N_MIX
MIX1 = N_MIX + N_FFN
MOE0 = MIX1 + N_MIX
N_CHUNKS = MOE0 + E * N_FFN

PP_LIST = [("norm_mix", 8), ("norm_ffn", 8), ("mix", 14), ("w0", 4), ("a0", 4), ("k_k", 4), ("k_a", 4), ("r_k", 4),
           ("ln_g", 4), ("ln_b", 4), ("conv_w", 32), ("conv_b", 8), ("norm_d", 4), ("skip", 4), ("b_scale", 4),
           ("norm_final", 8), ("dt_bias", 1), ("a_log", 1)]
PP, _n = {}, 0
for _name, _k in PP_LIST:
    PP[_name] = _n
    _n += _k
NPP = _n
LEVELS = 6
CC_LIST = [("ident", P), ("ones", P), ("heads", P), ("strict_up", P), ("incl_up", P), ("low2", P), ("up2", P),
           ("off", LEVELS * P), ("count", 4 * T), ("reset", 4 * T), ("sel", H * P), ("eps", 1), ("gn_eps", 1)]
CC, _n = {}, 0
for _name, _k in CC_LIST:
    CC[_name] = _n
    _n += _k
NCC = _n
SW_LIST = [("w_s", 512), ("pool", 512), ("w2a2", 512), ("g2", 512), ("dt", 64), ("router", 64)]
SW, _n = {}, 0
for _name, _k in SW_LIST:
    SW[_name] = _n
    _n += _k
NSW = _n
NREP = 3 * 512

M_USES = ([("norm1", 0), ("dt", 1), ("cb", 2), ("xt0", 3), ("xt1", 0), ("bt", 1), ("dtT", 2)]
          + [(f"row{i}", (3 + i) % 4) for i in range(4)]
          + [("st", 3), ("yd0", 0), ("yd1", 1), ("dn", 2), ("a0", 3), ("a1", 0), ("b0", 1), ("b1", 2)]
          + [("cw0", 3), ("cw1", 0), ("ca0", 1), ("ca1", 2), ("cg0", 3), ("cg1", 0), ("ss0", 1), ("ss1", 2),
             ("bo0", 3), ("bo1", 0), ("vt0", 1), ("vt1", 2), ("kt", 3), ("nt", 0)])
for _c in range(NCH):
    M_USES += [(f"n0{_c}", 1), (f"n1{_c}", 2)] + [(f"s{_h}{_c}", (3 + _h) % 4) for _h in range(H)]
    for _v in range(LEVELS):
        M_USES += [(f"t0{_v}{_c}", 0), (f"t1{_v}{_c}", 1)]
        if _v < LEVELS - 1:
            M_USES += [(f"x0{_v}{_c}", 2)]
        M_USES += [(f"z0{_v}{_c}", 3)]
        if _v < LEVELS - 1:
            M_USES += [(f"x1{_v}{_c}", 0)]
        M_USES += [(f"z1{_v}{_c}", 1)]
    M_USES += [(f"W0{_c}", 2), (f"W1{_c}", 1), (f"U{_c}", 3), (f"O{_c}", 0)]
    if _c == 0:
        M_USES += [("S", 1)]
M_USES += [("mu0", 1), ("mu1", 2), ("va0", 3), ("va1", 0)]
M_USES += [(f"pj{_d}{_i}", 2 * (_d % 2) + _i) for _d in range(DT) for _i in range(2)]
M_USES += [("norm2", 0)]
G_USES = [((u, i), n % 4) for n, (u, i) in enumerate(Z_UNITS)]
G_USES += [(("gate", _d, _i), 2 * (_d % 2) + _i) for _d in range(DT) for _i in range(2)]
G_USES += [(("out", _i), _i) for _i in range(N_OUT)]


def bank_plan(uses):
    total, plan = [0] * 4, {}
    for stage, bank in uses:
        total[bank] += 1
        assert stage not in plan
        plan[stage] = (bank, total[bank])
    return plan, total


M_PLAN, M_TOTAL = bank_plan(M_USES)
F_PLAN, F_TOTAL = bank_plan([(s, b) for s, b in M_USES if not (s.startswith("pj") and s.endswith("1"))])
G_PLAN, G_TOTAL = bank_plan(G_USES)


def trunk(nc, x_in, stream, pp_in, cc_in, sw_in, rep_in, out):
    with ExitStack() as ctx:
        def sb(name, shape):
            return ctx.enter_context(nc.sbuf_tensor(name, shape, F32))

        def sem(name):
            return ctx.enter_context(nc.semaphore(name))

        x = sb("x", [P, DT, T])
        h = sb("h", [P, DT, T])
        ring = sb("ring", [P, RING, CW])
        cc = sb("cc", [P, NCC])
        pp = sb("pp", [P, L, NPP])
        sw = sb("sw", [P, NSW])
        rep = sb("rep", [P, NREP])
        rstd = sb("rstd", [P, T])
        rms = sb("rms", [P, T])
        small = sb("small", [P, 256])
        arena = sb("arena", [P, 25304])

        gbank = [ctx.enter_context(nc.psum_tensor(f"g{i}", [P, 512], F32)) for i in range(4)]
        mbank = [ctx.enter_context(nc.psum_tensor(f"m{i}", [P, 512], F32)) for i in range(4)]
        fbank = gbank + mbank

        def area(at, n):
            return arena[:, at:at + n]

        def tiles(at, n, w=T):
            return area(at, n * w).rearrange("p (n t) -> p n t", n=n)

        def const(name, n=P):
            return cc[:, CC[name]:CC[name] + n]

        def par(l, name, j=0, rows=P):
            return pp[0:rows, l, PP[name] + j:PP[name] + j + 1]

        def over(ap, n):
            return ap.unsqueeze(1).to_broadcast([ap.shape[0], n, ap.shape[1]])

        def along(ap, w):
            return ap.unsqueeze(2).to_broadcast([ap.shape[0], ap.shape[1], w])

        ident, ones, heads = const("ident"), const("ones"), const("heads")

        yA, yB, yC, yD = (tiles(i * 1024, 4) for i in range(4))
        zc = tiles(4096, CT, T + 1)
        zg = tiles(7696, 4)
        xbc = tiles(8720, 8, T + 3)
        vtok = tiles(10792, 2, 512)
        u = tiles(11816, 4)
        zb = tiles(12840, 4, T + 16)
        conv = tiles(13928, 8)
        dtw = area(15976, 1280)
        d_raw, d_abs, d_ln, d_dt, d_cs = (dtw[0:H, i * T:(i + 1) * T] for i in range(5))
        tok = area(17256, 32).rearrange("p (a c h) -> p a c h", a=2, c=NCH)
        d_end = area(17288, H)
        ahead = area(17296, 2)
        cbm = tiles(17400, 4, P)
        xd = tiles(18024, 2, 512)
        btok = tiles(19048, 2, P)
        xde = area(19304, 512)
        mT = tiles(19816, H, P)
        seg = tiles(20840, H, P)
        cs = tiles(21864, H, P)
        st = tiles(22888, 2, T)
        seg1 = tiles(2048, H, P)
        p2 = tiles(23400, 4, T + 16)
        p4 = tiles(24216, 4, T + 16)
        ar = area(13928, 2048).rearrange("p (j c a t) -> p j c a t", j=4, c=NCH, a=2)
        nb = tiles(15976, 4)
        ka = tiles(17000, 4)
        cv = tiles(18024, 2, 512)
        kbt = tiles(19048, 2, 512)
        sc = area(20072, 4096).rearrange("p (h a t) -> p h a t", h=H, a=4)
        s0 = rms[:, :].rearrange("p (j f) -> p j f", j=4)
        wb = area(24168, 512)
        ub = area(24680, 512)
        xx = tiles(7696, H, P)
        zz = tiles(8720, H, P)
        tt = tiles(9744, H, P)
        bv = tiles(10792, 4)
        gg = tiles(11816, 4)
        oo = tiles(12840, 4)
        dif = tiles(20072, CT)
        w_log, c_sum, aa, kk = (tiles(20072 + i * 1024, 4) for i in range(4))
        e_in, e_neg, e_ex = (tiles(7696 + i * 1024, 4) for i in range(3))
        k2 = tiles(24168, 4)
        tmp1 = tiles(18024, 4)
        tmp2 = tiles(19048, 4)
        sg = area(13928, 2048).rearrange("p (b f) -> p b f", b=2)
        mg = tiles(15976, DT)
        sq = tiles(13928, DT)
        gu = tiles(4096, FT)
        sil = tiles(11264, RING)
        crow = tiles(18024, E)
        moe_tmp = area(16000, 512)
        combT = area(17000, T)[0:E]
        rt = area(17400, 256)

        landed = [sem(f"landed{i}") for i in range(RING)]
        chunks_used = sem("chunks_used")
        g_drained = [sem(f"g_drained{i}") for i in range(4)]
        m_filled = [sem(f"m_filled{i}") for i in range(4)]
        m_drained = [sem(f"m_drained{i}") for i in range(4)]
        consts_in = sem("consts_in")
        x_loaded = sem("x_loaded")
        layer_in = sem("layer_in")
        padded = sem("padded")
        sq_ready = sem("sq_ready")
        h_ready = sem("h_ready")
        x_mixed = sem("x_mixed")
        ffn_drained = sem("ffn_drained")
        silu_done = sem("silu_done")
        v_seq = sem("v_seq")
        a_seq = sem("a_seq")
        p_seq = sem("p_seq")
        out_stored = sem("out_stored")
        S = {n: sem(n) for n in (
            "conv_done conv_silu dt_raw dt_exp dt_soft ahead_ready cs_ready tok_ready seg_ready seg_exp "
            "mt_ready xd_ready d_endraw d_endexp xde_ready cbm_ready er_ready csc_ready yd_ready ydsq "
            "v_stats v_std vn_ready wm_ready ya_ready pooled zc_mixed lora_ready w_sig a_sig "
            "cum_ready e_ready kr_ready krsq ss_ready ss_sqrt rk_ready ab_ready x0_ready sc_ready t_ready z_ready x_ready "
            "s0_ready cent osq yc_ready sg_ready mg_ready b_done logits_top probs comb_ready combT_ready crow_ready "
            "em_ready out_ready ffn_x").split()}

        def filled(eng, l, stage):
            bank, n = F_PLAN[stage]
            eng.wait_ge(m_filled[bank], l * F_TOTAL[bank] + n)

        def m_free(eng, l, stage):
            bank, n = M_PLAN[stage]
            if l * M_TOTAL[bank] + n > 1:
                eng.wait_ge(m_drained[bank], l * M_TOTAL[bank] + n - 1)

        def m_done(eng, l, stage):
            bank, n = M_PLAN[stage]
            eng.wait_ge(m_drained[bank], l * M_TOTAL[bank] + n)

        def g_free(eng, l, unit):
            bank, n = G_PLAN[unit]
            if l * G_TOTAL[bank] + n > 1:
                eng.wait_ge(g_drained[bank], l * G_TOTAL[bank] + n - 1)

        def g_done(eng, l, unit):
            bank, n = G_PLAN[unit]
            eng.wait_ge(g_drained[bank], l * G_TOTAL[bank] + n)

        def mb(stage):
            return mbank[M_PLAN[stage][0]]

        def gb(unit):
            return gbank[G_PLAN[unit][0]]

        def chunk0(l):
            return l * MIX1

        def unit_chunk(l, unit):
            c = chunk0(l)
            if unit == ("v", 0):
                unit = ("v", 1)
            if unit in Z_UNITS:
                return c + Z_UNITS.index(unit)
            if unit[0] == "gate":
                return c + NZ + 3 * unit[1] + unit[2]
            return c + NZ + N_MERGE + unit[1]

        class Count:
            def __init__(self, eng, own):
                self.eng, self.own, self.n = eng, own, {}

            def add(self, ins, s):
                ins.then_inc(s, 1)
                self.n[id(s)] = self.n.get(id(s), 0) + 1

            def step(self, ins, s=None):
                s = s or self.own
                self.add(ins, s)
                self.eng.wait_ge(s, self.n[id(s)])

        block = ctx.enter_context(nc.Block())

        @block.sync
        def _(sp):
            for s in range(RING):
                sp.dma_start(ring[:, s, :], stream[s]).then_inc(landed[s], 16)
            turns = N_CHUNKS // RING
            with sp.Fori(1, turns) as i:
                for s in range(RING):
                    sp.wait_ge(chunks_used, i * RING + (s - RING + 1))
                    sp.dma_start(ring[:, s, :], stream[i * RING + s]).then_inc(landed[s], 16)
            for n in range(turns * RING, N_CHUNKS):
                sp.wait_ge(chunks_used, n - RING + 1)
                sp.dma_start(ring[:, n % RING, :], stream[n]).then_inc(landed[n % RING], 16)

        @block.tensor
        def _(pe):
            pe.wait_ge(consts_in, 32)

            def mm(o, a, b, start=True, stop=True):
                return pe.matmul(o, a, b, start=start, stop=stop, skip_group_check=True)

            def chunk(n):
                pe.wait_ge(landed[n % RING], 16 * (n // RING + 1))
                return ring[:, n % RING, :].rearrange("p (b m) -> p b m", b=BLK)

            def fill(l, stage, last):
                last.then_inc(m_filled[M_PLAN[stage][0]], 1)

            def feature_sum(l, stage, mat, src, n, scale=1):
                m_free(pe, l, stage)
                for j in range(n):
                    last = mm(mb(stage)[:, 0:T], mat, src[:, j, :], j == 0, j == n - 1)
                fill(l, stage, last)

            def two_banks(l, name, lhs, rhs):
                for i in range(2):
                    m_free(pe, l, f"{name}{i}")
                    for j in (2 * i, 2 * i + 1):
                        last = mm(mb(f"{name}{i}")[:, (j % 2) * T:(j % 2 + 1) * T], lhs(j), rhs(j))
                    fill(l, f"{name}{i}", last)

            def turn(l, stage, parts):
                m_free(pe, l, stage)
                for i, src in enumerate(parts):
                    last = pe.transpose(mb(stage)[:, i * P:(i + 1) * P], src, ident)
                fill(l, stage, last)

            def project(l, lo, hi):
                for n in range(lo, hi):
                    name, i = Z_UNITS[n]
                    w = chunk(chunk0(l) + n)
                    if n == 0:
                        pe.wait_ge(h_ready, 2 * DT * l + DT)
                    if name == "v":
                        if i == 0:
                            g_free(pe, l, ("v", 0))
                            g_free(pe, l, ("v", 1))
                        wv = ring[:, (chunk0(l) + n) % RING, :].rearrange("p (k f) -> p k f", k=4)
                        for c in range(NCH):
                            for k in range(4):
                                last = mm(gb(("v", c))[:, :], h[:, 4 * i + k, c * P:(c + 1) * P], wv[:, k, :],
                                          i == 0 and k == 0, i == 1 and k == 3)
                    else:
                        g_free(pe, l, (name, i))
                        for j in range(2):
                            for k in range(DT):
                                last = mm(gb((name, i))[:, j * T:(j + 1) * T], w[:, DT * j + k, :], h[:, k, :],
                                          k == 0, k == DT - 1)
                    last.then_inc(chunks_used, 1)
                    if n == 1:
                        pe.wait_ge(layer_in, 32 * (l + 1))
                        m_free(pe, l, "dt")
                        for k in range(DT):
                            last = mm(mb("dt")[0:H, 0:T], sw[:, SW["dt"] + H * k:SW["dt"] + H * (k + 1)], h[:, k, :],
                                      k == 0, k == DT - 1)
                        fill(l, "dt", last)

            def mixer_d_rows(l):
                pe.wait_ge(S["conv_silu"], l + 1)
                m_free(pe, l, "cb")
                for g in range(2):
                    for c in range(NCH):
                        i = 2 * g + c
                        last = mm(mb("cb")[:, i * P:(i + 1) * P], conv[:, 4 + g, c * P:(c + 1) * P],
                                  conv[:, 6 + g, c * P:(c + 1) * P])
                fill(l, "cb", last)
                for c in range(NCH):
                    turn(l, f"xt{c}", [conv[:, j, c * P:(c + 1) * P] for j in range(4)])
                turn(l, "bt", [conv[:, 4 + g, 0:P] for g in range(2)])
                pe.wait_ge(S["cs_ready"], l + 1)
                m_free(pe, l, "dtT")
                for i, src in enumerate((d_dt, d_cs)):
                    for c in range(NCH):
                        last = pe.transpose(mb("dtT")[:, (2 * i + c) * H:(2 * i + c + 1) * H], src[:, c * P:(c + 1) * P],
                                            ident[0:H, 0:H])
                fill(l, "dtT", last)
                for i in range(4):
                    m_free(pe, l, f"row{i}")
                    for j in range(2):
                        hd = 2 * i + j
                        last = mm(mb(f"row{i}")[:, j * T:(j + 1) * T], cc[0:H, CC["sel"] + hd * P:CC["sel"] + (hd + 1) * P], d_cs)
                    fill(l, f"row{i}", last)

            def mixer_d_out(l):
                m_done(pe, l, "bt")
                pe.wait_ge(S["xde_ready"], l + 1)
                m_free(pe, l, "st")
                for g in range(2):
                    last = mm(mb("st")[:, g * T:(g + 1) * T], btok[:, g, :], xde[:, g * T:(g + 1) * T])
                fill(l, "st", last)
                for c in range(NCH):
                    pe.wait_ge(S["mt_ready"], 2 * (NCH * l + c + 1))
                    m_free(pe, l, f"yd{c}")
                    if c:
                        pe.wait_ge(S["csc_ready"], 2 * (l + 1))
                        m_done(pe, l, "st")
                    for hd in range(H):
                        q, j = 64 * (hd % 2), hd // 2
                        o = mb(f"yd{c}")[q:q + 64, j * P:(j + 1) * P]
                        last = mm(o, xd[:, c, hd * 64:(hd + 1) * 64], mT[:, hd, :], True, c == 0)
                        if c:
                            last = mm(o, st[:, hd // 4, (hd % 4) * 64:(hd % 4 + 1) * 64], cs[:, hd, :], False, True)
                    fill(l, f"yd{c}", last)

            def mixer_d_norm(l):
                pe.wait_ge(S["ydsq"], l + 1)
                feature_sum(l, "dn", ones, seg4, 4)

            seg4 = tiles(20840, 4)

            def mixer_a(l):
                pe.wait_ge(S["wm_ready"], l + 1)
                for c in range(NCH):
                    pe.wait_ge(S["vn_ready"], NCH * l + c + 1)
                    m_free(pe, l, f"a{c}")
                    for g in range(4):
                        last = mm(mb(f"a{c}")[:, g * P:(g + 1) * P], vtok[:, c, g * P:(g + 1) * P],
                                  sw[:, SW["w_s"] + g * P:SW["w_s"] + (g + 1) * P])
                    fill(l, f"a{c}", last)

            def mixer_b(l):
                pe.wait_ge(S["pooled"], l + 1)
                two_banks(l, "b", lambda j: sw[:, SW["pool"] + j * P:SW["pool"] + (j + 1) * P], lambda j: yB[:, j, :])

            def mixer_c(l):
                pe.wait_ge(S["lora_ready"], 2 * (l + 1))
                w2 = sw[0:64, SW["w2a2"]:SW["w2a2"] + 512]
                a2 = sw[64:P, SW["w2a2"]:SW["w2a2"] + 512]
                two_banks(l, "cw", lambda j: w2[:, j * P:(j + 1) * P], lambda j: zc[0:64, 12, 1:T + 1])
                two_banks(l, "ca", lambda j: a2[:, j * P:(j + 1) * P], lambda j: zc[64:P, 12, 1:T + 1])
                two_banks(l, "cg", lambda j: sw[:, SW["g2"] + j * P:SW["g2"] + (j + 1) * P], lambda j: zc[:, 13, 1:T + 1])
                pe.wait_ge(S["krsq"], l + 1)
                two_banks(l, "ss", lambda j: heads, lambda j: tmp1[:, j, :])
                pe.wait_ge(S["rk_ready"], l + 1)
                two_banks(l, "bo", lambda j: heads, lambda j: tmp2[:, j, :])
                for c in range(NCH):
                    turn(l, f"vt{c}", [zc[:, 8 + j, 1 + c * P:1 + (c + 1) * P] for j in range(4)])
                pe.wait_ge(S["ab_ready"], l + 1)
                turn(l, "kt", [ka[:, j, 0:P] for j in range(4)])
                turn(l, "nt", [nb[:, j, 0:P] for j in range(4)])
                for c in range(NCH):
                    tc = slice(c * P, (c + 1) * P)
                    half = lambda hd: slice(64 * (hd % 2), 64 * (hd % 2) + 64)
                    for q in range(2):
                        m_free(pe, l, f"n{q}{c}")
                        for i in range(4):
                            hd = HEADS[4 * q + i]
                            last = mm(mb(f"n{q}{c}")[:, i * P:(i + 1) * P], ar[half(hd), hd // 2, c, 0, :], nb[half(hd), hd // 2, tc])
                        fill(l, f"n{q}{c}", last)
                    for slot in range(H):
                        hd, st_ = HEADS[slot], f"s{slot}{c}"
                        m_free(pe, l, st_)
                        both = ar[half(hd), hd // 2, c, :, :].rearrange("p a t -> p (a t)")
                        mm(mb(st_)[:, 0:T], nb[half(hd), hd // 2, tc], both)
                        last = mm(mb(st_)[:, T:2 * T], ka[half(hd), hd // 2, tc], both)
                        fill(l, st_, last)
                    for v in range(LEVELS):
                        base = (NCH * l + c) * LEVELS + v
                        for q in range(2):
                            pe.wait_ge(S["x_ready"], 2 * base + q + 1)
                            if v == 0:
                                pe.wait_ge(S["sc_ready"], H * (NCH * l + c) + 4 * q + 4)
                            m_free(pe, l, f"t{q}{v}{c}")
                            for i in range(4):
                                s_ = 4 * q + i
                                last = mm(mb(f"t{q}{v}{c}")[:, i * P:(i + 1) * P], sc[:, s_, 0, :], xx[:, s_, :])
                            fill(l, f"t{q}{v}{c}", last)
                        for q in range(2):
                            pe.wait_ge(S["z_ready"], 2 * base + 2 * (NCH * l + c) + q + 1)
                            pe.wait_ge(S["t_ready"], 2 * base + q + 1)
                            if v < LEVELS - 1:
                                m_free(pe, l, f"x{q}{v}{c}")
                                for i in range(4):
                                    s_ = 4 * q + i
                                    last = mm(mb(f"x{q}{v}{c}")[:, i * P:(i + 1) * P], zz[:, s_, :], tt[:, s_, :])
                                fill(l, f"x{q}{v}{c}", last)
                            m_free(pe, l, f"z{q}{v}{c}")
                            for i in range(4):
                                s_ = 4 * q + i
                                last = mm(mb(f"z{q}{v}{c}")[:, i * P:(i + 1) * P], tt[:, s_, :], zz[:, s_, :])
                            fill(l, f"z{q}{v}{c}", last)
                    if c == 0:
                        m_done(pe, l, "vt0")
                        m_done(pe, l, "vt1")
                    else:
                        pe.wait_ge(S["s0_ready"], l + 1)
                    for q in range(2):
                        m_free(pe, l, f"W{q}{c}")
                        for i in range(4):
                            slot = 4 * q + i
                            hd = HEADS[slot]
                            o = mb(f"W{q}{c}")[:, i * 64:(i + 1) * 64]
                            last = mm(o, sc[:, slot, 2, :], cv[:, c, hd * 64:(hd + 1) * 64], True, c == 0)
                            if c:
                                last = mm(o, ar[half(hd), hd // 2, c, 0, :], s0[half(hd), hd // 2, :], False, True)
                        fill(l, f"W{q}{c}", last)
                    pe.wait_ge(S["z_ready"], 2 * (LEVELS + 1) * (NCH * l + c + 1))
                    m_done(pe, l, f"W0{c}")
                    m_done(pe, l, f"W1{c}")
                    m_free(pe, l, f"U{c}")
                    for slot, hd in enumerate(HEADS):
                        last = mm(mb(f"U{c}")[:, hd * 64:(hd + 1) * 64], zz[:, slot, :], wb[:, slot * 64:(slot + 1) * 64])
                    fill(l, f"U{c}", last)
                    m_done(pe, l, f"U{c}")
                    m_free(pe, l, f"O{c}")
                    for slot, hd in enumerate(HEADS):
                        o = mb(f"O{c}")[half(hd), (hd // 2) * P:(hd // 2 + 1) * P]
                        mm(o, cv[:, c, hd * 64:(hd + 1) * 64], sc[:, slot, 3, :], True, False)
                        last = mm(o, ub[:, hd * 64:(hd + 1) * 64], sc[:, slot, 1, :], False, c == 0)
                        if c:
                            last = mm(o, s0[half(hd), hd // 2, :], ar[half(hd), hd // 2, c, 1, :], False, True)
                    fill(l, f"O{c}", last)
                    if c == 0:
                        m_done(pe, l, "kt")
                        m_done(pe, l, "nt")
                        m_free(pe, l, "S")
                        for hd in range(H):
                            o = mb("S")[half(hd), (hd // 2) * 64:(hd // 2 + 1) * 64]
                            mm(o, kbt[:, 0, hd * 64:(hd + 1) * 64], cv[:, 0, hd * 64:(hd + 1) * 64], True, False)
                            last = mm(o, kbt[:, 1, hd * 64:(hd + 1) * 64], ub[:, hd * 64:(hd + 1) * 64], False, True)
                        fill(l, "S", last)
                m_done(pe, l, "O1")
                two_banks(l, "mu", lambda j: heads, lambda j: oo[:, j, :])
                pe.wait_ge(S["osq"], l + 1)
                two_banks(l, "va", lambda j: heads, lambda j: tiles(7696, 4)[:, j, :])

            ys = [yA, yB, yC, yD]

            def merge(l):
                for d in range(DT):
                    c = chunk0(l) + NZ + 3 * d
                    for i in range(2):
                        w = chunk(c + i)
                        g_free(pe, l, ("gate", d, i))
                        for j in range(2):
                            for k in range(DT):
                                last = mm(gb(("gate", d, i))[:, j * T:(j + 1) * T], w[:, DT * j + k, :], h[:, k, :],
                                          k == 0, k == DT - 1)
                        last.then_inc(chunks_used, 1)
                    w = chunk(c + 2)
                    if d == 0:
                        pe.wait_ge(S["ya_ready"], NCH * (l + 1))
                        m_done(pe, l, "b0")
                        m_done(pe, l, "b1")
                        pe.wait_ge(S["yd_ready"], 4 * (l + 1))
                        pe.wait_ge(S["yc_ready"], l + 1)
                    for i in range(2):
                        m_free(pe, l, f"pj{d}{i}")
                        for j in range(2):
                            for k in range(4):
                                last = mm(mb(f"pj{d}{i}")[:, j * T:(j + 1) * T], w[:, 4 * (2 * i + j) + k, :],
                                          ys[2 * i + j][:, k, :], k == 0, k == 3)
                        if i == 0:
                            fill(l, f"pj{d}{i}", last)
                    last.then_inc(chunks_used, 1)
                for i in range(N_OUT):
                    w = chunk(chunk0(l) + NZ + N_MERGE + i)
                    if i == 0:
                        pe.wait_ge(S["mg_ready"], DT * (l + 1))
                    g_free(pe, l, ("out", i))
                    for j in range(2):
                        for k in range(DT):
                            last = mm(gb(("out", i))[:, j * T:(j + 1) * T], w[:, DT * j + k, :], mg[:, k, :],
                                      k == 0, k == DT - 1)
                    last.then_inc(chunks_used, 1)

            def norm_sum(l, stage, n):
                pe.wait_ge(sq_ready, n)
                feature_sum(l, stage, ones, sq, DT)

            def ffn(first, turn_of, unit):
                def slot(n, more=0):
                    pe.wait_ge(landed[(first + n) % RING], turn_of * 16 + more + 16 * ((first + n) // RING + 1))
                    return ring[:, (first + n) % RING, :].rearrange("p (b m) -> p b m", b=BLK)

                def gate_up(s, i):
                    w = slot(s, i * 16)
                    if not (isinstance(i, int) and isinstance(unit, int) and unit + i * RING + s < 7):
                        pe.wait_ge(ffn_drained, unit + i * RING + (s - 6))
                    bank = fbank[(s + 3) % 7]
                    for j in range(2):
                        for k in range(DT):
                            last = mm(bank[:, j * T:(j + 1) * T], w[:, DT * j + k, :], h[:, k, :], k == 0, k == DT - 1)
                    last.then_inc(chunks_used, 1)

                start = 0
                if isinstance(unit, int):
                    for s in range(RING):
                        gate_up(s, 0)
                    start = 1
                with pe.Fori(start, FT // RING) as i:
                    for s in range(RING):
                        gate_up(s, i)
                w = None
                for d in range(DT):
                    bank = fbank[[7, 0, 1, 2][d // 2]]
                    for k in range(FT):
                        b = d * FT + k
                        if b % BLK == 0:
                            w = slot(N_GU + b // BLK)
                        if d == 0 and (k == 0 or k > FT - RING):
                            pe.wait_ge(ffn_drained, unit + (FT - RING + 1 if k == 0 else k + 1))
                        last = mm(bank[:, (d % 2) * T:(d % 2 + 1) * T], w[:, b % BLK, :], gu[:, k, :], k == 0, k == FT - 1)
                        if b % BLK == BLK - 1:
                            last.then_inc(chunks_used, 1)

            def router():
                for i in range(1, 4):
                    pe.wait_ge(m_drained[i], L * M_TOTAL[i])
                for c in range(NCH):
                    for k in range(DT):
                        last = mm(mbank[1][:, c * E:(c + 1) * E], h[:, k, c * P:(c + 1) * P],
                                  sw[:, SW["router"] + E * k:SW["router"] + E * (k + 1)], k == 0, k == DT - 1)
                last.then_inc(m_filled[1], 1)
                pe.wait_ge(S["comb_ready"], 1)
                for c in range(NCH):
                    last = pe.transpose(mbank[2][0:E, c * P:(c + 1) * P], rt_comb[:, c, :], ident)
                last.then_inc(m_filled[2], 1)
                pe.wait_ge(S["combT_ready"], 1)
                for e in range(E):
                    last = mm(gbank[e // 2][:, (e % 2) * T:(e % 2 + 1) * T], cc[0:E, CC["sel"] + e * P:CC["sel"] + (e + 1) * P], combT)
                last.then_inc(m_filled[3], 1)

            rt_comb = rt[:, 0:2 * E].rearrange("p (c e) -> p c e", c=NCH)

            for l in range(L):
                norm_sum(l, "norm1", 2 * l + 1)
                project(l, 0, 14)
                mixer_d_rows(l)
                project(l, 14, 16)
                mixer_d_out(l)
                project(l, 16, 17)
                mixer_d_norm(l)
                mixer_a(l)
                project(l, 17, 18)
                mixer_b(l)
                project(l, 18, NZ)
                mixer_c(l)
                merge(l)
                norm_sum(l, "norm2", 2 * l + 2)
                pe.wait_ge(h_ready, 2 * DT * l + 2 * DT)
                for i in range(4):
                    pe.wait_ge(g_drained[i], (l + 1) * G_TOTAL[i])
                    pe.wait_ge(m_drained[i], (l + 1) * M_TOTAL[i])
                if l == 0:
                    ffn(FFN0, 0, 0)
                else:
                    router()
                    pe.wait_ge(S["crow_ready"], 1)
                    with pe.Fori(0, E) as e:
                        ffn(MOE0, e * (N_FFN // RING), e * (FT + 4) + (FT + 4))
            pe.wait_ge(sq_ready, 2 * L + 1)
            for j in range(DT):
                last = mm(mbank[0][:, 0:T], ones, sq[:, j, :], j == 0, j == DT - 1)
            last.then_inc(m_filled[0], 1)

        @block.scalar
        def _(act):
            q = Count(act, a_seq)
            A = nc.scalar.activation

            act.dma_start(x[:, :, :], x_in).then_inc(x_loaded, 16)
            act.dma_start(cc[:, :], cc_in).then_inc(consts_in, 16)
            act.dma_start(pp[:, :, :], pp_in).then_inc(consts_in, 16)
            act.dma_start(sw[:, :], sw_in[0]).then_inc(layer_in, 16)
            act.dma_start(rep[:, :], rep_in[0]).then_inc(layer_in, 16)
            act.wait_ge(consts_in, 32)
            eps = cc[:, CC["eps"]:CC["eps"] + 1]
            gn_eps = cc[:, CC["gn_eps"]:CC["gn_eps"] + 1]

            def drain(l, stage, ins):
                q.add(ins, m_drained[M_PLAN[stage][0]])

            def norm(stage_filled, root):
                q.add(A(sq[:, :, :], x[:, :, :], ACT.Square), sq_ready)
                stage_filled()
                root(A(rms[:, :], mbank[0][:, 0:T], ACT.Sqrt, scale=1.0 / D, bias=eps))

            def evacuate(l, units):
                for unit in units:
                    name, i = unit
                    act.wait_ge(chunks_used, unit_chunk(l, unit) + 1)
                    src = gb(unit)[:, :]
                    two = src.rearrange("p (j t) -> p j t", j=2)
                    if name == "zg":
                        ins = A(zg[:, 2 * i:2 * i + 2, :], two, ACT.Silu)
                    elif name == "xbc":
                        ins = A(xbc[:, 2 * i:2 * i + 2, 3:T + 3], two, ACT.Copy)
                    elif name == "v":
                        ins = A(vtok[:, i, :], src, ACT.Gelu_apprx_tanh)
                    elif name == "u":
                        ins = A(u[:, 2 * i:2 * i + 2, :], two, ACT.Gelu_apprx_tanh)
                    elif name == "b":
                        ins = A(zb[:, 2 * i:2 * i + 2, 16:T + 16], two, ACT.Copy)
                    else:
                        ins = A(zc[:, 2 * i:2 * i + 2, 1:T + 1], two, ACT.Copy)
                    q.add(ins, g_drained[G_PLAN[unit][0]])

            def mixer_d_dt(l):
                act.wait_ge(S["dt_raw"], l + 1)
                q.step(A(d_abs, d_raw, ACT.Abs))
                q.step(A(d_abs, d_abs, ACT.Exp, scale=-1.0))
                q.step(A(ahead[0:H, 0:1], par(l, "a_log", rows=H), ACT.Exp))
                q.step(A(d_ln, d_abs, ACT.Ln, bias=1.0), S["dt_exp"])

            def mixer_d(l):
                act.wait_ge(S["conv_done"], l + 1)
                q.add(A(conv[:, :, :], conv[:, :, :], ACT.Silu), S["conv_silu"])
                evacuate(l, Z_UNITS[12:14])
                filled(act, l, "bt")
                drain(l, "bt", A(btok[:, :, :], mb("bt")[:, 0:T].rearrange("p (g n) -> p g n", g=2), ACT.Copy))
                evacuate(l, Z_UNITS[14:16])
                act.wait_ge(S["d_endraw"], l + 1)
                q.step(A(d_end, d_end, ACT.Exp), S["d_endexp"])
                for c in range(NCH):
                    act.wait_ge(S["seg_ready"], NCH * l + c + 1)
                    q.step(A(mT[:, :, :], seg[:, :, :], ACT.Exp), S["seg_exp"])
                    if c == 0:
                        filled(act, l, "st")
                        drain(l, "st", A(st[:, :, :], mb("st")[:, :].rearrange("p (g n) -> p g n", g=2), ACT.Copy))
                        act.wait_ge(S["csc_ready"], 2 * l + 1)
                        q.step(A(cs[:, :, :], cs[:, :, :], ACT.Exp), S["er_ready"])
                evacuate(l, Z_UNITS[16:17])
                act.wait_ge(S["yd_ready"], 4 * l + 1)
                q.add(A(tiles(20840, 4)[:, :, :], yD[:, :, :], ACT.Square), S["ydsq"])
                filled(act, l, "dn")
                drain(l, "dn", A(rms[:, :], mb("dn")[:, 0:T], ACT.Sqrt, scale=1.0 / 512, bias=eps))

            def mixer_a(l):
                act.wait_ge(S["v_stats"], l + 1)
                q.add(A(small[:, 16:18], small[:, 16:18], ACT.Sqrt, bias=eps), S["v_std"])

            def mixer_b(l):
                for i in range(2):
                    filled(act, l, f"b{i}")
                    for j in range(2):
                        ins = A(yB[:, 2 * i + j, :], mb(f"b{i}")[:, j * T:(j + 1) * T], ACT.Copy, scale=par(l, "b_scale", 2 * i + j))
                        (q.add(ins, a_seq) if j == 0 else drain(l, f"b{i}", ins))

            def mixer_c(l):
                act.wait_ge(S["zc_mixed"], l + 1)
                q.add(A(zc[0:64, 12, 1:T + 1], zc[0:64, 12, 1:T + 1], ACT.Tanh), S["lora_ready"])
                q.add(A(zc[:, 13, 1:T + 1], zc[:, 13, 1:T + 1], ACT.Sigmoid), S["lora_ready"])
                for name, dst, bias, done in (("cw", w_log, "w0", "w_sig"), ("ca", aa, "a0", "a_sig")):
                    for i in range(2):
                        filled(act, l, f"{name}{i}")
                        for j in range(2):
                            ins = A(dst[:, 2 * i + j, :], mb(f"{name}{i}")[:, j * T:(j + 1) * T], ACT.Sigmoid,
                                    bias=par(l, bias, 2 * i + j))
                            (q.add(ins, a_seq) if j == 0 else drain(l, f"{name}{i}", ins))
                for i in range(2):
                    filled(act, l, f"cg{i}")
                    drain(l, f"cg{i}", A(gg[:, 2 * i:2 * i + 2, :], mb(f"cg{i}")[:, :].rearrange("p (j t) -> p j t", j=2), ACT.Copy))
                act.wait_ge(S["kr_ready"], l + 1)
                q.add(A(tmp1[:, :, :], kk[:, :, :], ACT.Square), S["krsq"])
                act.wait_ge(S["ss_ready"], l + 1)
                q.add(A(tmp1[:, :, :], tmp1[:, :, :], ACT.Sqrt), S["ss_sqrt"])
                act.wait_ge(S["cum_ready"], l + 1)
                q.add(A(e_in[:, :, :], c_sum[:, :, :], ACT.Exp), S["e_ready"])
                q.add(A(e_neg[:, :, :], c_sum[:, :, :], ACT.Exp, scale=-1.0), S["e_ready"])
                q.add(A(e_ex[:, :, :], w_log[:, :, :], ACT.Exp), S["e_ready"])
                q.add(A(small[:, 28:32], small[:, 28:32], ACT.Exp), S["e_ready"])
                act.wait_ge(S["ab_ready"], l + 1)
                m_done(act, l, "bo1")
                for c in range(NCH):
                    filled(act, l, f"vt{c}")
                    drain(l, f"vt{c}", A(cv[:, c, :], mb(f"vt{c}")[:, :], ACT.Copy))
                for i, name in enumerate(("kt", "nt")):
                    filled(act, l, name)
                    drain(l, name, A(kbt[:, i, :], mb(name)[:, :], ACT.Copy))
                for c in range(NCH):
                    filled(act, l, f"W0{c}")
                    filled(act, l, f"W1{c}")
                    if c == 0:
                        act.wait_ge(S["ab_ready"], l + 1)
                    else:
                        filled(act, l, "S")
                    for i in range(2):
                        drain(l, f"W{i}{c}", A(wb[:, i * T:(i + 1) * T], mb(f"W{i}{c}")[:, 0:T], ACT.Copy))
                    filled(act, l, f"U{c}")
                    drain(l, f"U{c}", A(ub, mb(f"U{c}")[:, :], ACT.Copy))
                    filled(act, l, f"O{c}")
                    drain(l, f"O{c}", A(oo[:, :, c * P:(c + 1) * P], mb(f"O{c}")[:, :].rearrange("p (j t) -> p j t", j=4), ACT.Copy))
                act.wait_ge(S["cent"], 2 * (l + 1))
                q.add(A(tiles(7696, 4)[:, :, :], oo[:, :, :], ACT.Square), S["osq"])
                for i in range(2):
                    filled(act, l, f"va{i}")
                    drain(l, f"va{i}", A(tiles(8720, 4)[:, 2 * i:2 * i + 2, :], mb(f"va{i}")[:, :].rearrange("p (j t) -> p j t", j=2),
                                         ACT.Sqrt, scale=1.0 / 64, bias=gn_eps))

            def merge(l):
                for d in range(DT):
                    if d == 0:
                        act.wait_ge(S["yc_ready"], l + 1)
                    if d >= 2:
                        act.wait_ge(S["mg_ready"], DT * l + d - 1)
                    for i in range(2):
                        act.wait_ge(chunks_used, unit_chunk(l, ("gate", d, i)) + 1)
                        q.add(A(sg[:, d % 2, i * 512:(i + 1) * 512], gb(("gate", d, i))[:, :], ACT.Sigmoid),
                              g_drained[G_PLAN[("gate", d, i)][0]])

            def silus(first, e42):
                for_static = isinstance(e42, int)

                def one(s, i):
                    act.wait_ge(chunks_used, e42 + i * RING + (first + s + 1))
                    A(sil[:, s, :], fbank[(s + 3) % 7][:, 0:T], ACT.Silu).then_inc(silu_done, 1)
                with act.Fori(0, FT // RING) as i:
                    for s in range(RING):
                        one(s, i)

            for l in range(L):
                if l == 0:
                    act.wait_ge(x_loaded, 16)
                else:
                    act.wait_ge(S["ffn_x"], 4)
                norm(lambda: filled(act, l, "norm1"), lambda ins: drain(l, "norm1", ins))
                act.wait_ge(padded, 3 * (l + 1))
                evacuate(l, Z_UNITS[:10])
                mixer_d_dt(l)
                evacuate(l, Z_UNITS[10:12])
                mixer_d(l)
                mixer_a(l)
                evacuate(l, Z_UNITS[17:18])
                mixer_b(l)
                evacuate(l, Z_UNITS[18:])
                mixer_c(l)
                if l == 0:
                    m_done(act, l, "S")
                    act.wait_ge(S["ya_ready"], NCH)
                    act.dma_start(sw[:, :], sw_in[1]).then_inc(layer_in, 16)
                    act.dma_start(rep[:, :], rep_in[1]).then_inc(layer_in, 16)
                merge(l)
                act.wait_ge(x_mixed, N_OUT * (l + 1))
                norm(lambda: filled(act, l, "norm2"), lambda ins: drain(l, "norm2", ins))
                if l == 0:
                    silus(FFN0, 0)
                else:
                    act.wait_ge(S["logits_top"], 1)
                    q.step(A(small[:, 40:42], small[:, 36:38], ACT.Sigmoid))
                    q.add(A(small[:, 42:44], small[:, 36:38], ACT.Sigmoid, scale=-1.0), S["probs"])
                    with act.Fori(0, E) as e:
                        silus(MOE0, e * N_FFN)
            act.wait_ge(S["ffn_x"], 8)
            norm(lambda: act.wait_ge(m_filled[0], L * F_TOTAL[0] + 1), lambda ins: q.add(ins, m_drained[0]))
            act.wait_ge(S["out_ready"], DT)
            act.dma_start(out, h[:, :, :]).then_inc(out_stored, 16)
            act.wait_ge(out_stored, 16)

        @block.gpsimd
        def _(pool):
            q = Count(pool, p_seq)
            G = nc.gpsimd
            pool.wait_ge(consts_in, 32)
            for l in range(L):
                if l:
                    pool.wait_ge(S["ffn_x"], 4)
                q.add(G.memset(zc[:, :, 0:1], 0.0), padded)
                q.add(G.memset(xbc[:, :, 0:3], 0.0), padded)
                q.add(G.memset(zb[:, :, 0:16], 0.0), padded)
                g_done(pool, l, ("b", 0))
                g_done(pool, l, ("b", 1))
                pool.wait_ge(padded, 3 * (l + 1))
                w = T + 16
                q.step(G.tensor_tensor(p2[:, :, 1:w], zb[:, :, 1:w], zb[:, :, 0:w - 1], ALU.add))
                q.step(G.tensor_tensor(p4[:, 1:4, 3:w], p2[:, 1:4, 3:w], p2[:, 1:4, 1:w - 2], ALU.add))
                q.step(G.tensor_tensor(p2[:, 2:4, 7:w], p4[:, 2:4, 7:w], p4[:, 2:4, 3:w - 4], ALU.add))
                q.step(G.tensor_tensor(p4[:, 3:4, 15:w], p2[:, 3:4, 15:w], p2[:, 3:4, 7:w - 8], ALU.add))
                count = cc[:, CC["count"]:CC["count"] + 4 * T].rearrange("p (g t) -> p g t", g=4)
                for g, src in enumerate((p2, p4, p2, p4)):
                    q.step(G.tensor_tensor(yB[:, g, :], src[:, g, 16:w], count[:, g, :], ALU.mult))
                q.step(G.tensor_tensor(yB[:, :, :], yB[:, :, :], zb[:, :, 16:w], ALU.subtract), S["pooled"])

        @block.vector
        def _(dve):
            q = Count(dve, v_seq)
            V = nc.vector
            TT = V.tensor_tensor

            def marker():
                return V.tensor_copy(small[:, 60:61], small[:, 61:62])

            q.step(V.memset(small[:, 60:62], 0.0))
            dve.wait_ge(consts_in, 32)

            def drain(stage, ins):
                q.add(ins, m_drained[M_PLAN[stage][0]])

            def drained_step(stage, ins):
                q.step(ins, m_drained_own[M_PLAN[stage][0]])

            def norm(root_done, gain, done):
                root_done()
                q.step(V.reciprocal(rstd[:, :], rms[:, :]))
                for k in range(DT):
                    q.add(V.scalar_tensor_tensor(h[:, k, :], x[:, k, :], gain(k), rstd[:, :], ALU.mult, ALU.mult), done)

            def mixer_d_dt(l):
                filled(dve, l, "dt")
                drain("dt", V.tensor_scalar(d_raw, mb("dt")[0:H, 0:T], par(l, "dt_bias", rows=H), None, ALU.add))
                m_done(dve, l, "dt")
                q.step(V.tensor_copy(d_raw, d_raw), S["dt_raw"])
                dve.wait_ge(S["dt_exp"], l + 1)
                q.step(V.scalar_tensor_tensor(d_dt, d_raw, 0.0, d_ln, ALU.max, ALU.add))
                q.step(V.tensor_scalar(d_abs, d_dt, ahead[0:H, 0:1], -1.0, ALU.mult, ALU.mult))
                q.step(V.tensor_tensor_scan(d_cs, cc[0:H, CC["reset"]:CC["reset"] + T], d_abs, 0.0, ALU.mult, ALU.add), S["cs_ready"])

            def mixer_d_conv(l):
                for i in range(4):
                    g_done(dve, l, ("xbc", i))
                for k in range(4):
                    for j in range(8):
                        w = par(l, "conv_w", 8 * k + j)
                        if k == 0:
                            ins = V.tensor_scalar(conv[:, j, :], xbc[:, j, 0:T], w, par(l, "conv_b", j), ALU.mult, ALU.add)
                        else:
                            ins = V.scalar_tensor_tensor(conv[:, j, :], xbc[:, j, k:k + T], w, conv[:, j, :], ALU.mult, ALU.add)
                        if k == 3 and j == 7:
                            q.step(ins, S["conv_done"])
                        elif j == 7:
                            q.step(ins)
                        else:
                            q.add(ins, v_seq)

            def mixer_d(l):
                up = const("incl_up")
                filled(dve, l, "cb")
                drain("cb", TT(cbm[:, :, :], mb("cb")[:, :].rearrange("p (i t) -> p i t", i=4), over(up, 4), ALU.mult))
                filled(dve, l, "dtT")
                drain("dtT", V.tensor_copy(area(17256, 32), mb("dtT")[:, 0:32]))
                m_done(dve, l, "dtT")
                for c in range(NCH):
                    filled(dve, l, f"xt{c}")
                    drain(f"xt{c}", TT(xd[:, c, :].rearrange("p (h d) -> p h d", h=H),
                                       mb(f"xt{c}")[:, :].rearrange("p (h d) -> p h d", h=H), along(tok[:, 0, c, :], 64), ALU.mult))
                for i in range(4):
                    row = mb(f"row{i}")[:, :].rearrange("p (j t) -> p j t", j=2)
                    filled(dve, l, f"row{i}")
                    for j in range(2):
                        hd = 2 * i + j
                        q.add(V.tensor_scalar(seg[:, hd, :], row[:, j, 0:P], tok[:, 1, 0, hd:hd + 1], 0.0, ALU.subtract, ALU.min), v_seq)
                        q.add(V.tensor_scalar(seg1[:, hd, :], row[:, j, P:T], tok[:, 1, 1, hd:hd + 1], 0.0, ALU.subtract, ALU.min), v_seq)
                    q.add(V.tensor_copy(cs[:, 2 * i:2 * i + 2, :], row[:, :, P:T]), v_seq)
                    drain(f"row{i}", TT(d_end[:, 2 * i:2 * i + 2].unsqueeze(2), row[:, :, P - 1:P], tok[:, 1, 0, 2 * i:2 * i + 2].unsqueeze(2),
                                        ALU.subtract))
                m_done(dve, l, "row3")
                m_done(dve, l, "row2")
                m_done(dve, l, "row1")
                m_done(dve, l, "row0")
                q.step(V.tensor_scalar(d_end, d_end, 0.0, None, ALU.min), S["d_endraw"])
                q.step(marker(), S["seg_ready"])
                dve.wait_ge(S["d_endexp"], l + 1)
                for c in range(NCH):
                    m_done(dve, l, f"xt{c}")
                q.step(TT(xde.rearrange("p (h d) -> p h d", h=H), xd[:, 0, :].rearrange("p (h d) -> p h d", h=H), along(d_end, 64), ALU.mult),
                       S["xde_ready"])
                q.step(marker(), S["csc_ready"])
                m_done(dve, l, "cb")
                for c in range(NCH):
                    dve.wait_ge(S["seg_exp"], NCH * l + c + 1)
                    for g in range(2):
                        q.step(TT(mT[:, 4 * g:4 * g + 4, :], mT[:, 4 * g:4 * g + 4, :], over(cbm[:, 2 * g + c, :], 4), ALU.mult), S["mt_ready"])
                    if c == 0:
                        dve.wait_ge(S["er_ready"], l + 1)
                        for g in range(2):
                            ins = TT(cs[:, 4 * g:4 * g + 4, :], cs[:, 4 * g:4 * g + 4, :], over(conv[:, 6 + g, P:T], 4), ALU.mult)
                            q.step(ins, S["csc_ready"] if g else None)
                        filled(dve, l, "yd0")
                        q.step(V.tensor_copy(seg[:, :, :], seg1[:, :, :]), S["seg_ready"])
                for c in range(NCH):
                    filled(dve, l, f"yd{c}")
                    for j in range(4):
                        ins = V.scalar_tensor_tensor(yD[:, j, c * P:(c + 1) * P], conv[:, j, c * P:(c + 1) * P], par(l, "skip", j),
                                                     mb(f"yd{c}")[:, j * P:(j + 1) * P], ALU.mult, ALU.add)
                        (q.add(ins, v_seq) if j < 3 else drain(f"yd{c}", ins))
                m_done(dve, l, "yd1")
                m_done(dve, l, "yd0")
                dve.wait_ge(v_seq, q.n[id(v_seq)])
                g_done(dve, l, ("zg", 0))
                g_done(dve, l, ("zg", 1))
                q.step(TT(yD[:, :, :], yD[:, :, :], zg[:, :, :], ALU.mult), S["yd_ready"])
                m_done(dve, l, "dn")
                q.step(V.reciprocal(rstd[:, :], rms[:, :]))
                for j in range(4):
                    ins = V.scalar_tensor_tensor(yD[:, j, :], yD[:, j, :], par(l, "norm_d", j), rstd[:, :], ALU.mult, ALU.mult)
                    (q.add(ins, v_seq) if j == 0 else q.add(ins, S["yd_ready"]))
                dve.wait_ge(S["yd_ready"], q.n[id(S["yd_ready"])])


            def mixer_a(l):
                dve.wait_ge(layer_in, 32 * (l + 1))
                ws = sw[:, SW["w_s"]:SW["w_s"] + 512].rearrange("p (g t) -> p g t", g=4)
                q.step(TT(ws, ws, over(const("incl_up"), 4), ALU.mult), S["wm_ready"])
                for c in range(NCH):
                    g_done(dve, l, ("v", c))
                    q.step(V.bn_stats(small[:, 6 * c:6 * c + 6], vtok[:, c, :]))
                    q.step(V.bn_aggr(small[:, 12 + 20 * c:14 + 20 * c], small[:, 6 * c:6 * c + 6]))
                    q.step(V.tensor_copy(small[:, 16 + c:17 + c], small[:, 13 + 20 * c:14 + 20 * c]), S["v_stats"] if c else None)
                dve.wait_ge(S["v_std"], l + 1)
                q.step(V.reciprocal(small[:, 16:18], small[:, 16:18]))
                for c in range(NCH):
                    v = vtok[:, c, :]
                    q.step(V.tensor_scalar(v, v, small[:, 12 + 20 * c:13 + 20 * c], small[:, 16 + c:17 + c], ALU.subtract, ALU.mult))
                    q.step(TT(v, v, rep[:, 0:512], ALU.mult))
                    q.step(TT(v, v, rep[:, 512:1024], ALU.add), S["vn_ready"])
                for i in range(2):
                    g_done(dve, l, ("u", i))
                for c in range(NCH):
                    filled(dve, l, f"a{c}")
                    y = yA[:, :, c * P:(c + 1) * P]
                    drain(f"a{c}", TT(y, mb(f"a{c}")[:, :].rearrange("p (g t) -> p g t", g=4),
                                      rep[:, 1024:1536].rearrange("p (g t) -> p g t", g=4), ALU.add))
                    m_done(dve, l, f"a{c}")
                    q.step(TT(y, y, u[:, :, c * P:(c + 1) * P], ALU.mult), S["ya_ready"])

            def mixer_c(l):
                for i in range(CT // 2):
                    g_done(dve, l, ("c", i))
                dve.wait_ge(S["pooled"], l + 1)
                now = zc[:, :, 1:T + 1]
                q.step(TT(dif[:, :, :], zc[:, :, 0:T], now, ALU.subtract))
                for j in range(CT):
                    ins = V.scalar_tensor_tensor(zc[:, j, 1:T + 1], dif[:, j, :], par(l, "mix", j), zc[:, j, 1:T + 1], ALU.mult, ALU.add)
                    (q.add(ins, v_seq) if j < CT - 1 else q.step(ins, S["zc_mixed"]))
                dve.wait_ge(v_seq, q.n[id(v_seq)])
                r, k, v = zc[:, 0:4, 1:T + 1], zc[:, 4:8, 1:T + 1], zc[:, 8:12, 1:T + 1]
                for j in range(4):
                    ins = V.tensor_scalar(kk[:, j, :], k[:, j, :], par(l, "k_k", j), None, ALU.mult)
                    (q.add(ins, v_seq) if j < 3 else q.step(ins, S["kr_ready"]))
                dve.wait_ge(v_seq, q.n[id(v_seq)])
                m_done(dve, l, "cw0")
                m_done(dve, l, "cw1")
                q.step(V.tensor_scalar(w_log[:, :, :], w_log[:, :, :], -DECAY, None, ALU.mult))
                flat = lambda ap: ap.rearrange("p j t -> p (j t)")
                q.step(V.tensor_tensor_scan(flat(c_sum), const("reset", 4 * T), flat(w_log), 0.0, ALU.mult, ALU.add))
                by_chunk = lambda ap: flat(ap).rearrange("p (n t) -> p n t", t=P)
                mid = small[:, 20:28]
                q.step(V.tensor_scalar(mid.unsqueeze(2), by_chunk(c_sum)[:, :, P - 1:P], 0.5, None, ALU.mult))
                q.step(TT(by_chunk(c_sum), by_chunk(c_sum), along(mid, P), ALU.subtract))
                q.step(TT(small[:, 28:32], small[:, 20:28:2], small[:, 21:28:2], ALU.add))
                q.step(TT(w_log[:, :, :], c_sum[:, :, :], w_log[:, :, :], ALU.subtract), S["cum_ready"])
                m_done(dve, l, "ca0")
                m_done(dve, l, "ca1")
                for j in range(4):
                    q.add(V.tensor_scalar(k2[:, j, :], aa[:, j, :], -1.0, par(l, "k_a", j), ALU.add, ALU.mult), v_seq)
                dve.wait_ge(v_seq, q.n[id(v_seq)])
                for j in range(4):
                    q.add(V.scalar_tensor_tensor(k2[:, j, :], k2[:, j, :], 1.0, k[:, j, :], ALU.add, ALU.mult), v_seq)
                dve.wait_ge(v_seq, q.n[id(v_seq)])
                for i in range(2):
                    filled(dve, l, f"ss{i}")
                filled(dve, l, "ss1")
                for i in range(2):
                    drain(f"ss{i}", V.tensor_scalar(tmp1[:, 2 * i:2 * i + 2, :], mb(f"ss{i}")[:, :].rearrange("p (j t) -> p j t", j=2),
                                                    FLOOR, None, ALU.max))
                for i in range(2):
                    m_done(dve, l, f"ss{i}")
                for j in range(4):
                    ins = V.scalar_tensor_tensor(tmp2[:, j, :], r[:, j, :], par(l, "r_k", j), k2[:, j, :], ALU.mult, ALU.mult)
                    if j < 3:
                        q.add(ins, v_seq)
                    else:
                        q.step(ins, S["rk_ready"])
                dve.wait_ge(v_seq, q.n[id(v_seq)])
                q.step(marker(), S["ss_ready"])
                dve.wait_ge(S["ss_sqrt"], l + 1)
                q.step(V.reciprocal(tmp1[:, :, :], tmp1[:, :, :]))
                q.step(TT(kk[:, :, :], kk[:, :, :], tmp1[:, :, :], ALU.mult))
                dve.wait_ge(S["e_ready"], 4 * (l + 1))
                arj = ar.rearrange("p j c a t -> p (j c) a t")
                q.add(TT(arj[:, :, 0, :], by_chunk(kk), by_chunk(e_ex), ALU.mult), v_seq)
                rc = r.rearrange("p j (c t) -> p j c t", c=NCH)
                q.add(TT(ar[:, :, :, 1, :], rc, e_in.rearrange("p j (c t) -> p j c t", c=NCH), ALU.mult), v_seq)
                q.add(TT(ka[:, :, :], k2[:, :, :], e_neg[:, :, :], ALU.mult), v_seq)
                q.step(V.scalar_tensor_tensor(flat(aa), flat(kk), -1.0, flat(aa), ALU.mult, ALU.mult))
                q.step(TT(nb[:, :, :], aa[:, :, :], e_neg[:, :, :], ALU.mult), S["ab_ready"])
                for i in range(2):
                    filled(dve, l, f"bo{i}")
                    drain(f"bo{i}", TT(bv[:, 2 * i:2 * i + 2, :], mb(f"bo{i}")[:, :].rearrange("p (j t) -> p j t", j=2),
                                       v[:, 2 * i:2 * i + 2, :], ALU.mult))
                mask = cc[:, CC["strict_up"]:CC["strict_up"] + 2 * P]
                for c in range(NCH):
                    for g in range(2):
                        four = slice(4 * g, 4 * g + 4)
                        filled(dve, l, f"n{g}{c}")
                        if c and g == 0:
                            filled(dve, l, "O0")
                        drain(f"n{g}{c}", TT(xx[:, four, :], mb(f"n{g}{c}")[:, :].rearrange("p (i t) -> p i t", i=4), over(const("low2"), 4), ALU.mult))
                        m_done(dve, l, f"n{g}{c}")
                        q.step(TT(xx[:, four, :], xx[:, four, :], over(ident, 4), ALU.add), S["x_ready"])
                    for hd in range(H):
                        filled(dve, l, f"s{hd}{c}")
                        drain(f"s{hd}{c}", TT(sc[:, hd, :, :].rearrange("p (b a) t -> p b (a t)", b=2), mb(f"s{hd}{c}")[:, :].rearrange("p (b f) -> p b f", b=2), over(mask, 2), ALU.mult))
                        m_done(dve, l, f"s{hd}{c}")
                        q.step(TT(zz[:, hd, :], sc[:, hd, 0, :], const("up2"), ALU.mult), S["sc_ready"])
                    for g in range(2):
                        four = slice(4 * g, 4 * g + 4)
                        q.step(TT(zz[:, four, :], zz[:, four, :], over(ident, 4), ALU.add), S["z_ready"])
                    for lv in range(LEVELS):
                        off = cc[:, CC["off"] + lv * P:CC["off"] + (lv + 1) * P]
                        for g in range(2):
                            four = slice(4 * g, 4 * g + 4)
                            filled(dve, l, f"t{g}{lv}{c}")
                            src = mb(f"t{g}{lv}{c}")[:, :].rearrange("p (i t) -> p i t", i=4)
                            drain(f"t{g}{lv}{c}", TT(tt[:, four, :], src, over(off, 4), ALU.mult))
                            m_done(dve, l, f"t{g}{lv}{c}")
                            q.add(marker(), S["t_ready"])
                        for g in range(2):
                            four = slice(4 * g, 4 * g + 4)
                            if lv < LEVELS - 1:
                                st_ = f"x{g}{lv}{c}"
                                filled(dve, l, st_)
                                drain(st_, TT(xx[:, four, :], mb(st_)[:, :].rearrange("p (i t) -> p i t", i=4), xx[:, four, :], ALU.add))
                                m_done(dve, l, st_)
                                q.add(marker(), S["x_ready"])
                            st_ = f"z{g}{lv}{c}"
                            filled(dve, l, st_)
                            drain(st_, TT(zz[:, four, :], mb(st_)[:, :].rearrange("p (i t) -> p i t", i=4), zz[:, four, :], ALU.add))
                            m_done(dve, l, st_)
                            q.add(marker(), S["z_ready"])
                    if c == 0:
                        filled(dve, l, "S")
                        drain("S", TT(s0[:, :, :], mb("S")[:, 0:256].rearrange("p (j f) -> p j f", j=4), along(small[:, 28:32], 64), ALU.mult))
                        m_done(dve, l, "S")
                        q.step(marker(), S["s0_ready"])
                m_done(dve, l, "O0")
                m_done(dve, l, "O1")
                for i in range(2):
                    filled(dve, l, f"mu{i}")
                filled(dve, l, "mu1")
                for i in range(2):
                    o2 = oo[:, 2 * i:2 * i + 2, :].rearrange("p j t -> p (j t)")
                    drain(f"mu{i}", V.scalar_tensor_tensor(o2, mb(f"mu{i}")[:, :], -1.0 / 64, o2, ALU.mult, ALU.add))
                    m_done(dve, l, f"mu{i}")
                    q.add(marker(), S["cent"])
                m_done(dve, l, "va0")
                m_done(dve, l, "va1")
                va = tiles(8720, 4)
                q.step(V.reciprocal(va[:, :, :], va[:, :, :]))
                q.step(TT(oo[:, :, :], oo[:, :, :], va[:, :, :], ALU.mult))
                for j in range(4):
                    q.add(V.tensor_scalar(oo[:, j, :], oo[:, j, :], par(l, "ln_g", j), par(l, "ln_b", j), ALU.mult, ALU.add), v_seq)
                dve.wait_ge(v_seq, q.n[id(v_seq)])
                for i in range(2):
                    m_done(dve, l, f"bo{i}")
                    m_done(dve, l, f"cg{i}")
                q.step(TT(oo[:, :, :], oo[:, :, :], bv[:, :, :], ALU.add))
                q.step(TT(yC[:, :, :], oo[:, :, :], gg[:, :, :], ALU.mult), S["yc_ready"])

            def merge(l):
                for d in range(DT):
                    for i in range(2):
                        if i == 0:
                            filled(dve, l, f"pj{d}0")
                        else:
                            dve.wait_ge(chunks_used, chunk0(l) + NZ + 3 * d + 3)
                        g_done(dve, l, ("gate", d, i))
                        s_ = sg[:, d % 2, i * 512:(i + 1) * 512]
                        drain(f"pj{d}{i}", TT(s_, mb(f"pj{d}{i}")[:, :], s_, ALU.mult))
                    for i in range(2):
                        m_done(dve, l, f"pj{d}{i}")
                    q.step(TT(sg[:, d % 2, 0:512], sg[:, d % 2, 0:512], sg[:, d % 2, 512:1024], ALU.add))
                    q.step(TT(mg[:, d, :], sg[:, d % 2, 0:T], sg[:, d % 2, T:2 * T], ALU.add), S["mg_ready"])
                for i in range(N_OUT):
                    unit = ("out", i)
                    dve.wait_ge(chunks_used, unit_chunk(l, unit) + 1)
                    x2 = x[:, 2 * i:2 * i + 2, :]
                    q.add(TT(x2, gb(unit)[:, :].rearrange("p (j t) -> p j t", j=2), x2, ALU.add), g_drained[G_PLAN[unit][0]])
                    g_done(dve, l, unit)
                    q.add(marker(), x_mixed)

            def ffn(first, e42, e28, expert):
                def hidden(s, i):
                    dve.wait_ge(silu_done, e28 + i * RING + (s + 1))
                    TT(gu[:, i * RING + s, :], fbank[(s + 3) % 7][:, T:2 * T], sil[:, s, :], ALU.mult).then_inc(ffn_drained, 1)
                with dve.Fori(0, FT // RING) as i:
                    for s in range(RING):
                        hidden(s, i)
                for d2 in range(4):
                    dve.wait_ge(chunks_used, e42 + (first + N_GU + (2 * FT * (d2 + 1) - 1) // BLK + 1))
                    bank = fbank[[7, 0, 1, 2][d2]][:, :].rearrange("p (j t) -> p j t", j=2)
                    x2 = x[:, 2 * d2:2 * d2 + 2, :]
                    if expert is None:
                        TT(x2, bank, x2, ALU.add).then_inc(ffn_drained, 1)
                    else:
                        m2 = moe_tmp.rearrange("p (j t) -> p j t", j=2)
                        dve.wait_ge(S["b_done"], expert * 4 + (4 + d2))
                        row = over(crow[:, expert, :], 2)
                        TT(m2, bank, row, ALU.mult).then_inc(ffn_drained, 1)
                        dve.wait_ge(ffn_drained, e28 + expert * 4 + (FT + 4 + d2 + 1))
                        TT(x2, m2, x2, ALU.add).then_inc(S["b_done"], 1)

            def router():
                dve.wait_ge(m_filled[1], L * F_TOTAL[1] + 1)
                r3 = lambda i: rt[:, 16 * i:16 * i + 16].rearrange("p (c e) -> p c e", c=NCH)
                comb, lg, eq, cum, first1, first2 = (r3(i) for i in range(6))
                v1, v2, dd = small[:, 32:34], small[:, 34:36], small[:, 36:38]
                p1, p2_ = small[:, 40:42], small[:, 42:44]
                q.step(V.tensor_copy(rt[:, 16:32], mbank[1][:, 0:16]))

                def pick(top, chosen):
                    q.step(V.tensor_reduce(top, lg, AX_X, ALU.max))
                    for c in range(NCH):
                        q.step(V.tensor_scalar(eq[:, c, :], lg[:, c, :], top[:, c:c + 1], None, ALU.is_equal))
                        q.step(V.tensor_tensor_scan(cum[:, c, :], const("ones", E), eq[:, c, :], 0.0, ALU.mult, ALU.add))
                    q.step(V.scalar_tensor_tensor(chosen, cum, 1.0, eq, ALU.is_equal, ALU.mult))

                pick(v1, first1)
                q.step(V.scalar_tensor_tensor(lg, first1, -3.0e38, lg, ALU.mult, ALU.add))
                pick(v2, first2)
                q.step(TT(dd, v1, v2, ALU.subtract), S["logits_top"])
                dve.wait_ge(S["probs"], 1)
                for c in range(NCH):
                    q.step(V.tensor_scalar(comb[:, c, :], first1[:, c, :], p1[:, c:c + 1], None, ALU.mult))
                    q.step(V.scalar_tensor_tensor(comb[:, c, :], first2[:, c, :], p2_[:, c:c + 1], comb[:, c, :], ALU.mult, ALU.add),
                           S["comb_ready"] if c else None)
                dve.wait_ge(m_filled[2], L * F_TOTAL[2] + 1)
                q.step(V.tensor_copy(combT, mbank[2][0:E, 0:T]), S["combT_ready"])
                dve.wait_ge(m_filled[3], L * F_TOTAL[3] + 1)
                for i in range(4):
                    ins = V.tensor_copy(crow[:, 2 * i:2 * i + 2, :], gbank[i][:, :].rearrange("p (j t) -> p j t", j=2))
                    (q.step(ins) if i < 3 else q.step(ins, S["crow_ready"]))

            for l in range(L):
                norm(lambda: m_done(dve, l, "norm1"), lambda k: par(l, "norm_mix", k), h_ready)
                dve.wait_ge(h_ready, 2 * DT * l + DT)
                mixer_d_dt(l)
                mixer_d_conv(l)
                mixer_d(l)
                mixer_a(l)
                mixer_c(l)
                merge(l)
                norm(lambda: m_done(dve, l, "norm2"), lambda k: par(l, "norm_ffn", k), h_ready)
                if l == 0:
                    ffn(FFN0, 0, 0, None)
                    dve.wait_ge(ffn_drained, FT + 4)
                    for _ in range(4):
                        q.step(marker(), S["ffn_x"])
                else:
                    router()
                    q.step(marker())
                    for _ in range(4):
                        q.step(marker(), S["b_done"])
                    with dve.Fori(0, E) as e:
                        ffn(MOE0, e * N_FFN, e * FT + FT, e)
                    dve.wait_ge(S["b_done"], 4 * E + 4)
                    for _ in range(4):
                        q.step(marker(), S["ffn_x"])
            dve.wait_ge(m_drained[0], L * M_TOTAL[0] + 1)
            q.step(V.reciprocal(rstd[:, :], rms[:, :]))
            for k in range(DT):
                q.add(V.scalar_tensor_tensor(h[:, k, :], x[:, k, :], par(0, "norm_final", k), rstd[:, :], ALU.mult, ALU.mult), S["out_ready"])


def kernel(x, norm_mix_g, w_in, a_ln_g, a_ln_b, a_w_s, a_b_s, b_w_pool, b_scale, c_mix, c_w0, c_w2, c_a0, c_a2, c_g2,
           c_k_k, c_k_a, c_r_k, c_ln_g, c_ln_b, d_conv_w, d_conv_b, d_dt_bias, d_a_log, d_skip, d_norm_g,
           w_branch, w_out, norm_ffn_g, ffn_w_gate, ffn_w_up, ffn_w_down, moe_router, moe_w_gate, moe_w_up, moe_w_down,
           norm_final_g):
    import numpy as np
    import concourse.bacc as bacc
    from concourse.bass_utils import run_bass_kernel_spmd

    f = lambda a: np.asarray(a)

    def col_tiles(w):
        k, n = w.shape
        return w.reshape(k // P, P, n // P, P).transpose(2, 1, 0, 3).reshape(n // P, P, k)

    def pairs(t):
        return t.reshape(-1, 2, P, D).transpose(0, 2, 1, 3).reshape(-1, P, CW)

    def swiglu_chunks(wg, wu, wd):
        g, up = col_tiles(wg), col_tiles(wu)
        hidden = np.stack([g, up], 1).transpose(0, 2, 1, 3).reshape(FT, P, CW)
        down = wd.reshape(FT, P, DT, P).transpose(2, 0, 1, 3).reshape(N_DOWN, BLK, P, P)
        return [hidden, down.transpose(0, 2, 1, 3).reshape(N_DOWN, P, CW)]

    def mixer_chunks(l):
        w = f(w_in)[l]
        v = w[:, 512:1024].reshape(2, 4, P, 512).transpose(0, 2, 1, 3).reshape(2, P, CW)
        gates = col_tiles(w[:, 4872:8968]).reshape(4, DT, P, D).transpose(1, 0, 2, 3).reshape(4 * DT, P, D)
        gates = pairs(gates).reshape(DT, 2, P, CW)
        branch = f(w_branch)[l].reshape(4, 4, P, DT, P).transpose(3, 2, 0, 1, 4).reshape(DT, 1, P, CW)
        return [pairs(col_tiles(w[:, 3328:3840])), pairs(col_tiles(w[:, 3840:4864])), v, pairs(col_tiles(w[:, 0:512])),
                pairs(col_tiles(w[:, 1024:1536])), pairs(col_tiles(w[:, 1536:3328])),
                np.concatenate([gates, branch], 1).reshape(N_MERGE, P, CW), pairs(col_tiles(f(w_out)[l]))]

    parts = mixer_chunks(0) + swiglu_chunks(f(ffn_w_gate)[0], f(ffn_w_up)[0], f(ffn_w_down)[0]) + mixer_chunks(1)
    for e in range(E):
        parts += swiglu_chunks(f(moe_w_gate)[0, e], f(moe_w_up)[0, e], f(moe_w_down)[0, e])
    stream = np.concatenate(parts, 0)
    assert stream.shape == (N_CHUNKS, P, CW)

    def cols(a):
        return f(a).reshape(-1, P).T

    pp = np.zeros((P, L, NPP), np.float32)
    for l in range(L):
        put = {"norm_mix": cols(f(norm_mix_g)[l]), "norm_ffn": cols(f(norm_ffn_g)[l]), "mix": cols(f(c_mix)[l]), "w0": cols(f(c_w0)[l]),
               "a0": cols(f(c_a0)[l]), "k_k": cols(f(c_k_k)[l]), "k_a": cols(f(c_k_a)[l]), "r_k": cols(f(c_r_k)[l]),
               "ln_g": cols(f(c_ln_g)[l]), "ln_b": cols(f(c_ln_b)[l]), "conv_w": cols(f(d_conv_w)[l]), "conv_b": cols(f(d_conv_b)[l]),
               "norm_d": cols(f(d_norm_g)[l]), "skip": cols(np.repeat(f(d_skip)[l], 64)), "b_scale": cols(f(b_scale)[l]),
               "norm_final": cols(norm_final_g)}
        for name, a in put.items():
            pp[:, l, PP[name]:PP[name] + a.shape[1]] = a
        pp[0:H, l, PP["dt_bias"]] = f(d_dt_bias)[l]
        pp[0:H, l, PP["a_log"]] = f(d_a_log)[l]

    sw = np.zeros((L, P, NSW), np.float32)
    rep = np.zeros((L, P, NREP), np.float32)
    for l in range(L):
        put = {"w_s": f(a_w_s)[l].transpose(2, 0, 1).reshape(P, 512), "pool": f(b_w_pool)[l].transpose(1, 0, 2).reshape(P, 512),
               "w2a2": np.concatenate([f(c_w2)[l], f(c_a2)[l]], 0), "g2": f(c_g2)[l],
               "dt": f(w_in)[l][:, 4864:4872].reshape(DT, P, H).transpose(1, 0, 2).reshape(P, DT * H)}
        if l == 1:
            put["router"] = f(moe_router)[0].reshape(DT, P, E).transpose(1, 0, 2).reshape(P, DT * E)
        for name, a in put.items():
            sw[l, :, SW[name]:SW[name] + a.shape[1]] = a
        rep[l, :, 0:512] = f(a_ln_g)[l]
        rep[l, :, 512:1024] = f(a_ln_b)[l]
        rep[l, :, 1024:1536] = f(a_b_s)[l].reshape(512)

    i, j = np.arange(P)[:, None], np.arange(P)[None, :]
    t = np.arange(T)
    off = [((i // (2 * m) == j // (2 * m)) & (i // m != j // m)) for m in (2, 4, 8, 16, 32, 64)]
    put = {"ident": i == j, "ones": np.ones((P, P)), "heads": i // 64 == j // 64, "strict_up": i < j, "incl_up": i <= j,
           "low2": (i > j) & (i // 2 == j // 2), "up2": (i < j) & (i // 2 == j // 2), "off": np.concatenate(off, 1),
           "count": np.tile(np.concatenate([1.0 / np.minimum(t + 1, w) for w in (2, 4, 8, 16)]), (P, 1)),
           "reset": np.tile((np.arange(4 * T) % P != 0), (P, 1)),
           "sel": np.concatenate([np.repeat(i == hd, P, 1) for hd in range(H)], 1),
           "eps": np.full((P, 1), EPS), "gn_eps": np.full((P, 1), GN_EPS)}
    cc = np.zeros((P, NCC), np.float32)
    for name, a in put.items():
        cc[:, CC[name]:CC[name] + a.shape[1]] = a

    xt = np.ascontiguousarray(f(x)[0].T.reshape(DT, P, T).transpose(1, 0, 2))
    nc = bacc.Bacc("TRN2", target_bir_lowering=False, num_devices=1)
    arrays, args = {}, []
    for name, a in (("x_in", xt), ("stream", stream), ("pp_in", pp), ("cc_in", cc), ("sw_in", sw), ("rep_in", rep)):
        arrays[name] = a
        args.append(nc.dram_tensor(name, a.shape, F32, kind="ExternalInput").ap())
    args.append(nc.dram_tensor("out", (P, DT, T), F32, kind="ExternalOutput").ap())
    trunk(nc, *args)
    r = run_bass_kernel_spmd(nc, [arrays], core_ids=[0])
    got = np.asarray(r.results[0]["out"])
    return np.ascontiguousarray(got.transpose(1, 0, 2).reshape(D, T).T)[None]
```

```python
from contextlib import ExitStack

import concourse.bass as bass
from concourse import mybir

F32 = mybir.dt.float32
ALU = mybir.AluOpType
ACT = mybir.ActivationFunctionType
AX_X = mybir.AxisListType.X

P = 128
T = 256
D = 1024
DT = D // P
L = 2
NCH = T // P
FF = 3584
FT = FF // P
E = 8
H = 8
HEADS = [0, 2, 4, 6, 1, 3, 5, 7]
CT = 14
CAP = 96
BLK = 16
CW = BLK * P
RING = 7
EPS = 1e-6
GN_EPS = 64e-5
DECAY = 0.6065306597126334
FLOOR = 1e-24

Z_UNITS = [("zg", 0), ("zg", 1), ("xbc", 0), ("xbc", 1), ("xbc", 2), ("xbc", 3), ("v", 0), ("v", 1), ("u", 0), ("u", 1),
           ("b", 0), ("b", 1)] + [("c", i) for i in range(CT // 2)]
NZ = len(Z_UNITS)
MERGE_ORDER = [0, 1, 3, 2]
STEPS = 8
N_MERGE = 3 * STEPS
SIDE = [("cw", 12), ("ss", 4), ("bo", 8), ("kt", 8)]
for _c in range(2):
    for _v in range(6):
        SIDE += [(f"t{_v}{_c}", 1), (f"z{_v}{_c}", 2)]
    SIDE += [(f"U{_c}", 1), (f"O{_c}", 1)]
SIDE += [("mu", 4), ("va", 4)]
N_OUT = DT // 2
N_MIX = NZ + N_MERGE + N_OUT
N_GU = FT
N_DOWN = DT * FT // BLK
N_FFN = N_GU + N_DOWN
FFN0 = N_MIX
MIX1 = N_MIX + N_FFN
MOE0 = MIX1 + N_MIX
N_CHUNKS = MOE0 + E * N_FFN

PP_LIST = [("norm_mix", 8), ("norm_ffn", 8), ("mix", 14), ("w0", 4), ("a0", 4), ("k_k", 4), ("k_a", 4), ("r_k", 4),
           ("ln_g", 4), ("ln_b", 4), ("conv_w", 32), ("conv_b", 8), ("norm_d", 4), ("skip", 4), ("b_scale", 4),
           ("norm_final", 8), ("dt_bias", 1), ("a_log", 1)]
PP, _n = {}, 0
for _name, _k in PP_LIST:
    PP[_name] = _n
    _n += _k
NPP = _n
LEVELS = 6
CC_LIST = [("ident", P), ("ones", T), ("heads", P), ("strict_up", P), ("incl_up", P), ("low2", P), ("up2", P),
           ("off", LEVELS * P), ("count", 4 * T), ("reset", 4 * T), ("sel", H * P), ("eps", 1), ("gn_eps", 1), ("slots", CAP), ("slot", 1)]
CC, _n = {}, 0
for _name, _k in CC_LIST:
    CC[_name] = _n
    _n += _k
NCC = _n
SW_LIST = [("w_s", 512), ("pool", 512), ("w2a2", 512), ("g2", 512), ("dt", 64), ("router", 64)]
SW, _n = {}, 0
for _name, _k in SW_LIST:
    SW[_name] = _n
    _n += _k
NSW = _n
NREP = 3 * 512

M_USES = ([("norm1", 0), ("dt", 1), ("cb", 2), ("xt0", 3), ("xt1", 0), ("bt", 1), ("dtT", 2)]
          + [(f"row{i}", (3 + i) % 4) for i in range(4)]
          + [("st", 3), ("yd0", 0), ("yd1", 1), ("dn", 2), ("a0", 3), ("a1", 0), ("b0", 1), ("b1", 2)]
          + [("cw0", 3), ("cw1", 0), ("ca0", 1), ("ca1", 2), ("cg0", 3), ("cg1", 0), ("ss0", 1), ("ss1", 2),
             ("bo0", 3), ("bo1", 0), ("vt0", 1), ("vt1", 2), ("kt", 3), ("nt", 0)])
for _c in range(NCH):
    M_USES += [(f"n0{_c}", 1), (f"n1{_c}", 2)] + [(f"s{_h}{_c}", (3 + _h) % 4) for _h in range(H)]
    for _v in range(LEVELS):
        M_USES += [(f"t0{_v}{_c}", 0), (f"t1{_v}{_c}", 1)]
        if _v < LEVELS - 1:
            M_USES += [(f"x0{_v}{_c}", 2)]
        M_USES += [(f"z0{_v}{_c}", 3)]
        if _v < LEVELS - 1:
            M_USES += [(f"x1{_v}{_c}", 0)]
        M_USES += [(f"z1{_v}{_c}", 1)]
    M_USES += [(f"W0{_c}", 2), (f"W1{_c}", 1), (f"U{_c}", 3), (f"O{_c}", 0)]
    if _c == 0:
        M_USES += [("S", 1)]
M_USES += [("mu0", 1), ("mu1", 2), ("va0", 3), ("va1", 0)]
M_USES += [("norm2", 0)]
G_USES = [((u, i), n % 4) for n, (u, i) in enumerate(Z_UNITS)]
for _s in range(STEPS):
    G_USES += [(("gate", _s, 0), 0), (("gate", _s, 1), 1), (("pj", _s, 0), 2), (("pj", _s, 1), 3)]
G_USES += [(("out", _i), _i) for _i in range(N_OUT)]


def bank_plan(uses):
    total, plan = [0] * 4, {}
    for stage, bank in uses:
        total[bank] += 1
        assert stage not in plan
        plan[stage] = (bank, total[bank])
    return plan, total


M_PLAN, M_TOTAL = bank_plan(M_USES)
SIDE_AT, _n = {}, 0
for _name, _k in SIDE:
    SIDE_AT[_name] = (_n, _n + _k)
    _n += _k
SIDE_END = _n
G_PLAN, G_TOTAL = bank_plan(G_USES)


def trunk(nc, x_in, stream, pp_in, cc_in, sw_in, rep_in, out):
    with ExitStack() as ctx:
        def sb(name, shape):
            return ctx.enter_context(nc.sbuf_tensor(name, shape, F32))

        def sem(name):
            return ctx.enter_context(nc.semaphore(name))

        x = sb("x", [P, DT, T])
        h = sb("h", [P, DT, T])
        ring = sb("ring", [P, RING, CW])
        cc = sb("cc", [P, NCC])
        pp = sb("pp", [P, L, NPP])
        sw = sb("sw", [P, NSW])
        rep = sb("rep", [P, NREP])
        rstd = sb("rstd", [P, T])
        rms = sb("rms", [P, T])
        small = sb("small", [P, 256])
        arena = sb("arena", [P, 28264])

        gbank = [ctx.enter_context(nc.psum_tensor(f"g{i}", [P, 512], F32)) for i in range(4)]
        mbank = [ctx.enter_context(nc.psum_tensor(f"m{i}", [P, 512], F32)) for i in range(4)]
        fbank = gbank + mbank

        def area(at, n):
            return arena[:, at:at + n]

        def tiles(at, n, w=T):
            return area(at, n * w).rearrange("p (n t) -> p n t", n=n)

        def const(name, n=P):
            return cc[:, CC[name]:CC[name] + n]

        def par(l, name, j=0, rows=P):
            return pp[0:rows, l, PP[name] + j:PP[name] + j + 1]

        def over(ap, n):
            return ap.unsqueeze(1).to_broadcast([ap.shape[0], n, ap.shape[1]])

        def along(ap, w):
            return ap.unsqueeze(2).to_broadcast([ap.shape[0], ap.shape[1], w])

        ident, ones, heads = const("ident"), const("ones"), const("heads")

        yA, yB, yC, yD = (tiles(i * 1024, 4) for i in range(4))
        zc = tiles(4096, CT, T + 1)
        zg = tiles(7696, 4)
        xbc = tiles(8720, 8, T + 3)
        vtok = tiles(10792, 2, 512)
        u = tiles(11816, 4)
        zb = tiles(12840, 4, T + 16)
        conv = tiles(13928, 8)
        dtw = area(15976, 1280)
        d_raw, d_abs, d_ln, d_dt, d_cs = (dtw[0:H, i * T:(i + 1) * T] for i in range(5))
        tok = area(17256, 32).rearrange("p (a c h) -> p a c h", a=2, c=NCH)
        d_end = area(17288, H)
        ahead = small[:, 120:122]
        cbm = tiles(17296, 4, P)
        xd = tiles(17808, 2, 512)
        btok = tiles(18832, 2, P)
        xde = area(19088, 512)
        mT = tiles(19600, H, P)
        seg = tiles(20624, H, P)
        cs = tiles(21648, H, P)
        st = tiles(22672, 2, T)
        seg1 = tiles(2048, H, P)
        p2 = tiles(23184, 4, T + 16)
        p4 = tiles(24000, 4, T + 16)
        ar = area(13928, 2048).rearrange("p (j c a t) -> p j c a t", j=4, c=NCH, a=2)
        nb = tiles(15976, 4)
        ka = tiles(17000, 4)
        cv = tiles(18024, 2, 512)
        kbt = tiles(19048, 2, 512)
        sc = area(20072, 4096).rearrange("p (h a t) -> p h a t", h=H, a=4)
        s0 = rms[:, :].rearrange("p (j f) -> p j f", j=4)
        wb = area(24168, 512)
        ub = area(24680, 512)
        xx = tiles(7696, H, P)
        zz = tiles(8720, H, P)
        tt = tiles(9744, H, P)
        bv = tiles(10792, 4)
        gg = tiles(11816, 4)
        oo = tiles(12840, 4)
        dif = tiles(20072, CT)
        w_log, c_sum, aa, kk = (tiles(20072 + i * 1024, 4) for i in range(4))
        e_in, e_neg, e_ex = (tiles(7696 + i * 1024, 4) for i in range(3))
        k2 = tiles(24168, 4)
        tmp1 = tiles(18024, 4)
        tmp2 = tiles(19048, 4)
        sg = area(25192, 1024).rearrange("p (b f) -> p b f", b=2)
        mg = tiles(26216, DT)
        sq = tiles(13928, DT)
        gbanks = [0, 1, 2, 3, 0, 1, 2]
        gu = tiles(4096, FT)
        sil = tiles(11264, RING)
        crow = tiles(18024, E)
        prow = tiles(20072, E)
        moe_tmp = area(16000, 512)
        routeT = area(16512, 1024)[0:E].rearrange("p (i t) -> p i t", i=4)
        rt = area(17536, 256)
        htok = area(22120, 2048).rearrange("p (c f) -> p c f", c=NCH)
        hg = tiles(24168, DT, CAP)
        put = area(13952, 2 * CAP).rearrange("p (c s) -> p c s", c=NCH)
        back = area(14144, T)[0:CAP]
        ytok = area(14400, D)[0:CAP]

        landed = [sem(f"landed{i}") for i in range(RING)]
        chunks_used = sem("chunks_used")
        g_drained = [sem(f"g_drained{i}") for i in range(4)]
        m_filled = [sem(f"m_filled{i}") for i in range(4)]
        m_drained = [sem(f"m_drained{i}") for i in range(4)]
        consts_in = sem("consts_in")
        x_loaded = sem("x_loaded")
        layer_in = sem("layer_in")
        padded = sem("padded")
        merged = sem("merged")
        sq_ready = sem("sq_ready")
        h_ready = sem("h_ready")
        x_mixed = sem("x_mixed")
        ffn_drained = sem("ffn_drained")
        silu_done = sem("silu_done")
        v_seq = sem("v_seq")
        a_seq = sem("a_seq")
        p_seq = sem("p_seq")
        out_stored = sem("out_stored")
        S = {n: sem(n) for n in (
            "conv_done conv_silu dt_raw dt_exp dt_soft ahead_ready cs_ready tok_ready seg_ready seg_exp "
            "mt_ready xd_ready d_endraw d_endexp xde_ready cbm_ready er_ready csc_ready yd_ready ydsq "
            "v_stats v_std vn_ready wm_ready ya_ready pooled zc_mixed lora_ready w_sig a_sig "
            "cum_ready e_ready kr_ready krsq ss_ready ss_sqrt rk_ready ab_ready x0_ready sc_ready t_ready z_ready x_ready "
            "s0_ready cent osq yc_ready gated b_done logits_top probs comb_ready combT_ready crow_ready "
            "em_ready out_ready ffn_x combs_done places rows_done tok_done htok_done flag_ready put_ready back_ready "
            "hg_filled hg_ready down_filled y_ready back_filled back_drained").split()}
        flag = ctx.enter_context(nc.sbuf_tensor("flag", [P, 2], mybir.dt.int32))

        def filled(eng, l, stage):
            bank, n = M_PLAN[stage]
            eng.wait_ge(m_filled[bank], l * M_TOTAL[bank] + n)

        def m_free(eng, l, stage):
            bank, n = M_PLAN[stage]
            if l * M_TOTAL[bank] + n > 1:
                eng.wait_ge(m_drained[bank], l * M_TOTAL[bank] + n - 1)

        def m_done(eng, l, stage):
            bank, n = M_PLAN[stage]
            eng.wait_ge(m_drained[bank], l * M_TOTAL[bank] + n)

        def g_free(eng, l, unit):
            bank, n = G_PLAN[unit]
            if l * G_TOTAL[bank] + n > 1:
                eng.wait_ge(g_drained[bank], l * G_TOTAL[bank] + n - 1)

        def g_done(eng, l, unit):
            bank, n = G_PLAN[unit]
            eng.wait_ge(g_drained[bank], l * G_TOTAL[bank] + n)

        def mb(stage):
            return mbank[M_PLAN[stage][0]]

        def gb(unit):
            return gbank[G_PLAN[unit][0]]

        def chunk0(l):
            return l * MIX1

        def unit_chunk(l, unit):
            c = chunk0(l)
            if unit == ("v", 0):
                unit = ("v", 1)
            if unit in Z_UNITS:
                return c + Z_UNITS.index(unit)
            if unit[0] == "gate":
                return c + NZ + 3 * unit[1] + unit[2]
            if unit[0] == "pj":
                return c + NZ + 3 * unit[1] + 2
            return c + NZ + N_MERGE + unit[1]

        class Count:
            def __init__(self, eng, own):
                self.eng, self.own, self.n = eng, own, {}

            def add(self, ins, s):
                ins.then_inc(s, 1)
                self.n[id(s)] = self.n.get(id(s), 0) + 1

            def step(self, ins, s=None):
                s = s or self.own
                self.add(ins, s)
                self.eng.wait_ge(s, self.n[id(s)])

        block = ctx.enter_context(nc.Block())

        @block.sync
        def _(sp):
            for s in range(RING):
                sp.dma_start(ring[:, s, :], stream[s]).then_inc(landed[s], 16)
            turns = N_CHUNKS // RING
            with sp.Fori(1, turns) as i:
                for s in range(RING):
                    sp.wait_ge(chunks_used, i * RING + (s - RING + 1))
                    sp.dma_start(ring[:, s, :], stream[i * RING + s]).then_inc(landed[s], 16)
            for n in range(turns * RING, N_CHUNKS):
                sp.wait_ge(chunks_used, n - RING + 1)
                sp.dma_start(ring[:, n % RING, :], stream[n]).then_inc(landed[n % RING], 16)
            sp.wait_ge(S["flag_ready"], 1)
            overflow = sp.value_load(flag[0:1, 0:1], min_val=0, max_val=1)
            with sp.If(overflow > 0):
                with sp.Fori(0, E * N_FFN // RING) as i:
                    for s in range(RING):
                        sp.wait_ge(chunks_used, i * RING + (N_CHUNKS + s - RING + 1))
                        slot = (N_CHUNKS + s) % RING
                        sp.dma_start(ring[:, slot, :], stream[i * RING + (MOE0 + s)]).then_inc(landed[slot], 16)

        @block.tensor
        def _(pe):
            pe.wait_ge(consts_in, 32)

            def mm(o, a, b, start=True, stop=True):
                return pe.matmul(o, a, b, start=start, stop=stop, skip_group_check=True)

            def chunk(n):
                pe.wait_ge(landed[n % RING], 16 * (n // RING + 1))
                return ring[:, n % RING, :].rearrange("p (b m) -> p b m", b=BLK)

            def fill(l, stage, last):
                last.then_inc(m_filled[M_PLAN[stage][0]], 1)

            def feature_sum(l, stage, mat, src, n, scale=1):
                m_free(pe, l, stage)
                for j in range(n):
                    last = mm(mb(stage)[:, 0:T], mat, src[:, j, :], j == 0, j == n - 1)
                fill(l, stage, last)

            def two_banks(l, name, lhs, rhs):
                for i in range(2):
                    m_free(pe, l, f"{name}{i}")
                    for j in (2 * i, 2 * i + 1):
                        last = mm(mb(f"{name}{i}")[:, (j % 2) * T:(j % 2 + 1) * T], lhs(j), rhs(j))
                    fill(l, f"{name}{i}", last)

            def turn(l, stage, parts):
                m_free(pe, l, stage)
                for i, src in enumerate(parts):
                    last = pe.transpose(mb(stage)[:, i * P:(i + 1) * P], src, ident)
                fill(l, stage, last)

            def project(l, lo, hi):
                for n in range(lo, hi):
                    name, i = Z_UNITS[n]
                    w = chunk(chunk0(l) + n)
                    if n == 0:
                        pe.wait_ge(h_ready, 2 * DT * l + DT)
                    if name == "v":
                        if i == 0:
                            g_free(pe, l, ("v", 0))
                            g_free(pe, l, ("v", 1))
                        wv = ring[:, (chunk0(l) + n) % RING, :].rearrange("p (k f) -> p k f", k=4)
                        for c in range(NCH):
                            for k in range(4):
                                last = mm(gb(("v", c))[:, :], h[:, 4 * i + k, c * P:(c + 1) * P], wv[:, k, :],
                                          i == 0 and k == 0, i == 1 and k == 3)
                    else:
                        g_free(pe, l, (name, i))
                        for j in range(2):
                            for k in range(DT):
                                last = mm(gb((name, i))[:, j * T:(j + 1) * T], w[:, DT * j + k, :], h[:, k, :],
                                          k == 0, k == DT - 1)
                    last.then_inc(chunks_used, 1)
                    if n == 1:
                        pe.wait_ge(layer_in, 32 * (l + 1))
                        m_free(pe, l, "dt")
                        for k in range(DT):
                            last = mm(mb("dt")[0:H, 0:T], sw[:, SW["dt"] + H * k:SW["dt"] + H * (k + 1)], h[:, k, :],
                                      k == 0, k == DT - 1)
                        fill(l, "dt", last)

            def mixer_d_rows(l):
                pe.wait_ge(S["conv_silu"], l + 1)
                m_free(pe, l, "cb")
                for g in range(2):
                    for c in range(NCH):
                        i = 2 * g + c
                        last = mm(mb("cb")[:, i * P:(i + 1) * P], conv[:, 4 + g, c * P:(c + 1) * P],
                                  conv[:, 6 + g, c * P:(c + 1) * P])
                fill(l, "cb", last)
                for c in range(NCH):
                    turn(l, f"xt{c}", [conv[:, j, c * P:(c + 1) * P] for j in range(4)])
                turn(l, "bt", [conv[:, 4 + g, 0:P] for g in range(2)])
                pe.wait_ge(S["cs_ready"], l + 1)
                m_free(pe, l, "dtT")
                for i, src in enumerate((d_dt, d_cs)):
                    for c in range(NCH):
                        last = pe.transpose(mb("dtT")[:, (2 * i + c) * H:(2 * i + c + 1) * H], src[:, c * P:(c + 1) * P],
                                            ident[0:H, 0:H])
                fill(l, "dtT", last)
                for i in range(4):
                    m_free(pe, l, f"row{i}")
                    for j in range(2):
                        hd = 2 * i + j
                        last = mm(mb(f"row{i}")[:, j * T:(j + 1) * T], cc[0:H, CC["sel"] + hd * P:CC["sel"] + (hd + 1) * P], d_cs)
                    fill(l, f"row{i}", last)

            def mixer_d_out(l):
                m_done(pe, l, "bt")
                pe.wait_ge(S["xde_ready"], l + 1)
                m_free(pe, l, "st")
                for g in range(2):
                    last = mm(mb("st")[:, g * T:(g + 1) * T], btok[:, g, :], xde[:, g * T:(g + 1) * T])
                fill(l, "st", last)
                for c in range(NCH):
                    pe.wait_ge(S["mt_ready"], 2 * (NCH * l + c + 1))
                    m_free(pe, l, f"yd{c}")
                    if c:
                        pe.wait_ge(S["csc_ready"], 2 * (l + 1))
                        m_done(pe, l, "st")
                    for hd in range(H):
                        q, j = 64 * (hd % 2), hd // 2
                        o = mb(f"yd{c}")[q:q + 64, j * P:(j + 1) * P]
                        last = mm(o, xd[:, c, hd * 64:(hd + 1) * 64], mT[:, hd, :], True, c == 0)
                        if c:
                            last = mm(o, st[:, hd // 4, (hd % 4) * 64:(hd % 4 + 1) * 64], cs[:, hd, :], False, True)
                    fill(l, f"yd{c}", last)

            def mixer_d_norm(l):
                pe.wait_ge(S["ydsq"], l + 1)
                feature_sum(l, "dn", ones, seg4, 4)

            seg4 = tiles(20840, 4)

            def mixer_a(l):
                pe.wait_ge(S["wm_ready"], l + 1)
                for c in range(NCH):
                    pe.wait_ge(S["vn_ready"], NCH * l + c + 1)
                    m_free(pe, l, f"a{c}")
                    for g in range(4):
                        last = mm(mb(f"a{c}")[:, g * P:(g + 1) * P], vtok[:, c, g * P:(g + 1) * P],
                                  sw[:, SW["w_s"] + g * P:SW["w_s"] + (g + 1) * P])
                    fill(l, f"a{c}", last)

            def mixer_b(l):
                pe.wait_ge(S["pooled"], l + 1)
                two_banks(l, "b", lambda j: sw[:, SW["pool"] + j * P:SW["pool"] + (j + 1) * P], lambda j: yB[:, j, :])

            def mixer_c(l):
                def side(point):
                    merge_quarters(l, *SIDE_AT[point])

                side("cw")
                pe.wait_ge(S["lora_ready"], 2 * (l + 1))
                w2 = sw[0:64, SW["w2a2"]:SW["w2a2"] + 512]
                a2 = sw[64:P, SW["w2a2"]:SW["w2a2"] + 512]
                two_banks(l, "cw", lambda j: w2[:, j * P:(j + 1) * P], lambda j: zc[0:64, 12, 1:T + 1])
                two_banks(l, "ca", lambda j: a2[:, j * P:(j + 1) * P], lambda j: zc[64:P, 12, 1:T + 1])
                two_banks(l, "cg", lambda j: sw[:, SW["g2"] + j * P:SW["g2"] + (j + 1) * P], lambda j: zc[:, 13, 1:T + 1])
                side("ss")
                pe.wait_ge(S["krsq"], l + 1)
                two_banks(l, "ss", lambda j: heads, lambda j: tmp1[:, j, :])
                side("bo")
                pe.wait_ge(S["rk_ready"], l + 1)
                two_banks(l, "bo", lambda j: heads, lambda j: tmp2[:, j, :])
                for c in range(NCH):
                    turn(l, f"vt{c}", [zc[:, 8 + j, 1 + c * P:1 + (c + 1) * P] for j in range(4)])
                side("kt")
                pe.wait_ge(S["ab_ready"], l + 1)
                turn(l, "kt", [ka[:, j, 0:P] for j in range(4)])
                turn(l, "nt", [nb[:, j, 0:P] for j in range(4)])
                for c in range(NCH):
                    tc = slice(c * P, (c + 1) * P)
                    half = lambda hd: slice(64 * (hd % 2), 64 * (hd % 2) + 64)
                    for q in range(2):
                        m_free(pe, l, f"n{q}{c}")
                        for i in range(4):
                            hd = HEADS[4 * q + i]
                            last = mm(mb(f"n{q}{c}")[:, i * P:(i + 1) * P], ar[half(hd), hd // 2, c, 0, :], nb[half(hd), hd // 2, tc])
                        fill(l, f"n{q}{c}", last)
                    for slot in range(H):
                        hd, st_ = HEADS[slot], f"s{slot}{c}"
                        m_free(pe, l, st_)
                        both = ar[half(hd), hd // 2, c, :, :].rearrange("p a t -> p (a t)")
                        mm(mb(st_)[:, 0:T], nb[half(hd), hd // 2, tc], both)
                        last = mm(mb(st_)[:, T:2 * T], ka[half(hd), hd // 2, tc], both)
                        fill(l, st_, last)
                    for v in range(LEVELS):
                        base = (NCH * l + c) * LEVELS + v
                        side(f"t{v}{c}")
                        for q in range(2):
                            pe.wait_ge(S["x_ready"], 2 * base + q + 1)
                            if v == 0:
                                pe.wait_ge(S["sc_ready"], H * (NCH * l + c) + 4 * q + 4)
                            m_free(pe, l, f"t{q}{v}{c}")
                            for i in range(4):
                                s_ = 4 * q + i
                                last = mm(mb(f"t{q}{v}{c}")[:, i * P:(i + 1) * P], sc[:, s_, 0, :], xx[:, s_, :])
                            fill(l, f"t{q}{v}{c}", last)
                        side(f"z{v}{c}")
                        for q in range(2):
                            pe.wait_ge(S["z_ready"], 2 * base + 2 * (NCH * l + c) + q + 1)
                            pe.wait_ge(S["t_ready"], 2 * base + q + 1)
                            if v < LEVELS - 1:
                                m_free(pe, l, f"x{q}{v}{c}")
                                for i in range(4):
                                    s_ = 4 * q + i
                                    last = mm(mb(f"x{q}{v}{c}")[:, i * P:(i + 1) * P], zz[:, s_, :], tt[:, s_, :])
                                fill(l, f"x{q}{v}{c}", last)
                            m_free(pe, l, f"z{q}{v}{c}")
                            for i in range(4):
                                s_ = 4 * q + i
                                last = mm(mb(f"z{q}{v}{c}")[:, i * P:(i + 1) * P], tt[:, s_, :], zz[:, s_, :])
                            fill(l, f"z{q}{v}{c}", last)
                    if c == 0:
                        m_done(pe, l, "vt0")
                        m_done(pe, l, "vt1")
                    else:
                        pe.wait_ge(S["s0_ready"], l + 1)
                    for q in range(2):
                        m_free(pe, l, f"W{q}{c}")
                        for i in range(4):
                            slot = 4 * q + i
                            hd = HEADS[slot]
                            o = mb(f"W{q}{c}")[:, i * 64:(i + 1) * 64]
                            last = mm(o, sc[:, slot, 2, :], cv[:, c, hd * 64:(hd + 1) * 64], True, c == 0)
                            if c:
                                last = mm(o, ar[half(hd), hd // 2, c, 0, :], s0[half(hd), hd // 2, :], False, True)
                        fill(l, f"W{q}{c}", last)
                    side(f"U{c}")
                    pe.wait_ge(S["z_ready"], 2 * (LEVELS + 1) * (NCH * l + c + 1))
                    m_done(pe, l, f"W0{c}")
                    m_done(pe, l, f"W1{c}")
                    m_free(pe, l, f"U{c}")
                    for slot, hd in enumerate(HEADS):
                        last = mm(mb(f"U{c}")[:, hd * 64:(hd + 1) * 64], zz[:, slot, :], wb[:, slot * 64:(slot + 1) * 64])
                    fill(l, f"U{c}", last)
                    side(f"O{c}")
                    m_done(pe, l, f"U{c}")
                    m_free(pe, l, f"O{c}")
                    for slot, hd in enumerate(HEADS):
                        o = mb(f"O{c}")[half(hd), (hd // 2) * P:(hd // 2 + 1) * P]
                        mm(o, cv[:, c, hd * 64:(hd + 1) * 64], sc[:, slot, 3, :], True, False)
                        last = mm(o, ub[:, hd * 64:(hd + 1) * 64], sc[:, slot, 1, :], False, c == 0)
                        if c:
                            last = mm(o, s0[half(hd), hd // 2, :], ar[half(hd), hd // 2, c, 1, :], False, True)
                    fill(l, f"O{c}", last)
                    if c == 0:
                        m_done(pe, l, "kt")
                        m_done(pe, l, "nt")
                        m_free(pe, l, "S")
                        for hd in range(H):
                            o = mb("S")[half(hd), (hd // 2) * 64:(hd // 2 + 1) * 64]
                            mm(o, kbt[:, 0, hd * 64:(hd + 1) * 64], cv[:, 0, hd * 64:(hd + 1) * 64], True, False)
                            last = mm(o, kbt[:, 1, hd * 64:(hd + 1) * 64], ub[:, hd * 64:(hd + 1) * 64], False, True)
                        fill(l, "S", last)
                side("mu")
                m_done(pe, l, "O1")
                two_banks(l, "mu", lambda j: heads, lambda j: oo[:, j, :])
                side("va")
                pe.wait_ge(S["osq"], l + 1)
                two_banks(l, "va", lambda j: heads, lambda j: tiles(7696, 4)[:, j, :])

            ys = [yA, yB, yC, yD]

            def merge_quarters(l, lo, hi):
                for n in range(lo, hi):
                    step, unit, part = n // 12, n % 12 // 4, n % 4
                    w = chunk(chunk0(l) + NZ + n // 4)
                    if unit < 2:
                        if part == 0:
                            g_free(pe, l, ("gate", step, unit))
                        j = part // 2
                        for k in range(4 * (part % 2), 4 * (part % 2) + 4):
                            last = mm(gb(("gate", step, unit))[:, j * T:(j + 1) * T], w[:, DT * j + k, :], h[:, k, :],
                                      k == 0, k == DT - 1)
                    else:
                        branch = MERGE_ORDER[step // 2]
                        if part == 0:
                            if branch == 0:
                                pe.wait_ge(S["ya_ready"], NCH * (l + 1))
                            elif branch == 1:
                                m_done(pe, l, "b0")
                                m_done(pe, l, "b1")
                            elif branch == 2:
                                pe.wait_ge(S["yc_ready"], l + 1)
                            else:
                                pe.wait_ge(S["yd_ready"], 4 * (l + 1))
                        if part % 2 == 0:
                            g_free(pe, l, ("pj", step, part // 2))
                        for k in range(4):
                            last = mm(gb(("pj", step, part // 2))[:, (part % 2) * T:(part % 2 + 1) * T], w[:, 4 * part + k, :],
                                      ys[branch][:, k, :], k == 0, k == 3)
                    if part == 3:
                        last.then_inc(chunks_used, 1)

            def merge(l):
                merge_quarters(l, SIDE_END, 12 * STEPS)
                for i in range(N_OUT):
                    w = chunk(chunk0(l) + NZ + N_MERGE + i)
                    if i == 0:
                        pe.wait_ge(merged, 2 * STEPS * (l + 1))
                    g_free(pe, l, ("out", i))
                    for j in range(2):
                        for k in range(DT):
                            last = mm(gb(("out", i))[:, j * T:(j + 1) * T], w[:, DT * j + k, :], mg[:, k, :],
                                      k == 0, k == DT - 1)
                    last.then_inc(chunks_used, 1)

            def norm_sum(l, stage, n):
                pe.wait_ge(sq_ready, n)
                feature_sum(l, stage, ones, sq, DT)

            def slot_of(first, n, turn_of, more=0):
                pe.wait_ge(landed[(first + n) % RING], turn_of * 16 + more + 16 * ((first + n) // RING + 1))
                return ring[:, (first + n) % RING, :].rearrange("p (b m) -> p b m", b=BLK)

            def gate_up(first, turn_of, unit, s, i, tokens, width):
                w = slot_of(first, s, turn_of, i * 16)
                if not (isinstance(i, int) and isinstance(unit, int) and unit + i * RING + s < 3):
                    pe.wait_ge(ffn_drained, unit + i * RING + (s - 2))
                bank = gbank[gbanks[s]]
                for j in range(2):
                    for k in range(DT):
                        last = mm(bank[:, j * T:j * T + width], w[:, DT * j + k, :], tokens[:, k, :], k == 0, k == DT - 1)
                last.then_inc(chunks_used, 1)

            def hidden_ready(unit, k):
                if k == 0 or k > FT - RING:
                    pe.wait_ge(ffn_drained, unit + (FT - RING + 1 if k == 0 else k + 1))

            def ffn(first, turn_of, unit):
                start = 0
                if isinstance(unit, int):
                    for s in range(RING):
                        gate_up(first, turn_of, unit, s, 0, h, T)
                    start = 1
                with pe.Fori(start, FT // RING) as i:
                    for s in range(RING):
                        gate_up(first, turn_of, unit, s, i, h, T)
                for k in range(FT):
                    if k % 2 == 0:
                        w = slot_of(first, N_GU + k // 2, turn_of)
                    hidden_ready(unit, k)
                    for d in range(DT):
                        last = mm(mbank[d // 2][:, (d % 2) * T:(d % 2 + 1) * T], w[:, (k % 2) * DT + d, :], gu[:, k, :],
                                  k == 0 and d % 2 == 0, k == FT - 1)
                    if k % 2:
                        last.then_inc(chunks_used, 1)

            def gather(done):
                for i in range(2):
                    for j in range(4):
                        for c in range(NCH):
                            k = 4 * i + j
                            last = mm(mbank[i][:, j * CAP:(j + 1) * CAP], htok[:, c, k * P:(k + 1) * P], put[:, c, :], c == 0, c == 1)
                    last.then_inc(S["hg_filled"], 1)

            def experts():
                pe.wait_ge(S["put_ready"], 1)
                gather(0)
                hid0 = FT + 4
                with pe.Fori(0, E) as e:
                    turn_of, unit = e * (N_FFN // RING), e * FT + hid0
                    with pe.Fori(0, FT // RING) as i:
                        pe.wait_ge(S["hg_ready"], e * 2 + 2)
                        for s in range(RING):
                            gate_up(MOE0, turn_of, unit, s, i, hg, CAP)
                    for k in range(FT):
                        if k % 2 == 0:
                            slot_of(MOE0, N_GU + k // 2, turn_of)
                        hidden_ready(unit, k)
                        wd = ring[:, (MOE0 + N_GU + k // 2) % RING, :].rearrange("p (k f) -> p k f", k=4)
                        for i in range(2):
                            last = mm(mbank[2 + i][0:CAP, :], gu[:, k, 0:CAP], wd[:, 2 * (k % 2) + i, :], k == 0, k == FT - 1)
                        if k % 2:
                            last.then_inc(chunks_used, 1)
                    pe.wait_ge(S["put_ready"], e + 2)
                    gather(0)
                    pe.wait_ge(S["y_ready"], e * 2 + 2)
                    pe.wait_ge(S["back_ready"], e + 1)
                    pe.wait_ge(S["hg_ready"], e * 2 + 4)
                    for i in range(4):
                        if i >= 2:
                            pe.wait_ge(S["back_drained"], e * 4 + (i - 1))
                        for j in range(2):
                            k = 2 * i + j
                            last = mm(mbank[i % 2][:, j * T:(j + 1) * T], ytok[:, k * P:(k + 1) * P], back)
                        last.then_inc(S["back_filled"], 1)

            def router():
                for c in range(NCH):
                    for k in range(DT):
                        last = mm(mbank[1][:, c * E:(c + 1) * E], h[:, k, c * P:(c + 1) * P],
                                  sw[:, SW["router"] + E * k:SW["router"] + E * (k + 1)], k == 0, k == DT - 1)
                last.then_inc(m_filled[1], 1)
                for c in range(NCH):
                    for i in range(2):
                        for j in range(4):
                            last = pe.transpose(gbank[2 * c + i][:, j * P:(j + 1) * P], h[:, 4 * i + j, c * P:(c + 1) * P], ident)
                        last.then_inc(S["htok_done"], 1)
                pe.wait_ge(S["comb_ready"], 1)
                for c in range(NCH):
                    last = pe.transpose(mbank[2][0:E, c * P:(c + 1) * P], rt_comb[:, c, :], ident)
                last.then_inc(m_filled[2], 1)
                pe.wait_ge(S["places"], 1)
                sel = lambda e: cc[0:E, CC["sel"] + e * P:CC["sel"] + (e + 1) * P]
                for i in range(4):
                    pe.wait_ge(g_drained[i], L * G_TOTAL[i] + 1)
                for e in range(E):
                    last = mm(gbank[e // 2][:, (e % 2) * T:(e % 2 + 1) * T], sel(e), routeT[:, 0, :])
                last.then_inc(S["combs_done"], 1)
                for c in range(NCH):
                    last = pe.transpose(mbank[0][:, c * E:(c + 1) * E], routeT[:, 3, c * P:(c + 1) * P], ident[0:E, 0:E])
                last.then_inc(S["tok_done"], 1)
                pe.wait_ge(S["crow_ready"], 1)
                for e in range(E):
                    last = mm(gbank[e // 2][:, (e % 2) * T:(e % 2 + 1) * T], sel(e), routeT[:, 3, :])
                last.then_inc(S["rows_done"], 1)

            rt_comb = rt[:, 0:2 * E].rearrange("p (c e) -> p c e", c=NCH)

            for l in range(L):
                norm_sum(l, "norm1", 2 * l + 1)
                project(l, 0, 14)
                mixer_d_rows(l)
                project(l, 14, 16)
                mixer_d_out(l)
                project(l, 16, 17)
                mixer_d_norm(l)
                mixer_a(l)
                project(l, 17, 18)
                mixer_b(l)
                project(l, 18, NZ)
                mixer_c(l)
                merge(l)
                norm_sum(l, "norm2", 2 * l + 2)
                pe.wait_ge(h_ready, 2 * DT * l + 2 * DT)
                for i in range(4):
                    pe.wait_ge(g_drained[i], (l + 1) * G_TOTAL[i])
                    pe.wait_ge(m_drained[i], (l + 1) * M_TOTAL[i])
                if l == 0:
                    ffn(FFN0, 0, 0)
                else:
                    router()
                    pe.wait_ge(S["flag_ready"], 1)
                    overflow = pe.value_load(flag[0:1, 0:1], min_val=0, max_val=1)
                    experts()
                    with pe.If(overflow > 0):
                        with pe.Fori(0, E) as e:
                            ffn(MOE0, (e + E) * (N_FFN // RING), e * (FT + 4) + (FT + 4 + E * FT))
            pe.wait_ge(sq_ready, 2 * L + 1)
            for j in range(DT):
                last = mm(mbank[0][:, 0:T], ones, sq[:, j, :], j == 0, j == DT - 1)
            last.then_inc(m_filled[0], 1)

        @block.scalar
        def _(act):
            q = Count(act, a_seq)
            A = nc.scalar.activation

            act.dma_start(x[:, :, :], x_in).then_inc(x_loaded, 16)
            act.dma_start(cc[:, :], cc_in).then_inc(consts_in, 16)
            act.dma_start(pp[:, :, :], pp_in).then_inc(consts_in, 16)
            act.dma_start(sw[:, :], sw_in[0]).then_inc(layer_in, 16)
            act.dma_start(rep[:, :], rep_in[0]).then_inc(layer_in, 16)
            act.wait_ge(consts_in, 32)
            eps = cc[:, CC["eps"]:CC["eps"] + 1]
            gn_eps = cc[:, CC["gn_eps"]:CC["gn_eps"] + 1]

            def drain(l, stage, ins):
                q.add(ins, m_drained[M_PLAN[stage][0]])

            def norm(stage_filled, root):
                q.add(A(sq[:, :, :], x[:, :, :], ACT.Square), sq_ready)
                stage_filled()
                root(A(rms[:, :], mbank[0][:, 0:T], ACT.Sqrt, scale=1.0 / D, bias=eps))

            def evacuate(l, units):
                for unit in units:
                    name, i = unit
                    act.wait_ge(chunks_used, unit_chunk(l, unit) + 1)
                    src = gb(unit)[:, :]
                    two = src.rearrange("p (j t) -> p j t", j=2)
                    if name == "zg":
                        ins = A(zg[:, 2 * i:2 * i + 2, :], two, ACT.Silu)
                    elif name == "xbc":
                        ins = A(xbc[:, 2 * i:2 * i + 2, 3:T + 3], two, ACT.Copy)
                    elif name == "v":
                        ins = A(vtok[:, i, :], src, ACT.Gelu_apprx_tanh)
                    elif name == "u":
                        ins = A(u[:, 2 * i:2 * i + 2, :], two, ACT.Gelu_apprx_tanh)
                    elif name == "b":
                        ins = A(zb[:, 2 * i:2 * i + 2, 16:T + 16], two, ACT.Copy)
                    else:
                        ins = A(zc[:, 2 * i:2 * i + 2, 1:T + 1], two, ACT.Copy)
                    q.add(ins, g_drained[G_PLAN[unit][0]])

            def mixer_d_dt(l):
                act.wait_ge(S["dt_raw"], l + 1)
                q.step(A(d_abs, d_raw, ACT.Abs))
                q.step(A(d_abs, d_abs, ACT.Exp, scale=-1.0))
                q.step(A(ahead[0:H, 0:1], par(l, "a_log", rows=H), ACT.Exp))
                q.step(A(d_ln, d_abs, ACT.Ln, bias=1.0), S["dt_exp"])

            def mixer_d(l):
                act.wait_ge(S["conv_done"], l + 1)
                q.add(A(conv[:, :, :], conv[:, :, :], ACT.Silu), S["conv_silu"])
                evacuate(l, Z_UNITS[12:14])
                filled(act, l, "bt")
                drain(l, "bt", A(btok[:, :, :], mb("bt")[:, 0:T].rearrange("p (g n) -> p g n", g=2), ACT.Copy))
                evacuate(l, Z_UNITS[14:16])
                act.wait_ge(S["d_endraw"], l + 1)
                q.step(A(d_end, d_end, ACT.Exp), S["d_endexp"])
                for c in range(NCH):
                    act.wait_ge(S["seg_ready"], NCH * l + c + 1)
                    q.step(A(mT[:, :, :], seg[:, :, :], ACT.Exp), S["seg_exp"])
                    if c == 0:
                        filled(act, l, "st")
                        drain(l, "st", A(st[:, :, :], mb("st")[:, :].rearrange("p (g n) -> p g n", g=2), ACT.Copy))
                        act.wait_ge(S["csc_ready"], 2 * l + 1)
                        q.step(A(cs[:, :, :], cs[:, :, :], ACT.Exp), S["er_ready"])
                evacuate(l, Z_UNITS[16:17])
                act.wait_ge(S["yd_ready"], 4 * l + 1)
                q.add(A(tiles(20840, 4)[:, :, :], yD[:, :, :], ACT.Square), S["ydsq"])
                filled(act, l, "dn")
                drain(l, "dn", A(rms[:, :], mb("dn")[:, 0:T], ACT.Sqrt, scale=1.0 / 512, bias=eps))

            def mixer_a(l):
                act.wait_ge(S["v_stats"], l + 1)
                q.add(A(small[:, 16:18], small[:, 16:18], ACT.Sqrt, bias=eps), S["v_std"])

            def mixer_b(l):
                for i in range(2):
                    filled(act, l, f"b{i}")
                    for j in range(2):
                        ins = A(yB[:, 2 * i + j, :], mb(f"b{i}")[:, j * T:(j + 1) * T], ACT.Copy, scale=par(l, "b_scale", 2 * i + j))
                        (q.add(ins, a_seq) if j == 0 else drain(l, f"b{i}", ins))

            def mixer_c(l):
                def side(first, last=None):
                    gates(l, SIDE_AT[first][0], SIDE_AT[last or first][1])

                side("cw")
                act.wait_ge(S["zc_mixed"], l + 1)
                q.add(A(zc[0:64, 12, 1:T + 1], zc[0:64, 12, 1:T + 1], ACT.Tanh), S["lora_ready"])
                q.add(A(zc[:, 13, 1:T + 1], zc[:, 13, 1:T + 1], ACT.Sigmoid), S["lora_ready"])
                for name, dst, bias, done in (("cw", w_log, "w0", "w_sig"), ("ca", aa, "a0", "a_sig")):
                    for i in range(2):
                        filled(act, l, f"{name}{i}")
                        for j in range(2):
                            ins = A(dst[:, 2 * i + j, :], mb(f"{name}{i}")[:, j * T:(j + 1) * T], ACT.Sigmoid,
                                    bias=par(l, bias, 2 * i + j))
                            (q.add(ins, a_seq) if j == 0 else drain(l, f"{name}{i}", ins))
                for i in range(2):
                    filled(act, l, f"cg{i}")
                    drain(l, f"cg{i}", A(gg[:, 2 * i:2 * i + 2, :], mb(f"cg{i}")[:, :].rearrange("p (j t) -> p j t", j=2), ACT.Copy))
                side("ss")
                act.wait_ge(S["kr_ready"], l + 1)
                q.add(A(tmp1[:, :, :], kk[:, :, :], ACT.Square), S["krsq"])
                act.wait_ge(S["ss_ready"], l + 1)
                q.add(A(tmp1[:, :, :], tmp1[:, :, :], ACT.Sqrt), S["ss_sqrt"])
                side("bo")
                act.wait_ge(S["cum_ready"], l + 1)
                q.add(A(e_in[:, :, :], c_sum[:, :, :], ACT.Exp), S["e_ready"])
                q.add(A(e_neg[:, :, :], c_sum[:, :, :], ACT.Exp, scale=-1.0), S["e_ready"])
                q.add(A(e_ex[:, :, :], w_log[:, :, :], ACT.Exp), S["e_ready"])
                q.add(A(small[:, 28:32], small[:, 28:32], ACT.Exp), S["e_ready"])
                act.wait_ge(S["ab_ready"], l + 1)
                m_done(act, l, "bo1")
                for c in range(NCH):
                    filled(act, l, f"vt{c}")
                    drain(l, f"vt{c}", A(cv[:, c, :], mb(f"vt{c}")[:, :], ACT.Copy))
                side("kt")
                for i, name in enumerate(("kt", "nt")):
                    filled(act, l, name)
                    drain(l, name, A(kbt[:, i, :], mb(name)[:, :], ACT.Copy))
                for c in range(NCH):
                    side(f"t0{c}", f"z{LEVELS - 1}{c}")
                    filled(act, l, f"W0{c}")
                    filled(act, l, f"W1{c}")
                    if c == 0:
                        act.wait_ge(S["ab_ready"], l + 1)
                    else:
                        filled(act, l, "S")
                    for i in range(2):
                        drain(l, f"W{i}{c}", A(wb[:, i * T:(i + 1) * T], mb(f"W{i}{c}")[:, 0:T], ACT.Copy))
                    side(f"U{c}")
                    filled(act, l, f"U{c}")
                    drain(l, f"U{c}", A(ub, mb(f"U{c}")[:, :], ACT.Copy))
                    side(f"O{c}")
                    filled(act, l, f"O{c}")
                    drain(l, f"O{c}", A(oo[:, :, c * P:(c + 1) * P], mb(f"O{c}")[:, :].rearrange("p (j t) -> p j t", j=4), ACT.Copy))
                side("mu")
                act.wait_ge(S["cent"], 2 * (l + 1))
                q.add(A(tiles(7696, 4)[:, :, :], oo[:, :, :], ACT.Square), S["osq"])
                side("va")
                for i in range(2):
                    filled(act, l, f"va{i}")
                    drain(l, f"va{i}", A(tiles(8720, 4)[:, 2 * i:2 * i + 2, :], mb(f"va{i}")[:, :].rearrange("p (j t) -> p j t", j=2),
                                         ACT.Sqrt, scale=1.0 / 64, bias=gn_eps))

            def gates(l, lo, hi):
                for n in range(2 * STEPS):
                    step, i = n // 2, n % 2
                    if lo < 12 * step + 4 * i + 4 <= hi:
                        unit = ("gate", step, i)
                        act.wait_ge(chunks_used, unit_chunk(l, unit) + 1)
                        if 2 * STEPS * l + n > 1:
                            act.wait_ge(merged, 2 * STEPS * l + n - 1)
                        q.add(A(sg[:, i, :], gb(unit)[:, :], ACT.Sigmoid), g_drained[G_PLAN[unit][0]])

            def silus(first, e42, width):
                with act.Fori(0, FT // RING) as i:
                    for s in range(RING):
                        act.wait_ge(chunks_used, e42 + i * RING + (first + s + 1))
                        A(sil[:, s, 0:width], gbank[gbanks[s]][:, 0:width], ACT.Silu).then_inc(silu_done, 1)

            def gathered():
                for i in range(2):
                    A(hg[:, 4 * i:4 * i + 4, :], mbank[i][:, 0:4 * CAP].rearrange("p (j s) -> p j s", j=4), ACT.Copy)\
                        .then_inc(S["hg_ready"], 1)

            def experts():
                act.wait_ge(S["hg_filled"], 2)
                gathered()
                with act.Fori(0, E) as e:
                    silus(MOE0, e * N_FFN, CAP)
                    act.wait_ge(chunks_used, e * N_FFN + (MOE0 + N_FFN))
                    for i in range(2):
                        A(ytok[:, i * 512:(i + 1) * 512], mbank[2 + i][0:CAP, :], ACT.Copy).then_inc(S["y_ready"], 1)
                    act.wait_ge(S["hg_filled"], e * 2 + 4)
                    gathered()

            for l in range(L):
                if l == 0:
                    act.wait_ge(x_loaded, 16)
                else:
                    act.wait_ge(S["ffn_x"], 4)
                norm(lambda: filled(act, l, "norm1"), lambda ins: drain(l, "norm1", ins))
                act.wait_ge(padded, 3 * (l + 1))
                evacuate(l, Z_UNITS[:10])
                mixer_d_dt(l)
                evacuate(l, Z_UNITS[10:12])
                mixer_d(l)
                mixer_a(l)
                evacuate(l, Z_UNITS[17:18])
                mixer_b(l)
                evacuate(l, Z_UNITS[18:])
                mixer_c(l)
                if l == 0:
                    m_done(act, l, "S")
                    act.wait_ge(S["ya_ready"], NCH)
                    act.dma_start(sw[:, :], sw_in[1]).then_inc(layer_in, 16)
                    act.dma_start(rep[:, :], rep_in[1]).then_inc(layer_in, 16)
                gates(l, SIDE_END, 12 * STEPS)
                act.wait_ge(x_mixed, N_OUT * (l + 1))
                norm(lambda: filled(act, l, "norm2"), lambda ins: drain(l, "norm2", ins))
                if l == 0:
                    silus(FFN0, 0, T)
                else:
                    act.wait_ge(S["logits_top"], 1)
                    q.step(A(small[:, 40:42], small[:, 36:38], ACT.Sigmoid))
                    q.add(A(small[:, 42:44], small[:, 36:38], ACT.Sigmoid, scale=-1.0), S["probs"])
                    act.wait_ge(S["htok_done"], 4)
                    for i in range(4):
                        q.add(A(htok[:, i // 2, (i % 2) * 512:(i % 2 + 1) * 512], gbank[i][:, :], ACT.Copy), g_drained[i])
                    act.wait_ge(S["flag_ready"], 1)
                    overflow = act.value_load(flag[0:1, 0:1], min_val=0, max_val=1)
                    experts()
                    with act.If(overflow > 0):
                        with act.Fori(0, E) as e:
                            silus(MOE0, (e + E) * N_FFN, T)
            act.wait_ge(S["ffn_x"], 8)
            norm(lambda: act.wait_ge(m_filled[0], L * M_TOTAL[0] + 1), lambda ins: q.add(ins, m_drained[0]))
            act.wait_ge(S["out_ready"], DT)
            act.dma_start(out, h[:, :, :]).then_inc(out_stored, 16)
            act.wait_ge(out_stored, 16)

        @block.gpsimd
        def _(pool):
            q = Count(pool, p_seq)
            G = nc.gpsimd
            pool.wait_ge(consts_in, 32)
            for l in range(L):
                if l:
                    pool.wait_ge(S["ffn_x"], 4)
                q.add(G.memset(zc[:, :, 0:1], 0.0), padded)
                q.add(G.memset(xbc[:, :, 0:3], 0.0), padded)
                q.add(G.memset(zb[:, :, 0:16], 0.0), padded)
                g_done(pool, l, ("b", 0))
                g_done(pool, l, ("b", 1))
                pool.wait_ge(padded, 3 * (l + 1))
                w = T + 16
                q.step(G.tensor_tensor(p2[:, :, 1:w], zb[:, :, 1:w], zb[:, :, 0:w - 1], ALU.add))
                q.step(G.tensor_tensor(p4[:, 1:4, 3:w], p2[:, 1:4, 3:w], p2[:, 1:4, 1:w - 2], ALU.add))
                q.step(G.tensor_tensor(p2[:, 2:4, 7:w], p4[:, 2:4, 7:w], p4[:, 2:4, 3:w - 4], ALU.add))
                q.step(G.tensor_tensor(p4[:, 3:4, 15:w], p2[:, 3:4, 15:w], p2[:, 3:4, 7:w - 8], ALU.add))
                count = cc[:, CC["count"]:CC["count"] + 4 * T].rearrange("p (g t) -> p g t", g=4)
                for g, src in enumerate((p2, p4, p2, p4)):
                    q.step(G.tensor_tensor(yB[:, g, :], src[:, g, 16:w], count[:, g, :], ALU.mult))
                q.step(G.tensor_tensor(yB[:, :, :], yB[:, :, :], zb[:, :, 16:w], ALU.subtract), S["pooled"])
                for n in range(4, 2 * STEPS):
                    pool.wait_ge(S["gated"], (2 * STEPS - 4) * l + n - 3)
                    pool.wait_ge(merged, 2 * STEPS * l + n)
                    m2 = mg[:, 2 * (n % 4):2 * (n % 4) + 2, :]
                    G.tensor_tensor(m2, sg[:, n % 2, :].rearrange("p (j t) -> p j t", j=2), m2, ALU.add).then_inc(merged, 1)

        @block.vector
        def _(dve):
            q = Count(dve, v_seq)
            V = nc.vector
            TT = V.tensor_tensor

            def marker():
                return V.tensor_copy(small[:, 60:61], small[:, 61:62])

            q.step(V.memset(small[:, 60:62], 0.0))
            dve.wait_ge(consts_in, 32)

            def drain(stage, ins):
                q.add(ins, m_drained[M_PLAN[stage][0]])

            def drained_step(stage, ins):
                q.step(ins, m_drained_own[M_PLAN[stage][0]])

            def norm(root_done, gain, done):
                root_done()
                q.step(V.reciprocal(rstd[:, :], rms[:, :]))
                for k in range(DT):
                    q.add(V.scalar_tensor_tensor(h[:, k, :], x[:, k, :], gain(k), rstd[:, :], ALU.mult, ALU.mult), done)

            def mixer_d_dt(l):
                filled(dve, l, "dt")
                drain("dt", V.tensor_scalar(d_raw, mb("dt")[0:H, 0:T], par(l, "dt_bias", rows=H), None, ALU.add))
                m_done(dve, l, "dt")
                q.step(V.tensor_copy(d_raw, d_raw), S["dt_raw"])
                dve.wait_ge(S["dt_exp"], l + 1)
                q.step(V.scalar_tensor_tensor(d_dt, d_raw, 0.0, d_ln, ALU.max, ALU.add))
                q.step(V.tensor_scalar(d_abs, d_dt, ahead[0:H, 0:1], -1.0, ALU.mult, ALU.mult))
                q.step(V.tensor_tensor_scan(d_cs, cc[0:H, CC["reset"]:CC["reset"] + T], d_abs, 0.0, ALU.mult, ALU.add), S["cs_ready"])

            def mixer_d_conv(l):
                for i in range(4):
                    g_done(dve, l, ("xbc", i))
                for k in range(4):
                    for j in range(8):
                        w = par(l, "conv_w", 8 * k + j)
                        if k == 0:
                            ins = V.tensor_scalar(conv[:, j, :], xbc[:, j, 0:T], w, par(l, "conv_b", j), ALU.mult, ALU.add)
                        else:
                            ins = V.scalar_tensor_tensor(conv[:, j, :], xbc[:, j, k:k + T], w, conv[:, j, :], ALU.mult, ALU.add)
                        if k == 3 and j == 7:
                            q.step(ins, S["conv_done"])
                        elif j == 7:
                            q.step(ins)
                        else:
                            q.add(ins, v_seq)

            def mixer_d(l):
                up = const("incl_up")
                filled(dve, l, "cb")
                drain("cb", TT(cbm[:, :, :], mb("cb")[:, :].rearrange("p (i t) -> p i t", i=4), over(up, 4), ALU.mult))
                filled(dve, l, "dtT")
                drain("dtT", V.tensor_copy(area(17256, 32), mb("dtT")[:, 0:32]))
                m_done(dve, l, "dtT")
                for c in range(NCH):
                    filled(dve, l, f"xt{c}")
                    drain(f"xt{c}", TT(xd[:, c, :].rearrange("p (h d) -> p h d", h=H),
                                       mb(f"xt{c}")[:, :].rearrange("p (h d) -> p h d", h=H), along(tok[:, 0, c, :], 64), ALU.mult))
                for i in range(4):
                    row = mb(f"row{i}")[:, :].rearrange("p (j t) -> p j t", j=2)
                    filled(dve, l, f"row{i}")
                    for j in range(2):
                        hd = 2 * i + j
                        q.add(V.tensor_scalar(seg[:, hd, :], row[:, j, 0:P], tok[:, 1, 0, hd:hd + 1], 0.0, ALU.subtract, ALU.min), v_seq)
                        q.add(V.tensor_scalar(seg1[:, hd, :], row[:, j, P:T], tok[:, 1, 1, hd:hd + 1], 0.0, ALU.subtract, ALU.min), v_seq)
                    q.add(V.tensor_copy(cs[:, 2 * i:2 * i + 2, :], row[:, :, P:T]), v_seq)
                    drain(f"row{i}", TT(d_end[:, 2 * i:2 * i + 2].unsqueeze(2), row[:, :, P - 1:P], tok[:, 1, 0, 2 * i:2 * i + 2].unsqueeze(2),
                                        ALU.subtract))
                m_done(dve, l, "row3")
                m_done(dve, l, "row2")
                m_done(dve, l, "row1")
                m_done(dve, l, "row0")
                q.step(V.tensor_scalar(d_end, d_end, 0.0, None, ALU.min), S["d_endraw"])
                q.step(marker(), S["seg_ready"])
                dve.wait_ge(S["d_endexp"], l + 1)
                for c in range(NCH):
                    m_done(dve, l, f"xt{c}")
                q.step(TT(xde.rearrange("p (h d) -> p h d", h=H), xd[:, 0, :].rearrange("p (h d) -> p h d", h=H), along(d_end, 64), ALU.mult),
                       S["xde_ready"])
                q.step(marker(), S["csc_ready"])
                m_done(dve, l, "cb")
                for c in range(NCH):
                    dve.wait_ge(S["seg_exp"], NCH * l + c + 1)
                    for g in range(2):
                        q.step(TT(mT[:, 4 * g:4 * g + 4, :], mT[:, 4 * g:4 * g + 4, :], over(cbm[:, 2 * g + c, :], 4), ALU.mult), S["mt_ready"])
                    if c == 0:
                        dve.wait_ge(S["er_ready"], l + 1)
                        for g in range(2):
                            ins = TT(cs[:, 4 * g:4 * g + 4, :], cs[:, 4 * g:4 * g + 4, :], over(conv[:, 6 + g, P:T], 4), ALU.mult)
                            q.step(ins, S["csc_ready"] if g else None)
                        filled(dve, l, "yd0")
                        q.step(V.tensor_copy(seg[:, :, :], seg1[:, :, :]), S["seg_ready"])
                for c in range(NCH):
                    filled(dve, l, f"yd{c}")
                    for j in range(4):
                        ins = V.scalar_tensor_tensor(yD[:, j, c * P:(c + 1) * P], conv[:, j, c * P:(c + 1) * P], par(l, "skip", j),
                                                     mb(f"yd{c}")[:, j * P:(j + 1) * P], ALU.mult, ALU.add)
                        (q.add(ins, v_seq) if j < 3 else drain(f"yd{c}", ins))
                m_done(dve, l, "yd1")
                m_done(dve, l, "yd0")
                dve.wait_ge(v_seq, q.n[id(v_seq)])
                g_done(dve, l, ("zg", 0))
                g_done(dve, l, ("zg", 1))
                q.step(TT(yD[:, :, :], yD[:, :, :], zg[:, :, :], ALU.mult), S["yd_ready"])
                m_done(dve, l, "dn")
                q.step(V.reciprocal(rstd[:, :], rms[:, :]))
                for j in range(4):
                    ins = V.scalar_tensor_tensor(yD[:, j, :], yD[:, j, :], par(l, "norm_d", j), rstd[:, :], ALU.mult, ALU.mult)
                    (q.add(ins, v_seq) if j == 0 else q.add(ins, S["yd_ready"]))
                dve.wait_ge(S["yd_ready"], q.n[id(S["yd_ready"])])


            def mixer_a(l):
                dve.wait_ge(layer_in, 32 * (l + 1))
                ws = sw[:, SW["w_s"]:SW["w_s"] + 512].rearrange("p (g t) -> p g t", g=4)
                q.step(TT(ws, ws, over(const("incl_up"), 4), ALU.mult), S["wm_ready"])
                for c in range(NCH):
                    g_done(dve, l, ("v", c))
                    q.step(V.bn_stats(small[:, 6 * c:6 * c + 6], vtok[:, c, :]))
                    q.step(V.bn_aggr(small[:, 12 + 20 * c:14 + 20 * c], small[:, 6 * c:6 * c + 6]))
                    q.step(V.tensor_copy(small[:, 16 + c:17 + c], small[:, 13 + 20 * c:14 + 20 * c]), S["v_stats"] if c else None)
                dve.wait_ge(S["v_std"], l + 1)
                q.step(V.reciprocal(small[:, 16:18], small[:, 16:18]))
                for c in range(NCH):
                    v = vtok[:, c, :]
                    q.step(V.tensor_scalar(v, v, small[:, 12 + 20 * c:13 + 20 * c], small[:, 16 + c:17 + c], ALU.subtract, ALU.mult))
                    q.step(TT(v, v, rep[:, 0:512], ALU.mult))
                    q.step(TT(v, v, rep[:, 512:1024], ALU.add), S["vn_ready"])
                for i in range(2):
                    g_done(dve, l, ("u", i))
                for c in range(NCH):
                    filled(dve, l, f"a{c}")
                    y = yA[:, :, c * P:(c + 1) * P]
                    drain(f"a{c}", TT(y, mb(f"a{c}")[:, :].rearrange("p (g t) -> p g t", g=4),
                                      rep[:, 1024:1536].rearrange("p (g t) -> p g t", g=4), ALU.add))
                    m_done(dve, l, f"a{c}")
                    q.step(TT(y, y, u[:, :, c * P:(c + 1) * P], ALU.mult), S["ya_ready"])

            def mixer_c(l):
                def side(first, last=None):
                    products(l, SIDE_AT[first][0], SIDE_AT[last or first][1])

                for i in range(CT // 2):
                    g_done(dve, l, ("c", i))
                dve.wait_ge(S["pooled"], l + 1)
                now = zc[:, :, 1:T + 1]
                q.step(TT(dif[:, :, :], zc[:, :, 0:T], now, ALU.subtract))
                for j in range(CT):
                    ins = V.scalar_tensor_tensor(zc[:, j, 1:T + 1], dif[:, j, :], par(l, "mix", j), zc[:, j, 1:T + 1], ALU.mult, ALU.add)
                    (q.add(ins, v_seq) if j < CT - 1 else q.step(ins, S["zc_mixed"]))
                dve.wait_ge(v_seq, q.n[id(v_seq)])
                r, k, v = zc[:, 0:4, 1:T + 1], zc[:, 4:8, 1:T + 1], zc[:, 8:12, 1:T + 1]
                for j in range(4):
                    ins = V.tensor_scalar(kk[:, j, :], k[:, j, :], par(l, "k_k", j), None, ALU.mult)
                    (q.add(ins, v_seq) if j < 3 else q.step(ins, S["kr_ready"]))
                dve.wait_ge(v_seq, q.n[id(v_seq)])
                side("cw")
                m_done(dve, l, "cw0")
                m_done(dve, l, "cw1")
                q.step(V.tensor_scalar(w_log[:, :, :], w_log[:, :, :], -DECAY, None, ALU.mult))
                flat = lambda ap: ap.rearrange("p j t -> p (j t)")
                q.step(V.tensor_tensor_scan(flat(c_sum), const("reset", 4 * T), flat(w_log), 0.0, ALU.mult, ALU.add))
                by_chunk = lambda ap: flat(ap).rearrange("p (n t) -> p n t", t=P)
                mid = small[:, 20:28]
                q.step(V.tensor_scalar(mid.unsqueeze(2), by_chunk(c_sum)[:, :, P - 1:P], 0.5, None, ALU.mult))
                q.step(TT(by_chunk(c_sum), by_chunk(c_sum), along(mid, P), ALU.subtract))
                q.step(TT(small[:, 28:32], small[:, 20:28:2], small[:, 21:28:2], ALU.add))
                q.step(TT(w_log[:, :, :], c_sum[:, :, :], w_log[:, :, :], ALU.subtract), S["cum_ready"])
                m_done(dve, l, "ca0")
                m_done(dve, l, "ca1")
                for j in range(4):
                    q.add(V.tensor_scalar(k2[:, j, :], aa[:, j, :], -1.0, par(l, "k_a", j), ALU.add, ALU.mult), v_seq)
                dve.wait_ge(v_seq, q.n[id(v_seq)])
                for j in range(4):
                    q.add(V.scalar_tensor_tensor(k2[:, j, :], k2[:, j, :], 1.0, k[:, j, :], ALU.add, ALU.mult), v_seq)
                dve.wait_ge(v_seq, q.n[id(v_seq)])
                for i in range(2):
                    filled(dve, l, f"ss{i}")
                filled(dve, l, "ss1")
                for i in range(2):
                    drain(f"ss{i}", V.tensor_scalar(tmp1[:, 2 * i:2 * i + 2, :], mb(f"ss{i}")[:, :].rearrange("p (j t) -> p j t", j=2),
                                                    FLOOR, None, ALU.max))
                for i in range(2):
                    m_done(dve, l, f"ss{i}")
                for j in range(4):
                    ins = V.scalar_tensor_tensor(tmp2[:, j, :], r[:, j, :], par(l, "r_k", j), k2[:, j, :], ALU.mult, ALU.mult)
                    if j < 3:
                        q.add(ins, v_seq)
                    else:
                        q.step(ins, S["rk_ready"])
                dve.wait_ge(v_seq, q.n[id(v_seq)])
                q.step(marker(), S["ss_ready"])
                side("ss", "bo")
                dve.wait_ge(S["ss_sqrt"], l + 1)
                q.step(V.reciprocal(tmp1[:, :, :], tmp1[:, :, :]))
                q.step(TT(kk[:, :, :], kk[:, :, :], tmp1[:, :, :], ALU.mult))
                dve.wait_ge(S["e_ready"], 4 * (l + 1))
                arj = ar.rearrange("p j c a t -> p (j c) a t")
                q.add(TT(arj[:, :, 0, :], by_chunk(kk), by_chunk(e_ex), ALU.mult), v_seq)
                rc = r.rearrange("p j (c t) -> p j c t", c=NCH)
                q.add(TT(ar[:, :, :, 1, :], rc, e_in.rearrange("p j (c t) -> p j c t", c=NCH), ALU.mult), v_seq)
                q.add(TT(ka[:, :, :], k2[:, :, :], e_neg[:, :, :], ALU.mult), v_seq)
                q.step(V.scalar_tensor_tensor(flat(aa), flat(kk), -1.0, flat(aa), ALU.mult, ALU.mult))
                q.step(TT(nb[:, :, :], aa[:, :, :], e_neg[:, :, :], ALU.mult), S["ab_ready"])
                for i in range(2):
                    filled(dve, l, f"bo{i}")
                    drain(f"bo{i}", TT(bv[:, 2 * i:2 * i + 2, :], mb(f"bo{i}")[:, :].rearrange("p (j t) -> p j t", j=2),
                                       v[:, 2 * i:2 * i + 2, :], ALU.mult))
                side("kt")
                mask = cc[:, CC["strict_up"]:CC["strict_up"] + 2 * P]
                for c in range(NCH):
                    for g in range(2):
                        four = slice(4 * g, 4 * g + 4)
                        filled(dve, l, f"n{g}{c}")
                        if c and g == 0:
                            filled(dve, l, "O0")
                        drain(f"n{g}{c}", TT(xx[:, four, :], mb(f"n{g}{c}")[:, :].rearrange("p (i t) -> p i t", i=4), over(const("low2"), 4), ALU.mult))
                        m_done(dve, l, f"n{g}{c}")
                        q.step(TT(xx[:, four, :], xx[:, four, :], over(ident, 4), ALU.add), S["x_ready"])
                    for hd in range(H):
                        filled(dve, l, f"s{hd}{c}")
                        drain(f"s{hd}{c}", TT(sc[:, hd, :, :].rearrange("p (b a) t -> p b (a t)", b=2), mb(f"s{hd}{c}")[:, :].rearrange("p (b f) -> p b f", b=2), over(mask, 2), ALU.mult))
                        m_done(dve, l, f"s{hd}{c}")
                        q.step(TT(zz[:, hd, :], sc[:, hd, 0, :], const("up2"), ALU.mult), S["sc_ready"])
                    for g in range(2):
                        four = slice(4 * g, 4 * g + 4)
                        q.step(TT(zz[:, four, :], zz[:, four, :], over(ident, 4), ALU.add), S["z_ready"])
                    for lv in range(LEVELS):
                        off = cc[:, CC["off"] + lv * P:CC["off"] + (lv + 1) * P]
                        for g in range(2):
                            four = slice(4 * g, 4 * g + 4)
                            filled(dve, l, f"t{g}{lv}{c}")
                            src = mb(f"t{g}{lv}{c}")[:, :].rearrange("p (i t) -> p i t", i=4)
                            drain(f"t{g}{lv}{c}", TT(tt[:, four, :], src, over(off, 4), ALU.mult))
                            m_done(dve, l, f"t{g}{lv}{c}")
                            q.add(marker(), S["t_ready"])
                        for g in range(2):
                            four = slice(4 * g, 4 * g + 4)
                            if lv < LEVELS - 1:
                                st_ = f"x{g}{lv}{c}"
                                filled(dve, l, st_)
                                drain(st_, TT(xx[:, four, :], mb(st_)[:, :].rearrange("p (i t) -> p i t", i=4), xx[:, four, :], ALU.add))
                                m_done(dve, l, st_)
                                q.add(marker(), S["x_ready"])
                            st_ = f"z{g}{lv}{c}"
                            filled(dve, l, st_)
                            drain(st_, TT(zz[:, four, :], mb(st_)[:, :].rearrange("p (i t) -> p i t", i=4), zz[:, four, :], ALU.add))
                            m_done(dve, l, st_)
                            q.add(marker(), S["z_ready"])
                        side(f"t{lv}{c}", f"z{lv}{c}")
                    side(f"U{c}", f"O{c}")
                    if c == 0:
                        filled(dve, l, "S")
                        drain("S", TT(s0[:, :, :], mb("S")[:, 0:256].rearrange("p (j f) -> p j f", j=4), along(small[:, 28:32], 64), ALU.mult))
                        m_done(dve, l, "S")
                        q.step(marker(), S["s0_ready"])
                m_done(dve, l, "O0")
                m_done(dve, l, "O1")
                for i in range(2):
                    filled(dve, l, f"mu{i}")
                filled(dve, l, "mu1")
                for i in range(2):
                    o2 = oo[:, 2 * i:2 * i + 2, :].rearrange("p j t -> p (j t)")
                    drain(f"mu{i}", V.scalar_tensor_tensor(o2, mb(f"mu{i}")[:, :], -1.0 / 64, o2, ALU.mult, ALU.add))
                    m_done(dve, l, f"mu{i}")
                    q.add(marker(), S["cent"])
                side("mu", "va")
                m_done(dve, l, "va0")
                m_done(dve, l, "va1")
                va = tiles(8720, 4)
                q.step(V.reciprocal(va[:, :, :], va[:, :, :]))
                q.step(TT(oo[:, :, :], oo[:, :, :], va[:, :, :], ALU.mult))
                for j in range(4):
                    q.add(V.tensor_scalar(oo[:, j, :], oo[:, j, :], par(l, "ln_g", j), par(l, "ln_b", j), ALU.mult, ALU.add), v_seq)
                dve.wait_ge(v_seq, q.n[id(v_seq)])
                for i in range(2):
                    m_done(dve, l, f"bo{i}")
                    m_done(dve, l, f"cg{i}")
                q.step(TT(oo[:, :, :], oo[:, :, :], bv[:, :, :], ALU.add))
                q.step(TT(yC[:, :, :], oo[:, :, :], gg[:, :, :], ALU.mult), S["yc_ready"])

            def products(l, lo, hi):
                for n in range(2 * STEPS):
                    step, i = n // 2, n % 2
                    if lo < 12 * step + 12 <= hi:
                        unit = ("pj", step, i)
                        dve.wait_ge(chunks_used, unit_chunk(l, unit) + 1)
                        g_done(dve, l, ("gate", step, i))
                        if n < 4:
                            two = mg[:, 2 * n:2 * n + 2, :]
                            q.add(TT(two, gb(unit)[:, :].rearrange("p (j t) -> p j t", j=2), sg[:, i, :].rearrange("p (j t) -> p j t", j=2),
                                     ALU.mult), g_drained[G_PLAN[unit][0]])
                        else:
                            q.add(TT(sg[:, i, :], gb(unit)[:, :], sg[:, i, :], ALU.mult), g_drained[G_PLAN[unit][0]])
                        g_done(dve, l, unit)
                        q.add(marker(), merged if n < 4 else S["gated"])

            def merge(l):
                products(l, SIDE_AT["va"][1], 12 * STEPS)
                for i in range(N_OUT):
                    unit = ("out", i)
                    dve.wait_ge(chunks_used, unit_chunk(l, unit) + 1)
                    x2 = x[:, 2 * i:2 * i + 2, :]
                    q.add(TT(x2, gb(unit)[:, :].rearrange("p (j t) -> p j t", j=2), x2, ALU.add), g_drained[G_PLAN[unit][0]])
                    g_done(dve, l, unit)
                    q.add(marker(), x_mixed)

            def hiddens(e28, width):
                with dve.Fori(0, FT // RING) as i:
                    for s in range(RING):
                        dve.wait_ge(silu_done, e28 + i * RING + (s + 1))
                        TT(gu[:, i * RING + s, 0:width], gbank[gbanks[s]][:, T:T + width], sil[:, s, 0:width], ALU.mult)\
                            .then_inc(ffn_drained, 1)

            def dense():
                hiddens(0, T)
                dve.wait_ge(chunks_used, FFN0 + N_FFN)
                for i in range(4):
                    x2 = x[:, 2 * i:2 * i + 2, :]
                    TT(x2, mbank[i][:, :].rearrange("p (j t) -> p j t", j=2), x2, ALU.add).then_inc(ffn_drained, 1)
                dve.wait_ge(ffn_drained, FT + 4)

            def overflowed(e):
                hiddens(e * FT + (FT + E * FT), T)
                dve.wait_ge(chunks_used, (e + E) * N_FFN + (MOE0 + N_FFN))
                m2 = moe_tmp.rearrange("p (j t) -> p j t", j=2)
                for i in range(4):
                    x2 = x[:, 2 * i:2 * i + 2, :]
                    dve.wait_ge(S["b_done"], e * 4 + (i + 1))
                    TT(m2, mbank[i][:, :].rearrange("p (j t) -> p j t", j=2), over(crow[:, e, :], 2), ALU.mult).then_inc(ffn_drained, 1)
                    dve.wait_ge(ffn_drained, e * (FT + 4) + (FT + 4 + E * FT + FT + i + 1))
                    TT(x2, m2, x2, ALU.add).then_inc(S["b_done"], 1)

            def put_tokens(e):
                for c in range(NCH):
                    ins = V.tensor_scalar(put[:, c, :], const("slots", CAP), place_tok[:, c, e:e + 1] if isinstance(e, int)
                                          else place_tok[:, c, bass.ds(e, 1)], None, ALU.is_equal)
                    ins.then_inc(S["put_ready"] if c else S["em_ready"], 1)

            place_tok = small[:, 100:118].rearrange("p (c e) -> p c e", c=NCH)

            def experts():
                put_tokens(0)
                with dve.Fori(0, E) as e:
                    dve.wait_ge(S["hg_ready"], e * 2 + 2)
                    put_tokens(e + 1)
                    V.scalar_tensor_tensor(back, prow[0:CAP, e, :], cc[0:CAP, CC["slot"]:CC["slot"] + 1], crow[0:CAP, e, :],
                                           ALU.is_equal, ALU.mult).then_inc(S["back_ready"], 1)
                    hiddens(e * FT + FT, CAP)
                    for i in range(4):
                        dve.wait_ge(S["back_filled"], e * 4 + (i + 1))
                        x2 = x[:, 2 * i:2 * i + 2, :]
                        TT(x2, mbank[i % 2][:, :].rearrange("p (j t) -> p j t", j=2), x2, ALU.add).then_inc(S["back_drained"], 1)

            def router():
                dve.wait_ge(m_filled[1], L * M_TOTAL[1] + 1)
                r3 = lambda i: rt[:, 16 * i:16 * i + 16].rearrange("p (c e) -> p c e", c=NCH)
                comb, lg, eq, cum, first1, first2 = (r3(i) for i in range(6))
                v1, v2, dd = small[:, 32:34], small[:, 34:36], small[:, 36:38]
                p1, p2_ = small[:, 40:42], small[:, 42:44]
                q.step(V.tensor_copy(rt[:, 16:32], mbank[1][:, 0:16]))

                def pick(top, chosen):
                    q.step(V.tensor_reduce(top, lg, AX_X, ALU.max))
                    for c in range(NCH):
                        q.step(V.tensor_scalar(eq[:, c, :], lg[:, c, :], top[:, c:c + 1], None, ALU.is_equal))
                        q.step(V.tensor_tensor_scan(cum[:, c, :], const("ones", E), eq[:, c, :], 0.0, ALU.mult, ALU.add))
                    q.step(V.scalar_tensor_tensor(chosen, cum, 1.0, eq, ALU.is_equal, ALU.mult))

                pick(v1, first1)
                q.step(V.scalar_tensor_tensor(lg, first1, -3.0e38, lg, ALU.mult, ALU.add))
                pick(v2, first2)
                q.step(TT(dd, v1, v2, ALU.subtract), S["logits_top"])
                dve.wait_ge(S["probs"], 1)
                for c in range(NCH):
                    q.step(V.tensor_scalar(comb[:, c, :], first1[:, c, :], p1[:, c:c + 1], None, ALU.mult))
                    q.step(V.scalar_tensor_tensor(comb[:, c, :], first2[:, c, :], p2_[:, c:c + 1], comb[:, c, :], ALU.mult, ALU.add),
                           S["comb_ready"] if c else None)
                dve.wait_ge(m_filled[2], L * M_TOTAL[2] + 1)
                comb_t, chosen, count, place = (routeT[:, i, :] for i in range(4))
                q.step(V.tensor_copy(comb_t, mbank[2][0:E, 0:T]))
                q.step(V.tensor_scalar(chosen, comb_t, 0.0, None, ALU.is_gt))
                q.step(V.tensor_tensor_scan(count, cc[0:E, CC["ones"]:CC["ones"] + T], chosen, 0.0, ALU.mult, ALU.add))
                q.step(TT(count, count, chosen, ALU.mult))
                q.step(V.tensor_scalar(place, count, -1.0, None, ALU.add), S["places"])
                q.step(V.memset(small[:, 100:118], -1.0))
                dve.wait_ge(S["tok_done"], 1)
                q.step(V.tensor_copy(place_tok[:, :, 0:E], mbank[0][:, 0:2 * E].rearrange("p (c e) -> p c e", c=NCH)))
                dve.wait_ge(S["combs_done"], 1)
                for i in range(4):
                    ins = V.tensor_copy(crow[:, 2 * i:2 * i + 2, :], gbank[i][:, :].rearrange("p (j t) -> p j t", j=2))
                    (q.step(ins) if i < 3 else q.step(ins, S["crow_ready"]))
                dve.wait_ge(S["rows_done"], 1)
                for i in range(4):
                    q.step(V.tensor_copy(prow[:, 2 * i:2 * i + 2, :], gbank[i][:, :].rearrange("p (j t) -> p j t", j=2)))
                q.step(V.tensor_reduce(small[:, 80:81], prow.rearrange("p e t -> p (e t)"), AX_X, ALU.max))
                q.step(V.tensor_scalar(small[:, 80:81], small[:, 80:81], CAP - 0.5, None, ALU.is_gt))
                q.step(V.tensor_copy(flag[:, 0:1], small[:, 80:81]), S["flag_ready"])

            for l in range(L):
                norm(lambda: m_done(dve, l, "norm1"), lambda k: par(l, "norm_mix", k), h_ready)
                dve.wait_ge(h_ready, 2 * DT * l + DT)
                mixer_d_dt(l)
                mixer_d_conv(l)
                mixer_d(l)
                mixer_a(l)
                mixer_c(l)
                merge(l)
                norm(lambda: m_done(dve, l, "norm2"), lambda k: par(l, "norm_ffn", k), h_ready)
                if l == 0:
                    dense()
                    for _ in range(4):
                        q.step(marker(), S["ffn_x"])
                else:
                    router()
                    overflow = dve.value_load(flag[0:1, 0:1], min_val=0, max_val=1)
                    experts()
                    dve.wait_ge(S["back_drained"], 4 * E)
                    q.step(marker(), S["b_done"])
                    with dve.If(overflow > 0):
                        V.scalar_tensor_tensor(crow.rearrange("p e t -> p (e t)"), prow.rearrange("p e t -> p (e t)"), CAP - 0.5,
                                               crow.rearrange("p e t -> p (e t)"), ALU.is_gt, ALU.mult).then_inc(S["back_ready"], 1)
                        dve.wait_ge(S["back_ready"], E + 1)
                        with dve.Fori(0, E) as e:
                            overflowed(e)
                        dve.wait_ge(S["b_done"], 4 * E + 1)
                    for _ in range(4):
                        q.step(marker(), S["ffn_x"])
            dve.wait_ge(m_drained[0], L * M_TOTAL[0] + 1)
            q.step(V.reciprocal(rstd[:, :], rms[:, :]))
            for k in range(DT):
                q.add(V.scalar_tensor_tensor(h[:, k, :], x[:, k, :], par(0, "norm_final", k), rstd[:, :], ALU.mult, ALU.mult), S["out_ready"])


def kernel(x, norm_mix_g, w_in, a_ln_g, a_ln_b, a_w_s, a_b_s, b_w_pool, b_scale, c_mix, c_w0, c_w2, c_a0, c_a2, c_g2,
           c_k_k, c_k_a, c_r_k, c_ln_g, c_ln_b, d_conv_w, d_conv_b, d_dt_bias, d_a_log, d_skip, d_norm_g,
           w_branch, w_out, norm_ffn_g, ffn_w_gate, ffn_w_up, ffn_w_down, moe_router, moe_w_gate, moe_w_up, moe_w_down,
           norm_final_g):
    import numpy as np
    import concourse.bacc as bacc
    from concourse.bass_utils import run_bass_kernel_spmd

    f = lambda a: np.asarray(a)

    def col_tiles(w):
        k, n = w.shape
        return w.reshape(k // P, P, n // P, P).transpose(2, 1, 0, 3).reshape(n // P, P, k)

    def pairs(t):
        return t.reshape(-1, 2, P, D).transpose(0, 2, 1, 3).reshape(-1, P, CW)

    def swiglu_chunks(wg, wu, wd):
        g, up = col_tiles(wg), col_tiles(wu)
        hidden = np.stack([g, up], 1).transpose(0, 2, 1, 3).reshape(FT, P, CW)
        return [hidden, wd.reshape(N_DOWN, 2, P, D).transpose(0, 2, 1, 3).reshape(N_DOWN, P, CW)]

    def mixer_chunks(l):
        w = f(w_in)[l]
        v = w[:, 512:1024].reshape(2, 4, P, 512).transpose(0, 2, 1, 3).reshape(2, P, CW)
        gates = pairs(col_tiles(w[:, 4872:8968])).reshape(4, 2, 2, P, CW)[MERGE_ORDER].reshape(STEPS, 2, P, CW)
        branch = f(w_branch)[l].reshape(4, 4, P, 2, 4, P).transpose(0, 3, 2, 4, 1, 5)[MERGE_ORDER].reshape(STEPS, 1, P, CW)
        return [pairs(col_tiles(w[:, 3328:3840])), pairs(col_tiles(w[:, 3840:4864])), v, pairs(col_tiles(w[:, 0:512])),
                pairs(col_tiles(w[:, 1024:1536])), pairs(col_tiles(w[:, 1536:3328])),
                np.concatenate([gates, branch], 1).reshape(N_MERGE, P, CW), pairs(col_tiles(f(w_out)[l]))]

    parts = mixer_chunks(0) + swiglu_chunks(f(ffn_w_gate)[0], f(ffn_w_up)[0], f(ffn_w_down)[0]) + mixer_chunks(1)
    for e in range(E):
        parts += swiglu_chunks(f(moe_w_gate)[0, e], f(moe_w_up)[0, e], f(moe_w_down)[0, e])
    stream = np.concatenate(parts, 0)
    assert stream.shape == (N_CHUNKS, P, CW)

    def cols(a):
        return f(a).reshape(-1, P).T

    pp = np.zeros((P, L, NPP), np.float32)
    for l in range(L):
        put = {"norm_mix": cols(f(norm_mix_g)[l]), "norm_ffn": cols(f(norm_ffn_g)[l]), "mix": cols(f(c_mix)[l]), "w0": cols(f(c_w0)[l]),
               "a0": cols(f(c_a0)[l]), "k_k": cols(f(c_k_k)[l]), "k_a": cols(f(c_k_a)[l]), "r_k": cols(f(c_r_k)[l]),
               "ln_g": cols(f(c_ln_g)[l]), "ln_b": cols(f(c_ln_b)[l]), "conv_w": cols(f(d_conv_w)[l]), "conv_b": cols(f(d_conv_b)[l]),
               "norm_d": cols(f(d_norm_g)[l]), "skip": cols(np.repeat(f(d_skip)[l], 64)), "b_scale": cols(f(b_scale)[l]),
               "norm_final": cols(norm_final_g)}
        for name, a in put.items():
            pp[:, l, PP[name]:PP[name] + a.shape[1]] = a
        pp[0:H, l, PP["dt_bias"]] = f(d_dt_bias)[l]
        pp[0:H, l, PP["a_log"]] = f(d_a_log)[l]

    sw = np.zeros((L, P, NSW), np.float32)
    rep = np.zeros((L, P, NREP), np.float32)
    for l in range(L):
        put = {"w_s": f(a_w_s)[l].transpose(2, 0, 1).reshape(P, 512), "pool": f(b_w_pool)[l].transpose(1, 0, 2).reshape(P, 512),
               "w2a2": np.concatenate([f(c_w2)[l], f(c_a2)[l]], 0), "g2": f(c_g2)[l],
               "dt": f(w_in)[l][:, 4864:4872].reshape(DT, P, H).transpose(1, 0, 2).reshape(P, DT * H)}
        if l == 1:
            put["router"] = f(moe_router)[0].reshape(DT, P, E).transpose(1, 0, 2).reshape(P, DT * E)
        for name, a in put.items():
            sw[l, :, SW[name]:SW[name] + a.shape[1]] = a
        rep[l, :, 0:512] = f(a_ln_g)[l]
        rep[l, :, 512:1024] = f(a_ln_b)[l]
        rep[l, :, 1024:1536] = f(a_b_s)[l].reshape(512)

    i, j = np.arange(P)[:, None], np.arange(P)[None, :]
    t = np.arange(T)
    off = [((i // (2 * m) == j // (2 * m)) & (i // m != j // m)) for m in (2, 4, 8, 16, 32, 64)]
    put = {"ident": i == j, "ones": np.ones((P, T)), "heads": i // 64 == j // 64, "strict_up": i < j, "incl_up": i <= j,
           "low2": (i > j) & (i // 2 == j // 2), "up2": (i < j) & (i // 2 == j // 2), "off": np.concatenate(off, 1),
           "count": np.tile(np.concatenate([1.0 / np.minimum(t + 1, w) for w in (2, 4, 8, 16)]), (P, 1)),
           "reset": np.tile((np.arange(4 * T) % P != 0), (P, 1)),
           "sel": np.concatenate([np.repeat(i == hd, P, 1) for hd in range(H)], 1),
           "eps": np.full((P, 1), EPS), "gn_eps": np.full((P, 1), GN_EPS),
           "slots": np.tile(np.arange(CAP), (P, 1)), "slot": np.arange(P)[:, None]}
    cc = np.zeros((P, NCC), np.float32)
    for name, a in put.items():
        cc[:, CC[name]:CC[name] + a.shape[1]] = a

    xt = np.ascontiguousarray(f(x)[0].T.reshape(DT, P, T).transpose(1, 0, 2))
    nc = bacc.Bacc("TRN2", target_bir_lowering=False, num_devices=1,
                   dynamic_dma_scratch_size=3 * 1024)
    arrays, args = {}, []
    for name, a in (("x_in", xt), ("stream", stream), ("pp_in", pp), ("cc_in", cc), ("sw_in", sw), ("rep_in", rep)):
        arrays[name] = a
        args.append(nc.dram_tensor(name, a.shape, F32, kind="ExternalInput").ap())
    args.append(nc.dram_tensor("out", (P, DT, T), F32, kind="ExternalOutput").ap())
    trunk(nc, *args)
    r = run_bass_kernel_spmd(nc, [arrays], core_ids=[0])
    got = np.asarray(r.results[0]["out"])
    return np.ascontiguousarray(got.transpose(1, 0, 2).reshape(D, T).T)[None]
```

```python
from contextlib import ExitStack

import concourse.bass as bass
from concourse import mybir

F32 = mybir.dt.float32
F32R = mybir.dt.float32r
ALU = mybir.AluOpType
ACT = mybir.ActivationFunctionType
AX_X = mybir.AxisListType.X

P = 128
T = 256
D = 1024
DT = D // P
L = 2
NCH = T // P
FF = 3584
FT = FF // P
E = 8
H = 8
HEADS = [0, 2, 4, 6, 1, 3, 5, 7]
CT = 14
CAP = 96
BLK = 16
CW = BLK * P
RING = 7
EPS = 1e-6
GN_EPS = 64e-5
DECAY = 0.6065306597126334
FLOOR = 1e-24

Z_UNITS = [("zg", 0), ("zg", 1), ("xbc", 0), ("xbc", 1), ("xbc", 2), ("xbc", 3), ("v", 0), ("v", 1), ("u", 0), ("u", 1),
           ("b", 0), ("b", 1)] + [("c", i) for i in range(CT // 2)]
NZ = len(Z_UNITS)
NS = 12
MERGE_ORDER = [0, 1, 3, 2]
STEPS = 8
N_MERGE = 3 * STEPS
MERGE_CHUNKS = [(_s, _u) for _s in range(STEPS - 2) for _u in range(3)] + [(6, 0), (6, 1), (7, 0), (7, 1), (6, 2), (7, 2)]
SIDE = [("cw", 12), ("ss", 4), ("bo", 12), ("kt", 8)]
for _c in range(2):
    for _v in range(6):
        SIDE += [(f"t{_v}{_c}", 1), (f"z{_v}{_c}", 1 + (_v > 1))]
    SIDE += [(f"U{_c}", 1), (f"O{_c}", 1)]
SIDE += [("mu", 4), ("va", 4)]
N_OUT = DT // 2
N_MIX = NZ + N_MERGE + N_OUT
N_GU = FT
N_DOWN = DT * FT // BLK
GROUPS = FF // 512
N_FFN = N_GU + N_DOWN
FFN0 = N_MIX
MIX1 = N_MIX + N_FFN
MOE0 = MIX1 + N_MIX
N_CHUNKS = MOE0 + E * N_FFN

PP_LIST = [("norm_mix", 8), ("norm_ffn", 8), ("mix", 14), ("w0", 4), ("a0", 4), ("k_k", 4), ("k_a", 4), ("r_k", 4),
           ("ln_g", 4), ("ln_b", 4), ("conv_w", 32), ("conv_b", 8), ("norm_d", 4), ("skip", 4), ("b_scale", 4),
           ("norm_final", 8), ("dt_bias", 1), ("a_log", 1)]
PP, _n = {}, 0
for _name, _k in PP_LIST:
    PP[_name] = _n
    _n += _k
NPP = _n
LEVELS = 6
CC_LIST = [("ones", T), ("eps", 1), ("gn_eps", 1), ("ident", P), ("heads", P), ("strict_up", P), ("incl_up", P), ("low2", P), ("up2", P),
           ("off", LEVELS * P), ("count", 4 * T), ("reset", 4 * T), ("sel", H * P), ("slots", CAP), ("slot", 1)]
CC, _n = {}, 0
for _name, _k in CC_LIST:
    CC[_name] = _n
    _n += _k
NCC = _n
SW_LIST = [("w_s", 512), ("pool", 512), ("w2a2", 512), ("g2", 512), ("dt", 64), ("router", 64)]
SW, _n = {}, 0
for _name, _k in SW_LIST:
    SW[_name] = _n
    _n += _k
NSW = _n
NREP = 3 * 512

M_USES = ([("norm1", 0), ("dt", 1), ("cb", 2), ("xt0", 3), ("xt1", 0), ("bt", 1), ("dtT", 2)]
          + [(f"row{i}", (3 + i) % 4) for i in range(4)]
          + [("st", 3), ("yd0", 0), ("yd1", 1), ("dn", 2), ("a0", 3), ("a1", 0), ("b0", 1), ("b1", 2)]
          + [("cw0", 3), ("cw1", 0), ("ca0", 1), ("ca1", 2), ("cg0", 3), ("cg1", 0), ("ss0", 1), ("ss1", 2),
             ("bo0", 3), ("bo1", 0), ("vt0", 1), ("vt1", 2), ("kt", 3), ("nt", 0)])
for _c in range(NCH):
    M_USES += [(f"n0{_c}", 1), (f"n1{_c}", 2)] + [(f"s{_h}{_c}", (3 + _h) % 4) for _h in range(H)]
    for _v in range(LEVELS):
        M_USES += [(f"t0{_v}{_c}", 0), (f"t1{_v}{_c}", 1)]
        if _v < LEVELS - 1:
            M_USES += [(f"x0{_v}{_c}", 2)]
        M_USES += [(f"z0{_v}{_c}", 3)]
        if _v < LEVELS - 1:
            M_USES += [(f"x1{_v}{_c}", 0)]
        M_USES += [(f"z1{_v}{_c}", 1)]
    M_USES += [(f"W0{_c}", 2), (f"W1{_c}", 1), (f"U{_c}", 3), (f"O{_c}", 0)]
    if _c == 0:
        M_USES += [("S", 1)]
M_USES += [("mu0", 1), ("mu1", 2), ("va0", 3), ("va1", 0)]
M_USES += [("norm2", 0)]
G_USES = [((u, i), n % 4) for n, (u, i) in enumerate(Z_UNITS)]
for _s in range(STEPS - 2):
    G_USES += [(("gate", _s, 0), 0), (("gate", _s, 1), 1), (("pj", _s, 0), 2), (("pj", _s, 1), 3)]
G_USES += [(("gate", 6, 0), 0), (("gate", 6, 1), 1), (("gate", 7, 0), 2), (("gate", 7, 1), 3),
           (("pj", 6, 0), 0), (("pj", 6, 1), 1), (("pj", 7, 0), 2), (("pj", 7, 1), 3)]
G_USES += [(("out", _i), _i) for _i in range(N_OUT)]


def bank_plan(uses):
    total, plan = [0] * 4, {}
    for stage, bank in uses:
        total[bank] += 1
        assert stage not in plan
        plan[stage] = (bank, total[bank])
    return plan, total


M_PLAN, M_TOTAL = bank_plan(M_USES)
SIDE_AT, _n = {}, 0
for _name, _k in SIDE:
    SIDE_AT[_name] = (_n, _n + _k)
    _n += _k
SIDE_END = _n
G_PLAN, G_TOTAL = bank_plan(G_USES)


def trunk(nc, x_in, stream, pp_in, cc_in, sw_in, rep_in, out):
    with ExitStack() as ctx:
        def sb(name, shape):
            return ctx.enter_context(nc.sbuf_tensor(name, shape, F32))

        def sem(name):
            return ctx.enter_context(nc.semaphore(name))

        x = sb("x", [P, DT, T])
        h = sb("h", [P, DT, T])
        ring_at = -(-nc.sbuf_base // 32) * 32
        ring = sb("ring", [P, RING, CW])
        cc = sb("cc", [P, NCC])
        pp = sb("pp", [P, L, NPP])
        sw = sb("sw", [P, NSW])
        rep = sb("rep", [P, NREP])
        rstd = sb("rstd", [P, T])
        rms = sb("rms", [P, T])
        small = sb("small", [P, 256])
        arena_at = -(-nc.sbuf_base // 32) * 32
        arena = sb("arena", [P, 28264])

        def part(name, at, shape):
            return nc.alloc_sbuf_tensor_at(name, [P] + shape, F32R, offset=arena_at + 4 * at)

        ring_low = nc.alloc_sbuf_tensor_at("ring_low", [P, RING, CW], F32R, offset=ring_at)

        gbank = [ctx.enter_context(nc.psum_tensor(f"g{i}", [P, 512], F32)) for i in range(4)]
        mbank = [ctx.enter_context(nc.psum_tensor(f"m{i}", [P, 512], F32)) for i in range(4)]

        def area(at, n):
            return arena[:, at:at + n]

        def tiles(at, n, w=T):
            return area(at, n * w).rearrange("p (n t) -> p n t", n=n)

        def const(name, n=P):
            return cc[:, CC[name]:CC[name] + n]

        def par(l, name, j=0, rows=P):
            return pp[0:rows, l, PP[name] + j:PP[name] + j + 1]

        def over(ap, n):
            return ap.unsqueeze(1).to_broadcast([ap.shape[0], n, ap.shape[1]])

        def along(ap, w):
            return ap.unsqueeze(2).to_broadcast([ap.shape[0], ap.shape[1], w])

        ident, ones, heads = const("ident"), const("ones"), const("heads")

        yA, yB, yC, yD = (tiles(i * 1024, 4) for i in range(4))
        zc = tiles(4096, CT, T + 1)
        zg = tiles(7696, 4)
        xbc = tiles(8720, 8, T + 3)
        vtok = tiles(10792, 2, 512)
        u = tiles(11816, 4)
        zb = tiles(12840, 4, T + 16)
        conv = tiles(13928, 8)
        dtw = area(15976, 1280)
        d_raw, d_abs, d_ln, d_dt, d_cs = (dtw[0:H, i * T:(i + 1) * T] for i in range(5))
        tok = area(17256, 32).rearrange("p (a c h) -> p a c h", a=2, c=NCH)
        d_end = area(17288, H)
        ahead = small[:, 120:122]
        cbm = tiles(17296, 4, P)
        xd = tiles(17808, 2, 512)
        btok = tiles(18832, 2, P)
        xde = area(19088, 512)
        mT = tiles(19600, H, P)
        seg = tiles(20624, H, P)
        cs = tiles(21648, H, P)
        st = tiles(22672, 2, T)
        seg1 = tiles(2048, H, P)
        p2 = tiles(23184, 4, T + 16)
        p4 = tiles(24000, 4, T + 16)
        ar = area(13928, 2048).rearrange("p (j c a t) -> p j c a t", j=4, c=NCH, a=2)
        nb = tiles(15976, 4)
        ka = tiles(17000, 4)
        cv = tiles(18024, 2, 512)
        kbt = tiles(19048, 2, 512)
        sc = area(20072, 4096).rearrange("p (h a t) -> p h a t", h=H, a=4)
        s0 = rms[:, :].rearrange("p (j f) -> p j f", j=4)
        wb = area(24168, 512)
        ub = area(24680, 512)
        xx = tiles(7696, H, P)
        zz = tiles(8720, H, P)
        tt = tiles(9744, H, P)
        bv = tiles(10792, 4)
        gg = tiles(11816, 4)
        oo = tiles(12840, 4)
        dif = tiles(20072, CT)
        w_log, c_sum, aa, kk = (tiles(20072 + i * 1024, 4) for i in range(4))
        e_in, e_neg, e_ex = (tiles(7696 + i * 1024, 4) for i in range(3))
        k2 = tiles(24168, 4)
        tmp1 = tiles(18024, 4)
        tmp2 = tiles(19048, 4)
        sg = area(25192, 1024).rearrange("p (b f) -> p b f", b=2)
        mg = tiles(26216, DT)

        def sg_of(step, i):
            return area(4096 + 512 * i, 512) if step == STEPS - 1 else sg[:, i, :]

        sq = tiles(13928, DT)
        gbanks = [0, 1, 2, 3, 0, 1, 2]
        gu = tiles(4096, FT)
        sil = tiles(11264, RING)
        sil2 = area(11264, 1024).rearrange("p (i f) -> p i f", i=2)
        h_high = part("h_high", 0, [DT, T])
        h_low = part("h_low", 2048, [DT, T])
        gu_high = part("gu_high", 4096, [FT, T])
        gu_low = part("gu_low", 15976, [FT, T])
        w_high = part("w_high", 23144, [2, CW])
        gu_tmp = area(13056, T)
        crow = tiles(18024, E)
        prow = tiles(20072, E)
        moe_tmp = area(16000, 512)
        routeT = area(16512, 1024)[0:E].rearrange("p (i t) -> p i t", i=4)
        rt = area(17536, 256)
        htok = area(22120, 2048).rearrange("p (c f) -> p c f", c=NCH)
        hg_high = part("hg_high", 24168, [DT, CAP])
        hg_low = part("hg_low", 27000, [DT, CAP])
        we_high = [part(f"we_high{i}", at, [CW]) for i, at in enumerate((0, CW, 24936))]
        eu_high = part("eu_high", 4096, [FT, CAP])
        eu_low = part("eu_low", 6784, [FT, CAP])
        sil_tok = area(9472, 1024)[0:CAP].rearrange("p (b f) -> p b f", b=2)
        hid_tok = area(10496, 1024)[0:CAP].rearrange("p (b f) -> p b f", b=2)
        put = area(13952, 2 * CAP).rearrange("p (c s) -> p c s", c=NCH)
        back = area(14144, T)[0:CAP]
        ytok = area(14400, D)[0:CAP]

        landed = [sem(f"landed{i}") for i in range(RING)]
        chunks_used = sem("chunks_used")
        g_drained = [sem(f"g_drained{i}") for i in range(4)]
        m_filled = [sem(f"m_filled{i}") for i in range(4)]
        m_drained = [sem(f"m_drained{i}") for i in range(4)]
        consts_in = sem("consts_in")
        all_consts_in = sem("all_consts_in")
        x_loaded = sem("x_loaded")
        layer_in = sem("layer_in")
        padded = sem("padded")
        merged = sem("merged")
        sq_ready = sem("sq_ready")
        h_ready = sem("h_ready")
        x_mixed = sem("x_mixed")
        ffn_drained = sem("ffn_drained")
        silu_done = sem("silu_done")
        high_ready = sem("high_ready")
        low_ready = sem("low_ready")
        v_seq = sem("v_seq")
        a_seq = sem("a_seq")
        p_seq = sem("p_seq")
        out_stored = sem("out_stored")
        S = {n: sem(n) for n in (
            "conv_done conv_silu dt_raw dt_exp cs_ready seg_ready seg_exp "
            "mt_ready d_endraw d_endexp xde_ready er_ready csc_ready yd_ready ydsq "
            "v_stats v_std vn_ready wm_ready ya_ready pooled zc_mixed lora_ready "
            "cum_ready e_ready kr_ready krsq ss_ready ss_sqrt rk_ready ab_ready sc_ready t_ready z_ready x_ready "
            "s0_ready cent osq yc_ready gated b_done logits_top probs comb_ready crow_ready "
            "out_ready ffn_x combs_done places rows_done tok_done htok_done flag_ready put_ready back_ready "
            "hg_filled hg_high_ready hg_ready silu_tok hid_ready hid_turned eu_high_ready eu_ready y_ready zeroed back_filled back_drained h_split h_split_high gu_part").split()}
        flag = ctx.enter_context(nc.sbuf_tensor("flag", [P, 2], mybir.dt.int32))

        def filled(eng, l, stage):
            bank, n = M_PLAN[stage]
            eng.wait_ge(m_filled[bank], l * M_TOTAL[bank] + n)

        def m_free(eng, l, stage):
            bank, n = M_PLAN[stage]
            if l * M_TOTAL[bank] + n > 1:
                eng.wait_ge(m_drained[bank], l * M_TOTAL[bank] + n - 1)

        def m_done(eng, l, stage):
            bank, n = M_PLAN[stage]
            eng.wait_ge(m_drained[bank], l * M_TOTAL[bank] + n)

        def g_free(eng, l, unit):
            bank, n = G_PLAN[unit]
            if l * G_TOTAL[bank] + n > 1:
                eng.wait_ge(g_drained[bank], l * G_TOTAL[bank] + n - 1)

        def g_done(eng, l, unit):
            bank, n = G_PLAN[unit]
            eng.wait_ge(g_drained[bank], l * G_TOTAL[bank] + n)

        def mb(stage):
            return mbank[M_PLAN[stage][0]]

        def gb(unit):
            return gbank[G_PLAN[unit][0]]

        def chunk0(l):
            return l * MIX1

        def unit_chunk(l, unit):
            c = chunk0(l)
            if unit == ("v", 0):
                unit = ("v", 1)
            if unit in Z_UNITS:
                return c + Z_UNITS.index(unit)
            if unit[0] == "gate":
                return c + NZ + MERGE_CHUNKS.index((unit[1], unit[2]))
            if unit[0] == "pj":
                return c + NZ + MERGE_CHUNKS.index((unit[1], 2))
            return c + NZ + N_MERGE + unit[1]

        class Count:
            def __init__(self, eng, own):
                self.eng, self.own, self.n = eng, own, {}

            def add(self, ins, s):
                ins.then_inc(s, 1)
                self.n[id(s)] = self.n.get(id(s), 0) + 1

            def step(self, ins, s=None):
                s = s or self.own
                self.add(ins, s)
                self.eng.wait_ge(s, self.n[id(s)])

        block = ctx.enter_context(nc.Block())

        @block.sync
        def _(sp):
            first = CC["ident"]
            sp.dma_start(x[:, :, :], x_in).then_inc(x_loaded, 16)
            sp.dma_start(cc[:, 0:first], cc_in[:, 0:first]).then_inc(consts_in, 16)
            sp.dma_start(pp[:, :, :], pp_in).then_inc(consts_in, 16)
            for s in range(RING):
                sp.dma_start(ring[:, s, :], stream[s]).then_inc(landed[s], 16)
                if s == 1:
                    sp.dma_start(sw[:, :], sw_in[0]).then_inc(layer_in, 16)
                    sp.dma_start(cc[:, first:NCC], cc_in[:, first:NCC]).then_inc(all_consts_in, 16)
                    sp.dma_start(rep[:, :], rep_in[0]).then_inc(layer_in, 16)
            turns = N_CHUNKS // RING
            with sp.Fori(1, turns) as i:
                for s in range(RING):
                    sp.wait_ge(chunks_used, i * RING + (s - RING + 1))
                    sp.dma_start(ring[:, s, :], stream[i * RING + s]).then_inc(landed[s], 16)
            for n in range(turns * RING, N_CHUNKS):
                sp.wait_ge(chunks_used, n - RING + 1)
                sp.dma_start(ring[:, n % RING, :], stream[n]).then_inc(landed[n % RING], 16)
            sp.wait_ge(S["flag_ready"], 1)
            overflow = sp.value_load(flag[0:1, 0:1], min_val=0, max_val=1)
            with sp.If(overflow > 0):
                with sp.Fori(0, E * N_FFN // RING) as i:
                    for s in range(RING):
                        sp.wait_ge(chunks_used, i * RING + (N_CHUNKS + s - RING + 1))
                        slot = (N_CHUNKS + s) % RING
                        sp.dma_start(ring[:, slot, :], stream[i * RING + (MOE0 + s)]).then_inc(landed[slot], 16)

        @block.tensor
        def _(pe):
            pe.wait_ge(consts_in, 32)

            def mm(o, a, b, start=True, stop=True):
                return pe.matmul(o, a, b, start=start, stop=stop, skip_group_check=True)

            def three(o, high, low, x_high, x_low, start, stop):
                mm(o, high, x_high, start, False)
                mm(o, high, x_low, False, False)
                return mm(o, low, x_high, False, stop)

            def chunk(n):
                pe.wait_ge(landed[n % RING], 16 * (n // RING + 1))
                return ring[:, n % RING, :].rearrange("p (b m) -> p b m", b=BLK)

            def fill(l, stage, last):
                last.then_inc(m_filled[M_PLAN[stage][0]], 1)

            def feature_sum(l, stage, mat, src, n, scale=1):
                m_free(pe, l, stage)
                for j in range(n):
                    last = mm(mb(stage)[:, 0:T], mat, src[:, j, :], j == 0, j == n - 1)
                fill(l, stage, last)

            def two_banks(l, name, lhs, rhs):
                for i in range(2):
                    m_free(pe, l, f"{name}{i}")
                    for j in (2 * i, 2 * i + 1):
                        last = mm(mb(f"{name}{i}")[:, (j % 2) * T:(j % 2 + 1) * T], lhs(j), rhs(j))
                    fill(l, f"{name}{i}", last)

            def turn(l, stage, parts):
                m_free(pe, l, stage)
                for i, src in enumerate(parts):
                    last = pe.transpose(mb(stage)[:, i * P:(i + 1) * P], src, ident)
                fill(l, stage, last)

            def project(l, lo, hi):
                for n in range(lo, hi):
                    name, i = Z_UNITS[n]
                    slot = (chunk0(l) + n) % RING
                    if n < NS:
                        pe.wait_ge(low_ready, l * (NS + N_FFN) + n + 1)
                        low = ring_low[:, slot, :].rearrange("p (b m) -> p b m", b=BLK)
                        high = w_high[:, n % 2, :].rearrange("p (b m) -> p b m", b=BLK)
                    else:
                        w = chunk(chunk0(l) + n)
                    if name == "v":
                        if i == 0:
                            g_free(pe, l, ("v", 0))
                            g_free(pe, l, ("v", 1))
                        wl = ring_low[:, slot, :].rearrange("p (k f) -> p k f", k=4)
                        wh = w_high[:, n % 2, :].rearrange("p (k f) -> p k f", k=4)
                        for c in range(NCH):
                            for k in range(4):
                                tc = slice(c * P, (c + 1) * P)
                                last = three(gb(("v", c))[:, :], h_high[:, 4 * i + k, tc], h_low[:, 4 * i + k, tc],
                                             wh[:, k, :], wl[:, k, :], i == 0 and k == 0, i == 1 and k == 3)
                    else:
                        g_free(pe, l, (name, i))
                        for j in range(2):
                            for k in range(DT):
                                if n == 0 and j == 0 and k % 2 == 0:
                                    pe.wait_ge(S["h_split"], 8 * l + k // 2 + 1)
                                o = gb((name, i))[:, j * T:(j + 1) * T]
                                if n < NS:
                                    last = three(o, high[:, DT * j + k, :], low[:, DT * j + k, :], h_high[:, k, :], h_low[:, k, :],
                                                 k == 0, k == DT - 1)
                                else:
                                    last = mm(o, w[:, DT * j + k, :], h[:, k, :], k == 0, k == DT - 1)
                    last.then_inc(chunks_used, 1)
                    if n == 1:
                        pe.wait_ge(layer_in, 32 * (l + 1))
                        pe.wait_ge(all_consts_in, 16)
                        m_free(pe, l, "dt")
                        for k in range(DT):
                            last = mm(mb("dt")[0:H, 0:T], sw[:, SW["dt"] + H * k:SW["dt"] + H * (k + 1)], h[:, k, :],
                                      k == 0, k == DT - 1)
                        fill(l, "dt", last)

            def mixer_d_rows(l):
                pe.wait_ge(S["conv_silu"], l + 1)
                m_free(pe, l, "cb")
                for g in range(2):
                    for c in range(NCH):
                        i = 2 * g + c
                        last = mm(mb("cb")[:, i * P:(i + 1) * P], conv[:, 4 + g, c * P:(c + 1) * P],
                                  conv[:, 6 + g, c * P:(c + 1) * P])
                fill(l, "cb", last)
                for c in range(NCH):
                    turn(l, f"xt{c}", [conv[:, j, c * P:(c + 1) * P] for j in range(4)])
                turn(l, "bt", [conv[:, 4 + g, 0:P] for g in range(2)])
                pe.wait_ge(S["cs_ready"], l + 1)
                m_free(pe, l, "dtT")
                for i, src in enumerate((d_dt, d_cs)):
                    for c in range(NCH):
                        last = pe.transpose(mb("dtT")[:, (2 * i + c) * H:(2 * i + c + 1) * H], src[:, c * P:(c + 1) * P],
                                            ident[0:H, 0:H])
                fill(l, "dtT", last)
                for i in range(4):
                    m_free(pe, l, f"row{i}")
                    for j in range(2):
                        hd = 2 * i + j
                        last = mm(mb(f"row{i}")[:, j * T:(j + 1) * T], cc[0:H, CC["sel"] + hd * P:CC["sel"] + (hd + 1) * P], d_cs)
                    fill(l, f"row{i}", last)

            def mixer_d_out(l):
                m_done(pe, l, "bt")
                pe.wait_ge(S["xde_ready"], l + 1)
                m_free(pe, l, "st")
                for g in range(2):
                    last = mm(mb("st")[:, g * T:(g + 1) * T], btok[:, g, :], xde[:, g * T:(g + 1) * T])
                fill(l, "st", last)
                for c in range(NCH):
                    pe.wait_ge(S["mt_ready"], 2 * (NCH * l + c + 1))
                    m_free(pe, l, f"yd{c}")
                    if c:
                        pe.wait_ge(S["csc_ready"], 2 * (l + 1))
                        m_done(pe, l, "st")
                    for hd in range(H):
                        q, j = 64 * (hd % 2), hd // 2
                        o = mb(f"yd{c}")[q:q + 64, j * P:(j + 1) * P]
                        last = mm(o, xd[:, c, hd * 64:(hd + 1) * 64], mT[:, hd, :], True, c == 0)
                        if c:
                            last = mm(o, st[:, hd // 4, (hd % 4) * 64:(hd % 4 + 1) * 64], cs[:, hd, :], False, True)
                    fill(l, f"yd{c}", last)

            def mixer_d_norm(l):
                pe.wait_ge(S["ydsq"], l + 1)
                feature_sum(l, "dn", ones, seg4, 4)

            seg4 = tiles(20840, 4)

            def mixer_a(l):
                pe.wait_ge(S["wm_ready"], l + 1)
                for c in range(NCH):
                    pe.wait_ge(S["vn_ready"], NCH * l + c + 1)
                    m_free(pe, l, f"a{c}")
                    for g in range(4):
                        last = mm(mb(f"a{c}")[:, g * P:(g + 1) * P], vtok[:, c, g * P:(g + 1) * P],
                                  sw[:, SW["w_s"] + g * P:SW["w_s"] + (g + 1) * P])
                    fill(l, f"a{c}", last)

            def mixer_b(l):
                pe.wait_ge(S["pooled"], l + 1)
                two_banks(l, "b", lambda j: sw[:, SW["pool"] + j * P:SW["pool"] + (j + 1) * P], lambda j: yB[:, j, :])

            def mixer_c(l):
                def side(point):
                    merge_quarters(l, *SIDE_AT[point])

                side("cw")
                pe.wait_ge(S["lora_ready"], 2 * (l + 1))
                w2 = sw[0:64, SW["w2a2"]:SW["w2a2"] + 512]
                a2 = sw[64:P, SW["w2a2"]:SW["w2a2"] + 512]
                two_banks(l, "cw", lambda j: w2[:, j * P:(j + 1) * P], lambda j: zc[0:64, 12, 1:T + 1])
                two_banks(l, "ca", lambda j: a2[:, j * P:(j + 1) * P], lambda j: zc[64:P, 12, 1:T + 1])
                two_banks(l, "cg", lambda j: sw[:, SW["g2"] + j * P:SW["g2"] + (j + 1) * P], lambda j: zc[:, 13, 1:T + 1])
                side("ss")
                pe.wait_ge(S["krsq"], l + 1)
                two_banks(l, "ss", lambda j: heads, lambda j: tmp1[:, j, :])
                side("bo")
                pe.wait_ge(S["rk_ready"], l + 1)
                two_banks(l, "bo", lambda j: heads, lambda j: tmp2[:, j, :])
                for c in range(NCH):
                    turn(l, f"vt{c}", [zc[:, 8 + j, 1 + c * P:1 + (c + 1) * P] for j in range(4)])
                side("kt")
                pe.wait_ge(S["ab_ready"], l + 1)
                turn(l, "kt", [ka[:, j, 0:P] for j in range(4)])
                turn(l, "nt", [nb[:, j, 0:P] for j in range(4)])
                for c in range(NCH):
                    tc = slice(c * P, (c + 1) * P)
                    half = lambda hd: slice(64 * (hd % 2), 64 * (hd % 2) + 64)
                    for q in range(2):
                        m_free(pe, l, f"n{q}{c}")
                        for i in range(4):
                            hd = HEADS[4 * q + i]
                            last = mm(mb(f"n{q}{c}")[:, i * P:(i + 1) * P], ar[half(hd), hd // 2, c, 0, :], nb[half(hd), hd // 2, tc])
                        fill(l, f"n{q}{c}", last)
                    for slot in range(H):
                        hd, st_ = HEADS[slot], f"s{slot}{c}"
                        m_free(pe, l, st_)
                        both = ar[half(hd), hd // 2, c, :, :].rearrange("p a t -> p (a t)")
                        mm(mb(st_)[:, 0:T], nb[half(hd), hd // 2, tc], both)
                        last = mm(mb(st_)[:, T:2 * T], ka[half(hd), hd // 2, tc], both)
                        fill(l, st_, last)
                    for v in range(LEVELS):
                        base = (NCH * l + c) * LEVELS + v
                        side(f"t{v}{c}")
                        for q in range(2):
                            pe.wait_ge(S["x_ready"], 2 * base + q + 1)
                            if v == 0:
                                pe.wait_ge(S["sc_ready"], H * (NCH * l + c) + 4 * q + 4)
                            m_free(pe, l, f"t{q}{v}{c}")
                            for i in range(4):
                                s_ = 4 * q + i
                                last = mm(mb(f"t{q}{v}{c}")[:, i * P:(i + 1) * P], sc[:, s_, 0, :], xx[:, s_, :])
                            fill(l, f"t{q}{v}{c}", last)
                        side(f"z{v}{c}")
                        for q in range(2):
                            pe.wait_ge(S["z_ready"], 2 * base + 2 * (NCH * l + c) + q + 1)
                            pe.wait_ge(S["t_ready"], 2 * base + q + 1)
                            if v < LEVELS - 1:
                                m_free(pe, l, f"x{q}{v}{c}")
                                for i in range(4):
                                    s_ = 4 * q + i
                                    last = mm(mb(f"x{q}{v}{c}")[:, i * P:(i + 1) * P], zz[:, s_, :], tt[:, s_, :])
                                fill(l, f"x{q}{v}{c}", last)
                            m_free(pe, l, f"z{q}{v}{c}")
                            for i in range(4):
                                s_ = 4 * q + i
                                last = mm(mb(f"z{q}{v}{c}")[:, i * P:(i + 1) * P], tt[:, s_, :], zz[:, s_, :])
                            fill(l, f"z{q}{v}{c}", last)
                    if c == 0:
                        m_done(pe, l, "vt0")
                        m_done(pe, l, "vt1")
                    else:
                        pe.wait_ge(S["s0_ready"], l + 1)
                    for q in range(2):
                        m_free(pe, l, f"W{q}{c}")
                        for i in range(4):
                            slot = 4 * q + i
                            hd = HEADS[slot]
                            o = mb(f"W{q}{c}")[:, i * 64:(i + 1) * 64]
                            last = mm(o, sc[:, slot, 2, :], cv[:, c, hd * 64:(hd + 1) * 64], True, c == 0)
                            if c:
                                last = mm(o, ar[half(hd), hd // 2, c, 0, :], s0[half(hd), hd // 2, :], False, True)
                        fill(l, f"W{q}{c}", last)
                    side(f"U{c}")
                    pe.wait_ge(S["z_ready"], 2 * (LEVELS + 1) * (NCH * l + c + 1))
                    m_done(pe, l, f"W0{c}")
                    m_done(pe, l, f"W1{c}")
                    m_free(pe, l, f"U{c}")
                    for slot, hd in enumerate(HEADS):
                        last = mm(mb(f"U{c}")[:, hd * 64:(hd + 1) * 64], zz[:, slot, :], wb[:, slot * 64:(slot + 1) * 64])
                    fill(l, f"U{c}", last)
                    side(f"O{c}")
                    m_done(pe, l, f"U{c}")
                    m_free(pe, l, f"O{c}")
                    for slot, hd in enumerate(HEADS):
                        o = mb(f"O{c}")[half(hd), (hd // 2) * P:(hd // 2 + 1) * P]
                        mm(o, cv[:, c, hd * 64:(hd + 1) * 64], sc[:, slot, 3, :], True, False)
                        last = mm(o, ub[:, hd * 64:(hd + 1) * 64], sc[:, slot, 1, :], False, c == 0)
                        if c:
                            last = mm(o, s0[half(hd), hd // 2, :], ar[half(hd), hd // 2, c, 1, :], False, True)
                    fill(l, f"O{c}", last)
                    if c == 0:
                        m_done(pe, l, "kt")
                        m_done(pe, l, "nt")
                        m_free(pe, l, "S")
                        for hd in range(H):
                            o = mb("S")[half(hd), (hd // 2) * 64:(hd // 2 + 1) * 64]
                            mm(o, kbt[:, 0, hd * 64:(hd + 1) * 64], cv[:, 0, hd * 64:(hd + 1) * 64], True, False)
                            last = mm(o, kbt[:, 1, hd * 64:(hd + 1) * 64], ub[:, hd * 64:(hd + 1) * 64], False, True)
                        fill(l, "S", last)
                side("mu")
                m_done(pe, l, "O1")
                two_banks(l, "mu", lambda j: heads, lambda j: oo[:, j, :])
                side("va")
                pe.wait_ge(S["osq"], l + 1)
                two_banks(l, "va", lambda j: heads, lambda j: tiles(7696, 4)[:, j, :])

            ys = [yA, yB, yC, yD]

            def merge_quarters(l, lo, hi):
                for n in range(lo, hi):
                    (step, unit), part = MERGE_CHUNKS[n // 4], n % 4
                    w = chunk(chunk0(l) + NZ + n // 4)
                    if unit < 2:
                        if part == 0:
                            g_free(pe, l, ("gate", step, unit))
                        j = part // 2
                        for k in range(4 * (part % 2), 4 * (part % 2) + 4):
                            last = mm(gb(("gate", step, unit))[:, j * T:(j + 1) * T], w[:, DT * j + k, :], h[:, k, :],
                                      k == 0, k == DT - 1)
                    else:
                        branch = MERGE_ORDER[step // 2]
                        if part == 0:
                            if branch == 0:
                                pe.wait_ge(S["ya_ready"], NCH * (l + 1))
                            elif branch == 1:
                                m_done(pe, l, "b0")
                                m_done(pe, l, "b1")
                            elif branch == 2:
                                pe.wait_ge(S["yc_ready"], l + 1)
                            else:
                                pe.wait_ge(S["yd_ready"], 4 * (l + 1))
                        if part % 2 == 0:
                            g_free(pe, l, ("pj", step, part // 2))
                        for k in range(4):
                            last = mm(gb(("pj", step, part // 2))[:, (part % 2) * T:(part % 2 + 1) * T], w[:, 4 * part + k, :],
                                      ys[branch][:, k, :], k == 0, k == 3)
                    if part == 3:
                        last.then_inc(chunks_used, 1)

            def merge(l):
                merge_quarters(l, SIDE_END, 12 * STEPS)
                for i in range(N_OUT):
                    w = chunk(chunk0(l) + NZ + N_MERGE + i)
                    if i == 0:
                        pe.wait_ge(merged, 2 * STEPS * (l + 1))
                    g_free(pe, l, ("out", i))
                    for j in range(2):
                        for k in range(DT):
                            last = mm(gb(("out", i))[:, j * T:(j + 1) * T], w[:, DT * j + k, :], mg[:, k, :],
                                      k == 0, k == DT - 1)
                    last.then_inc(chunks_used, 1)

            def norm_sum(l, stage, n):
                m_free(pe, l, stage)
                for j in range(DT):
                    if j % 2 == 0:
                        pe.wait_ge(sq_ready, 4 * n + j // 2 + 1)
                    last = mm(mb(stage)[:, 0:T], ones, sq[:, j, :], j == 0, j == DT - 1)
                fill(l, stage, last)

            def ffn_split():
                low = [ring_low[:, i, :].rearrange("p (b m) -> p b m", b=BLK) for i in range(RING)]
                high = [w_high[:, i, :].rearrange("p (b m) -> p b m", b=BLK) for i in range(2)]
                with pe.Fori(0, FT // (2 * RING)) as i:
                    for s in range(2 * RING):
                        pe.wait_ge(low_ready, i * (2 * RING) + (NS + s + 1))
                        if s >= 3:
                            pe.wait_ge(ffn_drained, i * (2 * RING) + (s - 2))
                        else:
                            pe.wait_ge(ffn_drained, i * (2 * RING))
                        for j in range(2):
                            for k in range(DT):
                                if s == 0 and j == 0 and k % 2 == 0:
                                    pe.wait_ge(S["h_split"], 4 + k // 2 + 1)
                                last = three(gbank[gbanks[s % RING]][:, j * T:(j + 1) * T], high[s % 2][:, DT * j + k, :],
                                             low[(FFN0 + s) % RING][:, DT * j + k, :], h_high[:, k, :], h_low[:, k, :], k == 0, k == DT - 1)
                        last.then_inc(chunks_used, 1)
                for k in range(FT):
                    n = N_GU + k // 2
                    if k % 2 == 0:
                        pe.wait_ge(low_ready, NS + n + 1)
                    if k == 0 or k > FT - RING:
                        pe.wait_ge(ffn_drained, FT - RING + 1 if k == 0 else k + 1)
                    for d in range(DT):
                        last = three(mbank[d // 2][:, (d % 2) * T:(d % 2 + 1) * T], high[n % 2][:, (k % 2) * DT + d, :],
                                     low[(FFN0 + n) % RING][:, (k % 2) * DT + d, :], gu_high[:, k, :], gu_low[:, k, :],
                                     k == 0 and d % 2 == 0, k == FT - 1)
                    if k % 2:
                        last.then_inc(chunks_used, 1)

            def expert_chunk(e, n):
                slot = (N_CHUNKS + n) % RING
                pe.wait_ge(landed[slot], e * (16 * N_FFN // RING) + 16 * ((N_CHUNKS + n) // RING + 1))
                return ring[:, slot, :]

            def overflowed(e):
                done = e * (2 * GROUPS + 4) + (FT + 4)
                for n in range(N_GU):
                    w = expert_chunk(e, n).rearrange("p (k j m) -> p k j m", k=4, j=4)
                    if n % 4 == 0:
                        pe.wait_ge(ffn_drained, done + 2 * (n // 4))
                    up, half_k = n % 4 // 2, n % 2
                    for k in range(4):
                        for j in range(4):
                            last = mm(gbank[2 * up + j // 2][:, (j % 2) * T:(j % 2 + 1) * T], w[:, k, j, :], h[:, 4 * half_k + k, :],
                                      half_k == 0 and k == 0 and j % 2 == 0, half_k == 1 and k == 3)
                    last.then_inc(chunks_used, 1)
                pe.wait_ge(ffn_drained, done + 2 * GROUPS)
                for k in range(FT):
                    if k % 2 == 0:
                        w = expert_chunk(e, N_GU + k // 2).rearrange("p (b m) -> p b m", b=BLK)
                    for d in range(DT):
                        last = mm(mbank[d // 2][:, (d % 2) * T:(d % 2 + 1) * T], w[:, (k % 2) * DT + d, :], gu[:, k, :],
                                  k == 0 and d % 2 == 0, k == FT - 1)
                    if k % 2:
                        last.then_inc(chunks_used, 1)

            def gather():
                for i in range(2):
                    for j in range(4):
                        for c in range(NCH):
                            k = 4 * i + j
                            last = mm(mbank[i][:, j * CAP:(j + 1) * CAP], htok[:, c, k * P:(k + 1) * P], put[:, c, :], c == 0, c == 1)
                    last.then_inc(S["hg_filled"], 1)

            def give_back(lo):
                for i in (lo, lo + 1):
                    for j in range(2):
                        k = 2 * i + j
                        last = mm(mbank[i % 2][:, j * T:(j + 1) * T], ytok[:, k * P:(k + 1) * P], back)
                    last.then_inc(S["back_filled"], 1)

            def experts():
                pe.wait_ge(S["flag_ready"], 1)
                low = [ring_low[:, i, :].rearrange("p (k f) -> p k f", k=4) for i in range(RING)]
                high = [we_high[i][:, :].rearrange("p (k f) -> p k f", k=4) for i in range(3)]
                with pe.Fori(0, E) as e:
                    groups = e * GROUPS
                    for n in range(N_FFN):
                        if n == 0:
                            pe.wait_ge(S["hg_ready"], e * 2 + 2)
                        if n < N_GU and n % 4 == 0:
                            pe.wait_ge(S["hid_ready"], groups + max(n // 4 - 1, 0))
                        if n >= N_GU and n % 2 == 0:
                            pe.wait_ge(S["eu_ready"], groups + ((n - N_GU) // 2 + 1))
                        pe.wait_ge(low_ready, e * N_FFN + (L * NS + N_FFN + n + 1))
                        wl, wh = low[(MOE0 + n) % RING], high[n % 3]
                        for k in range(4):
                            if n < N_GU:
                                bank = gbank[2 * (n // 4 % 2) + n % 4 // 2]
                                kt = 4 * (n % 2) + k
                                last = three(bank[0:CAP, :], hg_high[:, kt, :], hg_low[:, kt, :], wh[:, k, :], wl[:, k, :],
                                             kt == 0, kt == DT - 1)
                            else:
                                kt = 2 * (n - N_GU) + k // 2
                                last = three(mbank[2 + k % 2][0:CAP, :], eu_high[:, kt, :], eu_low[:, kt, :], wh[:, k, :], wl[:, k, :],
                                             kt == 0, kt == FT - 1)
                        last.then_inc(chunks_used, 1)
                        if n == 2:
                            pe.wait_ge(S["y_ready"], e * 2 + 2)
                            pe.wait_ge(S["back_ready"], e + 1)
                            give_back(0)
                        if n == 4:
                            pe.wait_ge(S["back_drained"], e * 4 + 2)
                            give_back(2)
                        if n >= 6 and (n - 6) % 4 == 0 and n <= 30:
                            g = (n - 6) // 4
                            pe.wait_ge(S["hid_ready"], groups + (g + 1))
                            if g < 2:
                                pe.wait_ge(S["back_drained"], e * 4 + 4)
                            else:
                                pe.wait_ge(S["eu_ready"], groups + (g - 1))
                            for j in range(4):
                                last = pe.transpose(mbank[g % 2][:, j * CAP:(j + 1) * CAP], hid_tok[:, g % 2, j * P:(j + 1) * P],
                                                    ident[0:CAP, 0:CAP])
                            last.then_inc(S["hid_turned"], 1)
                        if n == 36:
                            pe.wait_ge(S["put_ready"], e * NCH + 2 * NCH)
                            pe.wait_ge(S["eu_ready"], groups + GROUPS)
                            gather()
                pe.wait_ge(S["hg_ready"], 2 * E + 2)
                pe.wait_ge(S["y_ready"], 2 * E + 2)
                pe.wait_ge(S["back_ready"], E + 1)
                give_back(0)
                pe.wait_ge(S["back_drained"], 4 * E + 2)
                give_back(2)

            def router():
                for c in range(NCH):
                    for k in range(DT):
                        last = mm(mbank[1][:, c * E:(c + 1) * E], h[:, k, c * P:(c + 1) * P],
                                  sw[:, SW["router"] + E * k:SW["router"] + E * (k + 1)], k == 0, k == DT - 1)
                last.then_inc(m_filled[1], 1)
                for c in range(NCH):
                    for i in range(2):
                        for j in range(4):
                            last = pe.transpose(gbank[2 * c + i][:, j * P:(j + 1) * P], h[:, 4 * i + j, c * P:(c + 1) * P], ident)
                        last.then_inc(S["htok_done"], 1)
                pe.wait_ge(S["comb_ready"], 1)
                for c in range(NCH):
                    last = pe.transpose(mbank[2][0:E, c * P:(c + 1) * P], rt_comb[:, c, :], ident)
                last.then_inc(m_filled[2], 1)
                pe.wait_ge(S["places"], 1)
                for c in range(NCH):
                    last = pe.transpose(mbank[2][:, 256 + c * E:256 + (c + 1) * E], routeT[:, 3, c * P:(c + 1) * P], ident[0:E, 0:E])
                last.then_inc(S["tok_done"], 1)
                sel = lambda e: cc[0:E, CC["sel"] + e * P:CC["sel"] + (e + 1) * P]
                for i in range(4):
                    pe.wait_ge(g_drained[i], L * G_TOTAL[i] + 1)
                for e in range(E):
                    last = mm(gbank[e // 2][:, (e % 2) * T:(e % 2 + 1) * T], sel(e), routeT[:, 0, :])
                last.then_inc(S["combs_done"], 1)
                pe.wait_ge(S["put_ready"], NCH)
                gather()
                pe.wait_ge(S["crow_ready"], 1)
                for e in range(E):
                    last = mm(gbank[e // 2][:, (e % 2) * T:(e % 2 + 1) * T], sel(e), routeT[:, 3, :])
                last.then_inc(S["rows_done"], 1)

            rt_comb = rt[:, 0:2 * E].rearrange("p (c e) -> p c e", c=NCH)

            for l in range(L):
                norm_sum(l, "norm1", 2 * l)
                project(l, 0, 14)
                mixer_d_rows(l)
                project(l, 14, 16)
                mixer_d_out(l)
                project(l, 16, 17)
                mixer_d_norm(l)
                project(l, 17, 18)
                mixer_a(l)
                mixer_b(l)
                project(l, 18, NZ)
                mixer_c(l)
                merge(l)
                norm_sum(l, "norm2", 2 * l + 1)
                pe.wait_ge(h_ready, 2 * DT * l + 2 * DT)
                for i in range(4):
                    pe.wait_ge(g_drained[i], (l + 1) * G_TOTAL[i])
                    pe.wait_ge(m_drained[i], (l + 1) * M_TOTAL[i])
                if l == 0:
                    ffn_split()
                else:
                    router()
                    experts()
                    overflow = pe.value_load(flag[0:1, 0:1], min_val=0, max_val=1)
                    with pe.If(overflow > 0):
                        with pe.Fori(0, E) as e:
                            overflowed(e)
            for j in range(DT):
                if j % 2 == 0:
                    pe.wait_ge(sq_ready, 4 * 2 * L + j // 2 + 1)
                last = mm(mbank[0][:, 0:T], ones, sq[:, j, :], j == 0, j == DT - 1)
            last.then_inc(m_filled[0], 1)

        @block.scalar
        def _(act):
            q = Count(act, a_seq)
            A = nc.scalar.activation

            act.wait_ge(consts_in, 32)
            eps = cc[:, CC["eps"]:CC["eps"] + 1]
            gn_eps = cc[:, CC["gn_eps"]:CC["gn_eps"] + 1]

            def drain(l, stage, ins):
                q.add(ins, m_drained[M_PLAN[stage][0]])

            def norm(x_done, stage_filled, root, meanwhile=lambda: None):
                for i in range(4):
                    x_done(i)
                    q.add(A(sq[:, 2 * i:2 * i + 2, :], x[:, 2 * i:2 * i + 2, :], ACT.Square), sq_ready)
                meanwhile()
                stage_filled()
                root(A(rms[:, :], mbank[0][:, 0:T], ACT.Sqrt, scale=1.0 / D, bias=eps))

            def evacuate(l, units):
                for unit in units:
                    name, i = unit
                    act.wait_ge(chunks_used, unit_chunk(l, unit) + 1)
                    src = gb(unit)[:, :]
                    two = src.rearrange("p (j t) -> p j t", j=2)
                    if name == "zg":
                        ins = A(zg[:, 2 * i:2 * i + 2, :], two, ACT.Silu)
                    elif name == "xbc":
                        ins = A(xbc[:, 2 * i:2 * i + 2, 3:T + 3], two, ACT.Copy)
                    elif name == "v":
                        ins = A(vtok[:, i, :], src, ACT.Gelu_apprx_tanh)
                    elif name == "u":
                        ins = A(u[:, 2 * i:2 * i + 2, :], two, ACT.Gelu_apprx_tanh)
                    elif name == "b":
                        ins = A(zb[:, 2 * i:2 * i + 2, 16:T + 16], two, ACT.Copy)
                    else:
                        ins = A(zc[:, 2 * i:2 * i + 2, 1:T + 1], two, ACT.Copy)
                    q.add(ins, g_drained[G_PLAN[unit][0]])

            def mixer_d_dt(l):
                act.wait_ge(S["dt_raw"], l + 1)
                q.step(A(d_abs, d_raw, ACT.Abs))
                q.step(A(d_abs, d_abs, ACT.Exp, scale=-1.0))
                q.step(A(ahead[0:H, 0:1], par(l, "a_log", rows=H), ACT.Exp))
                q.step(A(d_ln, d_abs, ACT.Ln, bias=1.0), S["dt_exp"])

            def mixer_d(l):
                act.wait_ge(S["conv_done"], l + 1)
                q.add(A(conv[:, :, :], conv[:, :, :], ACT.Silu), S["conv_silu"])
                evacuate(l, Z_UNITS[12:14])
                filled(act, l, "bt")
                drain(l, "bt", A(btok[:, :, :], mb("bt")[:, 0:T].rearrange("p (g n) -> p g n", g=2), ACT.Copy))
                evacuate(l, Z_UNITS[14:16])
                act.wait_ge(S["d_endraw"], l + 1)
                q.step(A(d_end, d_end, ACT.Exp), S["d_endexp"])
                for c in range(NCH):
                    act.wait_ge(S["seg_ready"], NCH * l + c + 1)
                    q.step(A(mT[:, :, :], seg[:, :, :], ACT.Exp), S["seg_exp"])
                    if c == 0:
                        filled(act, l, "st")
                        drain(l, "st", A(st[:, :, :], mb("st")[:, :].rearrange("p (g n) -> p g n", g=2), ACT.Copy))
                        act.wait_ge(S["csc_ready"], 2 * l + 1)
                        q.step(A(cs[:, :, :], cs[:, :, :], ACT.Exp), S["er_ready"])
                evacuate(l, Z_UNITS[16:17])
                act.wait_ge(S["yd_ready"], 4 * l + 1)
                q.add(A(tiles(20840, 4)[:, :, :], yD[:, :, :], ACT.Square), S["ydsq"])
                filled(act, l, "dn")
                drain(l, "dn", A(rms[:, :], mb("dn")[:, 0:T], ACT.Sqrt, scale=1.0 / 512, bias=eps))

            def mixer_a(l):
                act.wait_ge(S["v_stats"], l + 1)
                q.add(A(small[:, 16:18], small[:, 16:18], ACT.Sqrt, bias=eps), S["v_std"])

            def mixer_b(l):
                for i in range(2):
                    filled(act, l, f"b{i}")
                    for j in range(2):
                        ins = A(yB[:, 2 * i + j, :], mb(f"b{i}")[:, j * T:(j + 1) * T], ACT.Copy, scale=par(l, "b_scale", 2 * i + j))
                        (q.add(ins, a_seq) if j == 0 else drain(l, f"b{i}", ins))

            def mixer_c(l):
                def side(first, last=None):
                    gates(l, SIDE_AT[first][0], SIDE_AT[last or first][1])

                side("cw")
                act.wait_ge(S["zc_mixed"], l + 1)
                q.add(A(zc[0:64, 12, 1:T + 1], zc[0:64, 12, 1:T + 1], ACT.Tanh), S["lora_ready"])
                q.add(A(zc[:, 13, 1:T + 1], zc[:, 13, 1:T + 1], ACT.Sigmoid), S["lora_ready"])
                for name, dst, bias in (("cw", w_log, "w0"), ("ca", aa, "a0")):
                    for i in range(2):
                        filled(act, l, f"{name}{i}")
                        for j in range(2):
                            ins = A(dst[:, 2 * i + j, :], mb(f"{name}{i}")[:, j * T:(j + 1) * T], ACT.Sigmoid,
                                    bias=par(l, bias, 2 * i + j))
                            (q.add(ins, a_seq) if j == 0 else drain(l, f"{name}{i}", ins))
                for i in range(2):
                    filled(act, l, f"cg{i}")
                    drain(l, f"cg{i}", A(gg[:, 2 * i:2 * i + 2, :], mb(f"cg{i}")[:, :].rearrange("p (j t) -> p j t", j=2), ACT.Copy))
                side("ss")
                act.wait_ge(S["kr_ready"], l + 1)
                q.add(A(tmp1[:, :, :], kk[:, :, :], ACT.Square), S["krsq"])
                act.wait_ge(S["ss_ready"], l + 1)
                q.add(A(tmp1[:, :, :], tmp1[:, :, :], ACT.Sqrt), S["ss_sqrt"])
                side("bo")
                act.wait_ge(S["cum_ready"], l + 1)
                q.add(A(e_in[:, :, :], c_sum[:, :, :], ACT.Exp), S["e_ready"])
                q.add(A(e_neg[:, :, :], c_sum[:, :, :], ACT.Exp, scale=-1.0), S["e_ready"])
                q.add(A(e_ex[:, :, :], w_log[:, :, :], ACT.Exp), S["e_ready"])
                q.add(A(small[:, 28:32], small[:, 28:32], ACT.Exp), S["e_ready"])
                act.wait_ge(S["ab_ready"], l + 1)
                m_done(act, l, "bo1")
                for c in range(NCH):
                    filled(act, l, f"vt{c}")
                    drain(l, f"vt{c}", A(cv[:, c, :], mb(f"vt{c}")[:, :], ACT.Copy))
                side("kt")
                for i, name in enumerate(("kt", "nt")):
                    filled(act, l, name)
                    drain(l, name, A(kbt[:, i, :], mb(name)[:, :], ACT.Copy))
                for c in range(NCH):
                    side(f"t0{c}", f"z{LEVELS - 1}{c}")
                    filled(act, l, f"W0{c}")
                    filled(act, l, f"W1{c}")
                    if c == 0:
                        act.wait_ge(S["ab_ready"], l + 1)
                    else:
                        filled(act, l, "S")
                    for i in range(2):
                        drain(l, f"W{i}{c}", A(wb[:, i * T:(i + 1) * T], mb(f"W{i}{c}")[:, 0:T], ACT.Copy))
                    side(f"U{c}")
                    filled(act, l, f"U{c}")
                    drain(l, f"U{c}", A(ub, mb(f"U{c}")[:, :], ACT.Copy))
                    side(f"O{c}")
                    filled(act, l, f"O{c}")
                    drain(l, f"O{c}", A(oo[:, :, c * P:(c + 1) * P], mb(f"O{c}")[:, :].rearrange("p (j t) -> p j t", j=4), ACT.Copy))
                side("mu")
                act.wait_ge(S["cent"], 2 * (l + 1))
                q.add(A(tiles(7696, 4)[:, :, :], oo[:, :, :], ACT.Square), S["osq"])
                side("va")
                for i in range(2):
                    filled(act, l, f"va{i}")
                    drain(l, f"va{i}", A(tiles(8720, 4)[:, 2 * i:2 * i + 2, :], mb(f"va{i}")[:, :].rearrange("p (j t) -> p j t", j=2),
                                         ACT.Sqrt, scale=1.0 / 64, bias=gn_eps))

            def gates(l, lo, hi):
                for n in range(2 * STEPS):
                    step, i = n // 2, n % 2
                    if lo < 4 * MERGE_CHUNKS.index((step, i)) + 4 <= hi:
                        unit = ("gate", step, i)
                        act.wait_ge(chunks_used, unit_chunk(l, unit) + 1)
                        if step < STEPS - 1 and 2 * STEPS * l + n > 1:
                            act.wait_ge(merged, 2 * STEPS * l + n - 1)
                        q.add(A(sg_of(step, i), gb(unit)[:, :], ACT.Sigmoid), g_drained[G_PLAN[unit][0]])

            def z_high(l, n):
                c = chunk0(l) + n
                act.wait_ge(landed[c % RING], 16 * (c // RING + 1))
                if c >= 2 and n < 2:
                    act.wait_ge(chunks_used, chunk0(l))
                A(w_high[:, n % 2, :], ring[:, c % RING, :], ACT.Copy).then_inc(high_ready, 1)

            def split_h(n):
                for i in range(4):
                    act.wait_ge(h_ready, DT * n + 2 * i + 2)
                    A(h_high[:, 2 * i:2 * i + 2, :], h[:, 2 * i:2 * i + 2, :], ACT.Copy).then_inc(S["h_split_high"], 1)

            def high(n, i=0):
                slot = (FFN0 + n) % RING
                act.wait_ge(landed[slot], i * 32 + 16 * ((FFN0 + n) // RING + 1))
                A(w_high[:, n % 2, :], ring[:, slot, :], ACT.Copy).then_inc(high_ready, 1)

            def dense():
                with act.Fori(0, FT // (2 * RING)) as i:
                    for s in range(2 * RING):
                        act.wait_ge(chunks_used, i * (2 * RING) + (FFN0 + s + 1))
                        A(sil[:, s % RING, :], gbank[gbanks[s % RING]][:, 0:T], ACT.Silu).then_inc(silu_done, 1)
                        high(s + 2, i)
                for n in range(FT + 2, N_FFN):
                    act.wait_ge(chunks_used, FFN0 + n - 1)
                    high(n)

            def gathered():
                for i in range(2):
                    A(hg_high[:, 4 * i:4 * i + 4, :], mbank[i][:, 0:4 * CAP].rearrange("p (j s) -> p j s", j=4), ACT.Copy)\
                        .then_inc(S["hg_high_ready"], 1)

            def output():
                for i in range(2):
                    A(ytok[:, i * 512:(i + 1) * 512], mbank[2 + i][0:CAP, :], ACT.Copy).then_inc(S["y_ready"], 1)

            def experts():
                act.wait_ge(S["hg_filled"], 2)
                gathered()
                with act.Fori(0, E) as e:
                    groups = e * GROUPS
                    for n in range(N_FFN):
                        slot = (MOE0 + n) % RING
                        act.wait_ge(landed[slot], e * (16 * N_FFN // RING) + 16 * ((MOE0 + n) // RING + 1))
                        act.wait_ge(chunks_used, e * N_FFN + (MOE0 + n - 2))
                        A(we_high[n % 3][:, :], ring[:, slot, :], ACT.Copy).then_inc(high_ready, 1)
                        if n == 2:
                            act.wait_ge(chunks_used, e * N_FFN + MOE0)
                            act.wait_ge(S["back_filled"], e * 4)
                            act.wait_ge(S["zeroed"], 2)
                            output()
                        if n % 4 == 0 and 4 <= n <= N_GU:
                            g = n // 4 - 1
                            act.wait_ge(chunks_used, e * N_FFN + (MOE0 + n - 2))
                            A(sil_tok[:, g % 2, :], gbank[2 * (g % 2)][0:CAP, :], ACT.Silu).then_inc(S["silu_tok"], 1)
                        if n >= 9 and (n - 9) % 4 == 0 and n <= 33:
                            g = (n - 9) // 4
                            act.wait_ge(S["hid_turned"], groups + (g + 1))
                            A(eu_high[:, 4 * g:4 * g + 4, :], mbank[g % 2][:, 0:4 * CAP].rearrange("p (j s) -> p j s", j=4), ACT.Copy)\
                                .then_inc(S["eu_high_ready"], 1)
                        if n == 39:
                            act.wait_ge(S["hg_filled"], e * 2 + 4)
                            gathered()
                act.wait_ge(chunks_used, N_CHUNKS)
                act.wait_ge(S["back_filled"], 4 * E)
                output()

            def overflowed(e):
                for g in range(GROUPS):
                    act.wait_ge(chunks_used, e * N_FFN + (N_CHUNKS + 4 * g + 2))
                    for i in range(2):
                        A(sil2[:, i, :], gbank[i][:, :], ACT.Silu).then_inc(silu_done, 1)

            for l in range(L):
                if l == 0:
                    act.wait_ge(x_loaded, 16)
                norm(lambda i: act.wait_ge(ffn_drained, FT + i + 1) if l else None, lambda: filled(act, l, "norm1"),
                     lambda ins: drain(l, "norm1", ins), lambda: (z_high(l, 0), z_high(l, 1)))
                split_h(2 * l)
                for n in range(10):
                    act.wait_ge(chunks_used, chunk0(l) + n + 1)
                    z_high(l, n + 2)
                    if n == 0:
                        act.wait_ge(padded, 3 * (l + 1))
                    evacuate(l, Z_UNITS[n:n + 1])
                mixer_d_dt(l)
                evacuate(l, Z_UNITS[10:12])
                mixer_d(l)
                mixer_a(l)
                evacuate(l, Z_UNITS[17:18])
                mixer_b(l)
                evacuate(l, Z_UNITS[18:])
                mixer_c(l)
                if l == 0:
                    m_done(act, l, "S")
                    act.wait_ge(S["ya_ready"], NCH)
                    act.dma_start(sw[:, :], sw_in[1]).then_inc(layer_in, 16)
                    act.dma_start(rep[:, :], rep_in[1]).then_inc(layer_in, 16)
                gates(l, SIDE_END, 12 * STEPS)
                if l == 0:
                    high(0)
                norm(lambda i: act.wait_ge(x_mixed, N_OUT * l + i + 1), lambda: filled(act, l, "norm2"), lambda ins: drain(l, "norm2", ins),
                     lambda: high(1) if l == 0 else None)
                if l == 0:
                    split_h(1)
                    dense()
                else:
                    act.wait_ge(S["logits_top"], 1)
                    q.step(A(small[:, 40:42], small[:, 36:38], ACT.Sigmoid))
                    q.add(A(small[:, 42:44], small[:, 36:38], ACT.Sigmoid, scale=-1.0), S["probs"])
                    act.wait_ge(S["htok_done"], 4)
                    for i in range(4):
                        q.add(A(htok[:, i // 2, (i % 2) * 512:(i % 2 + 1) * 512], gbank[i][:, :], ACT.Copy), g_drained[i])
                    experts()
                    act.wait_ge(S["flag_ready"], 1)
                    overflow = act.value_load(flag[0:1, 0:1], min_val=0, max_val=1)
                    with act.If(overflow > 0):
                        with act.Fori(0, E) as e:
                            overflowed(e)
            act.wait_ge(S["ffn_x"], 8)
            norm(lambda i: None, lambda: act.wait_ge(m_filled[0], L * M_TOTAL[0] + 1), lambda ins: q.add(ins, m_drained[0]))
            act.wait_ge(S["out_ready"], DT)
            act.dma_start(out, h[:, :, :]).then_inc(out_stored, 16)
            act.wait_ge(out_stored, 16)

        @block.gpsimd
        def _(pool):
            q = Count(pool, p_seq)
            G = nc.gpsimd
            pool.wait_ge(all_consts_in, 16)
            for l in range(L):
                if l:
                    pool.wait_ge(S["ffn_x"], 4)
                q.add(G.memset(zc[:, :, 0:1], 0.0), padded)
                q.add(G.memset(xbc[:, :, 0:3], 0.0), padded)
                q.add(G.memset(zb[:, :, 0:16], 0.0), padded)
                g_done(pool, l, ("b", 0))
                g_done(pool, l, ("b", 1))
                pool.wait_ge(padded, 3 * (l + 1))
                w = T + 16
                q.step(G.tensor_tensor(p2[:, :, 1:w], zb[:, :, 1:w], zb[:, :, 0:w - 1], ALU.add))
                q.step(G.tensor_tensor(p4[:, 1:4, 3:w], p2[:, 1:4, 3:w], p2[:, 1:4, 1:w - 2], ALU.add))
                q.step(G.tensor_tensor(p2[:, 2:4, 7:w], p4[:, 2:4, 7:w], p4[:, 2:4, 3:w - 4], ALU.add))
                q.step(G.tensor_tensor(p4[:, 3:4, 15:w], p2[:, 3:4, 15:w], p2[:, 3:4, 7:w - 8], ALU.add))
                count = cc[:, CC["count"]:CC["count"] + 4 * T].rearrange("p (g t) -> p g t", g=4)
                for g, src in enumerate((p2, p4, p2, p4)):
                    q.step(G.tensor_tensor(yB[:, g, :], src[:, g, 16:w], count[:, g, :], ALU.mult))
                q.step(G.tensor_tensor(yB[:, :, :], yB[:, :, :], zb[:, :, 16:w], ALU.subtract), S["pooled"])
                for n in range(4, 2 * STEPS):
                    pool.wait_ge(S["gated"], (2 * STEPS - 4) * l + n - 3)
                    pool.wait_ge(merged, 2 * STEPS * l + n)
                    m2 = mg[:, 2 * (n % 4):2 * (n % 4) + 2, :]
                    G.tensor_tensor(m2, sg_of(n // 2, n % 2).rearrange("p (j t) -> p j t", j=2), m2, ALU.add).then_inc(merged, 1)

        @block.vector
        def _(dve):
            q = Count(dve, v_seq)
            V = nc.vector
            TT = V.tensor_tensor

            def marker():
                return V.tensor_copy(small[:, 60:61], small[:, 61:62])

            q.step(V.memset(small[:, 60:62], 0.0))
            dve.wait_ge(consts_in, 32)

            def drain(stage, ins):
                q.add(ins, m_drained[M_PLAN[stage][0]])

            def norm(root_done, gain, done):
                root_done()
                q.step(V.reciprocal(rstd[:, :], rms[:, :]))
                for k in range(DT):
                    q.add(V.scalar_tensor_tensor(h[:, k, :], x[:, k, :], gain(k), rstd[:, :], ALU.mult, ALU.mult), done)

            def mixer_d_dt(l):
                filled(dve, l, "dt")
                drain("dt", V.tensor_scalar(d_raw, mb("dt")[0:H, 0:T], par(l, "dt_bias", rows=H), None, ALU.add))
                m_done(dve, l, "dt")
                q.step(V.tensor_copy(d_raw, d_raw), S["dt_raw"])

            def mixer_d_decay(l):
                dve.wait_ge(S["dt_exp"], l + 1)
                q.step(V.scalar_tensor_tensor(d_dt, d_raw, 0.0, d_ln, ALU.max, ALU.add))
                q.step(V.tensor_scalar(d_abs, d_dt, ahead[0:H, 0:1], -1.0, ALU.mult, ALU.mult))
                q.step(V.tensor_tensor_scan(d_cs, cc[0:H, CC["reset"]:CC["reset"] + T], d_abs, 0.0, ALU.mult, ALU.add), S["cs_ready"])

            def mixer_d_conv(l):
                for i in range(4):
                    g_done(dve, l, ("xbc", i))
                for k in range(4):
                    z_low(l, 8 + k)
                    for j in range(8):
                        w = par(l, "conv_w", 8 * k + j)
                        if k == 0:
                            ins = V.tensor_scalar(conv[:, j, :], xbc[:, j, 0:T], w, par(l, "conv_b", j), ALU.mult, ALU.add)
                        else:
                            ins = V.scalar_tensor_tensor(conv[:, j, :], xbc[:, j, k:k + T], w, conv[:, j, :], ALU.mult, ALU.add)
                        if k == 3 and j == 7:
                            q.step(ins, S["conv_done"])
                        elif j == 7:
                            q.step(ins)
                        else:
                            q.add(ins, v_seq)

            def mixer_d(l):
                up = const("incl_up")
                filled(dve, l, "cb")
                drain("cb", TT(cbm[:, :, :], mb("cb")[:, :].rearrange("p (i t) -> p i t", i=4), over(up, 4), ALU.mult))
                filled(dve, l, "dtT")
                drain("dtT", V.tensor_copy(area(17256, 32), mb("dtT")[:, 0:32]))
                m_done(dve, l, "dtT")
                for c in range(NCH):
                    filled(dve, l, f"xt{c}")
                    drain(f"xt{c}", TT(xd[:, c, :].rearrange("p (h d) -> p h d", h=H),
                                       mb(f"xt{c}")[:, :].rearrange("p (h d) -> p h d", h=H), along(tok[:, 0, c, :], 64), ALU.mult))
                for i in range(4):
                    row = mb(f"row{i}")[:, :].rearrange("p (j t) -> p j t", j=2)
                    filled(dve, l, f"row{i}")
                    for j in range(2):
                        hd = 2 * i + j
                        q.add(V.tensor_scalar(seg[:, hd, :], row[:, j, 0:P], tok[:, 1, 0, hd:hd + 1], 0.0, ALU.subtract, ALU.min), v_seq)
                        q.add(V.tensor_scalar(seg1[:, hd, :], row[:, j, P:T], tok[:, 1, 1, hd:hd + 1], 0.0, ALU.subtract, ALU.min), v_seq)
                    q.add(V.tensor_copy(cs[:, 2 * i:2 * i + 2, :], row[:, :, P:T]), v_seq)
                    drain(f"row{i}", TT(d_end[:, 2 * i:2 * i + 2].unsqueeze(2), row[:, :, P - 1:P], tok[:, 1, 0, 2 * i:2 * i + 2].unsqueeze(2),
                                        ALU.subtract))
                m_done(dve, l, "row3")
                m_done(dve, l, "row2")
                m_done(dve, l, "row1")
                m_done(dve, l, "row0")
                q.step(V.tensor_scalar(d_end, d_end, 0.0, None, ALU.min), S["d_endraw"])
                q.step(marker(), S["seg_ready"])
                dve.wait_ge(S["d_endexp"], l + 1)
                for c in range(NCH):
                    m_done(dve, l, f"xt{c}")
                q.step(TT(xde.rearrange("p (h d) -> p h d", h=H), xd[:, 0, :].rearrange("p (h d) -> p h d", h=H), along(d_end, 64), ALU.mult),
                       S["xde_ready"])
                q.step(marker(), S["csc_ready"])
                m_done(dve, l, "cb")
                for c in range(NCH):
                    dve.wait_ge(S["seg_exp"], NCH * l + c + 1)
                    for g in range(2):
                        q.step(TT(mT[:, 4 * g:4 * g + 4, :], mT[:, 4 * g:4 * g + 4, :], over(cbm[:, 2 * g + c, :], 4), ALU.mult), S["mt_ready"])
                    if c == 0:
                        dve.wait_ge(S["er_ready"], l + 1)
                        for g in range(2):
                            ins = TT(cs[:, 4 * g:4 * g + 4, :], cs[:, 4 * g:4 * g + 4, :], over(conv[:, 6 + g, P:T], 4), ALU.mult)
                            q.step(ins, S["csc_ready"] if g else None)
                        filled(dve, l, "yd0")
                        q.step(V.tensor_copy(seg[:, :, :], seg1[:, :, :]), S["seg_ready"])
                for c in range(NCH):
                    filled(dve, l, f"yd{c}")
                    for j in range(4):
                        ins = V.scalar_tensor_tensor(yD[:, j, c * P:(c + 1) * P], conv[:, j, c * P:(c + 1) * P], par(l, "skip", j),
                                                     mb(f"yd{c}")[:, j * P:(j + 1) * P], ALU.mult, ALU.add)
                        (q.add(ins, v_seq) if j < 3 else drain(f"yd{c}", ins))
                m_done(dve, l, "yd1")
                m_done(dve, l, "yd0")
                dve.wait_ge(v_seq, q.n[id(v_seq)])
                g_done(dve, l, ("zg", 0))
                g_done(dve, l, ("zg", 1))
                q.step(TT(yD[:, :, :], yD[:, :, :], zg[:, :, :], ALU.mult), S["yd_ready"])
                m_done(dve, l, "dn")
                q.step(V.reciprocal(rstd[:, :], rms[:, :]))
                for j in range(4):
                    ins = V.scalar_tensor_tensor(yD[:, j, :], yD[:, j, :], par(l, "norm_d", j), rstd[:, :], ALU.mult, ALU.mult)
                    (q.add(ins, v_seq) if j == 0 else q.add(ins, S["yd_ready"]))
                dve.wait_ge(S["yd_ready"], q.n[id(S["yd_ready"])])


            def mixer_a(l):
                dve.wait_ge(layer_in, 32 * (l + 1))
                ws = sw[:, SW["w_s"]:SW["w_s"] + 512].rearrange("p (g t) -> p g t", g=4)
                q.step(TT(ws, ws, over(const("incl_up"), 4), ALU.mult), S["wm_ready"])
                for c in range(NCH):
                    g_done(dve, l, ("v", c))
                    q.step(V.bn_stats(small[:, 6 * c:6 * c + 6], vtok[:, c, :]))
                    q.step(V.bn_aggr(small[:, 12 + 20 * c:14 + 20 * c], small[:, 6 * c:6 * c + 6]))
                    q.step(V.tensor_copy(small[:, 16 + c:17 + c], small[:, 13 + 20 * c:14 + 20 * c]), S["v_stats"] if c else None)
                dve.wait_ge(S["v_std"], l + 1)
                q.step(V.reciprocal(small[:, 16:18], small[:, 16:18]))
                for c in range(NCH):
                    v = vtok[:, c, :]
                    q.step(V.tensor_scalar(v, v, small[:, 12 + 20 * c:13 + 20 * c], small[:, 16 + c:17 + c], ALU.subtract, ALU.mult))
                    q.step(TT(v, v, rep[:, 0:512], ALU.mult))
                    q.step(TT(v, v, rep[:, 512:1024], ALU.add), S["vn_ready"])
                for i in range(2):
                    g_done(dve, l, ("u", i))
                for c in range(NCH):
                    filled(dve, l, f"a{c}")
                    y = yA[:, :, c * P:(c + 1) * P]
                    drain(f"a{c}", TT(y, mb(f"a{c}")[:, :].rearrange("p (g t) -> p g t", g=4),
                                      rep[:, 1024:1536].rearrange("p (g t) -> p g t", g=4), ALU.add))
                    m_done(dve, l, f"a{c}")
                    q.step(TT(y, y, u[:, :, c * P:(c + 1) * P], ALU.mult), S["ya_ready"])

            def mixer_c(l):
                def side(first, last=None):
                    products(l, SIDE_AT[first][0], SIDE_AT[last or first][1])

                for i in range(CT // 2):
                    g_done(dve, l, ("c", i))
                dve.wait_ge(S["pooled"], l + 1)
                now = zc[:, :, 1:T + 1]
                q.step(TT(dif[:, :, :], zc[:, :, 0:T], now, ALU.subtract))
                for j in range(CT):
                    ins = V.scalar_tensor_tensor(zc[:, j, 1:T + 1], dif[:, j, :], par(l, "mix", j), zc[:, j, 1:T + 1], ALU.mult, ALU.add)
                    (q.add(ins, v_seq) if j < CT - 1 else q.step(ins, S["zc_mixed"]))
                dve.wait_ge(v_seq, q.n[id(v_seq)])
                r, k, v = zc[:, 0:4, 1:T + 1], zc[:, 4:8, 1:T + 1], zc[:, 8:12, 1:T + 1]
                for j in range(4):
                    ins = V.tensor_scalar(kk[:, j, :], k[:, j, :], par(l, "k_k", j), None, ALU.mult)
                    (q.add(ins, v_seq) if j < 3 else q.step(ins, S["kr_ready"]))
                dve.wait_ge(v_seq, q.n[id(v_seq)])
                side("cw")
                m_done(dve, l, "cw0")
                m_done(dve, l, "cw1")
                q.step(V.tensor_scalar(w_log[:, :, :], w_log[:, :, :], -DECAY, None, ALU.mult))
                flat = lambda ap: ap.rearrange("p j t -> p (j t)")
                q.step(V.tensor_tensor_scan(flat(c_sum), const("reset", 4 * T), flat(w_log), 0.0, ALU.mult, ALU.add))
                by_chunk = lambda ap: flat(ap).rearrange("p (n t) -> p n t", t=P)
                mid = small[:, 20:28]
                q.step(V.tensor_scalar(mid.unsqueeze(2), by_chunk(c_sum)[:, :, P - 1:P], 0.5, None, ALU.mult))
                q.step(TT(by_chunk(c_sum), by_chunk(c_sum), along(mid, P), ALU.subtract))
                q.step(TT(small[:, 28:32], small[:, 20:28:2], small[:, 21:28:2], ALU.add))
                q.step(TT(w_log[:, :, :], c_sum[:, :, :], w_log[:, :, :], ALU.subtract), S["cum_ready"])
                m_done(dve, l, "ca0")
                m_done(dve, l, "ca1")
                for j in range(4):
                    q.add(V.tensor_scalar(k2[:, j, :], aa[:, j, :], -1.0, par(l, "k_a", j), ALU.add, ALU.mult), v_seq)
                dve.wait_ge(v_seq, q.n[id(v_seq)])
                for j in range(4):
                    q.add(V.scalar_tensor_tensor(k2[:, j, :], k2[:, j, :], 1.0, k[:, j, :], ALU.add, ALU.mult), v_seq)
                dve.wait_ge(v_seq, q.n[id(v_seq)])
                for i in range(2):
                    filled(dve, l, f"ss{i}")
                filled(dve, l, "ss1")
                for i in range(2):
                    drain(f"ss{i}", V.tensor_scalar(tmp1[:, 2 * i:2 * i + 2, :], mb(f"ss{i}")[:, :].rearrange("p (j t) -> p j t", j=2),
                                                    FLOOR, None, ALU.max))
                for i in range(2):
                    m_done(dve, l, f"ss{i}")
                for j in range(4):
                    ins = V.scalar_tensor_tensor(tmp2[:, j, :], r[:, j, :], par(l, "r_k", j), k2[:, j, :], ALU.mult, ALU.mult)
                    if j < 3:
                        q.add(ins, v_seq)
                    else:
                        q.step(ins, S["rk_ready"])
                dve.wait_ge(v_seq, q.n[id(v_seq)])
                q.step(marker(), S["ss_ready"])
                side("ss", "bo")
                dve.wait_ge(S["ss_sqrt"], l + 1)
                q.step(V.reciprocal(tmp1[:, :, :], tmp1[:, :, :]))
                q.step(TT(kk[:, :, :], kk[:, :, :], tmp1[:, :, :], ALU.mult))
                dve.wait_ge(S["e_ready"], 4 * (l + 1))
                arj = ar.rearrange("p j c a t -> p (j c) a t")
                q.add(TT(arj[:, :, 0, :], by_chunk(kk), by_chunk(e_ex), ALU.mult), v_seq)
                rc = r.rearrange("p j (c t) -> p j c t", c=NCH)
                q.add(TT(ar[:, :, :, 1, :], rc, e_in.rearrange("p j (c t) -> p j c t", c=NCH), ALU.mult), v_seq)
                q.add(TT(ka[:, :, :], k2[:, :, :], e_neg[:, :, :], ALU.mult), v_seq)
                q.step(V.scalar_tensor_tensor(flat(aa), flat(kk), -1.0, flat(aa), ALU.mult, ALU.mult))
                q.step(TT(nb[:, :, :], aa[:, :, :], e_neg[:, :, :], ALU.mult), S["ab_ready"])
                for i in range(2):
                    filled(dve, l, f"bo{i}")
                    drain(f"bo{i}", TT(bv[:, 2 * i:2 * i + 2, :], mb(f"bo{i}")[:, :].rearrange("p (j t) -> p j t", j=2),
                                       v[:, 2 * i:2 * i + 2, :], ALU.mult))
                side("kt")
                mask = cc[:, CC["strict_up"]:CC["strict_up"] + 2 * P]
                for c in range(NCH):
                    for g in range(2):
                        four = slice(4 * g, 4 * g + 4)
                        filled(dve, l, f"n{g}{c}")
                        if c and g == 0:
                            filled(dve, l, "O0")
                        drain(f"n{g}{c}", TT(xx[:, four, :], mb(f"n{g}{c}")[:, :].rearrange("p (i t) -> p i t", i=4), over(const("low2"), 4), ALU.mult))
                        m_done(dve, l, f"n{g}{c}")
                        q.step(TT(xx[:, four, :], xx[:, four, :], over(ident, 4), ALU.add), S["x_ready"])
                    for hd in range(H):
                        filled(dve, l, f"s{hd}{c}")
                        drain(f"s{hd}{c}", TT(sc[:, hd, :, :].rearrange("p (b a) t -> p b (a t)", b=2), mb(f"s{hd}{c}")[:, :].rearrange("p (b f) -> p b f", b=2), over(mask, 2), ALU.mult))
                        m_done(dve, l, f"s{hd}{c}")
                        q.step(TT(zz[:, hd, :], sc[:, hd, 0, :], const("up2"), ALU.mult), S["sc_ready"])
                    for g in range(2):
                        four = slice(4 * g, 4 * g + 4)
                        q.step(TT(zz[:, four, :], zz[:, four, :], over(ident, 4), ALU.add), S["z_ready"])
                    for lv in range(LEVELS):
                        off = cc[:, CC["off"] + lv * P:CC["off"] + (lv + 1) * P]
                        for g in range(2):
                            four = slice(4 * g, 4 * g + 4)
                            filled(dve, l, f"t{g}{lv}{c}")
                            src = mb(f"t{g}{lv}{c}")[:, :].rearrange("p (i t) -> p i t", i=4)
                            drain(f"t{g}{lv}{c}", TT(tt[:, four, :], src, over(off, 4), ALU.mult))
                            m_done(dve, l, f"t{g}{lv}{c}")
                            q.add(marker(), S["t_ready"])
                        for g in range(2):
                            four = slice(4 * g, 4 * g + 4)
                            if lv < LEVELS - 1:
                                st_ = f"x{g}{lv}{c}"
                                filled(dve, l, st_)
                                drain(st_, TT(xx[:, four, :], mb(st_)[:, :].rearrange("p (i t) -> p i t", i=4), xx[:, four, :], ALU.add))
                                m_done(dve, l, st_)
                                q.add(marker(), S["x_ready"])
                            st_ = f"z{g}{lv}{c}"
                            filled(dve, l, st_)
                            drain(st_, TT(zz[:, four, :], mb(st_)[:, :].rearrange("p (i t) -> p i t", i=4), zz[:, four, :], ALU.add))
                            m_done(dve, l, st_)
                            q.add(marker(), S["z_ready"])
                        side(f"t{lv}{c}", f"z{lv}{c}")
                    side(f"U{c}", f"O{c}")
                    if c == 0:
                        filled(dve, l, "S")
                        drain("S", TT(s0[:, :, :], mb("S")[:, 0:256].rearrange("p (j f) -> p j f", j=4), along(small[:, 28:32], 64), ALU.mult))
                        m_done(dve, l, "S")
                        q.step(marker(), S["s0_ready"])
                m_done(dve, l, "O0")
                m_done(dve, l, "O1")
                for i in range(2):
                    filled(dve, l, f"mu{i}")
                filled(dve, l, "mu1")
                for i in range(2):
                    o2 = oo[:, 2 * i:2 * i + 2, :].rearrange("p j t -> p (j t)")
                    drain(f"mu{i}", V.scalar_tensor_tensor(o2, mb(f"mu{i}")[:, :], -1.0 / 64, o2, ALU.mult, ALU.add))
                    m_done(dve, l, f"mu{i}")
                    q.add(marker(), S["cent"])
                side("mu", "va")
                m_done(dve, l, "va0")
                m_done(dve, l, "va1")
                va = tiles(8720, 4)
                q.step(V.reciprocal(va[:, :, :], va[:, :, :]))
                q.step(TT(oo[:, :, :], oo[:, :, :], va[:, :, :], ALU.mult))
                for j in range(4):
                    q.add(V.tensor_scalar(oo[:, j, :], oo[:, j, :], par(l, "ln_g", j), par(l, "ln_b", j), ALU.mult, ALU.add), v_seq)
                dve.wait_ge(v_seq, q.n[id(v_seq)])
                for i in range(2):
                    m_done(dve, l, f"bo{i}")
                    m_done(dve, l, f"cg{i}")
                q.step(TT(oo[:, :, :], oo[:, :, :], bv[:, :, :], ALU.add))
                q.step(TT(yC[:, :, :], oo[:, :, :], gg[:, :, :], ALU.mult), S["yc_ready"])

            def products(l, lo, hi):
                for n in range(2 * STEPS):
                    step, i = n // 2, n % 2
                    if lo < 4 * MERGE_CHUNKS.index((step, 2)) + 4 <= hi:
                        unit = ("pj", step, i)
                        dve.wait_ge(chunks_used, unit_chunk(l, unit) + 1)
                        g_done(dve, l, ("gate", step, i))
                        if n < 4:
                            two = mg[:, 2 * n:2 * n + 2, :]
                            q.add(TT(two, gb(unit)[:, :].rearrange("p (j t) -> p j t", j=2), sg_of(step, i).rearrange("p (j t) -> p j t", j=2),
                                     ALU.mult), g_drained[G_PLAN[unit][0]])
                        else:
                            q.add(TT(sg_of(step, i), gb(unit)[:, :], sg_of(step, i), ALU.mult), g_drained[G_PLAN[unit][0]])
                        g_done(dve, l, unit)
                        q.add(marker(), merged if n < 4 else S["gated"])

            def merge(l):
                products(l, SIDE_AT["va"][1], 12 * STEPS)
                for i in range(N_OUT):
                    unit = ("out", i)
                    dve.wait_ge(chunks_used, unit_chunk(l, unit) + 1)
                    x2 = x[:, 2 * i:2 * i + 2, :]
                    q.add(TT(x2, gb(unit)[:, :].rearrange("p (j t) -> p j t", j=2), x2, ALU.add), g_drained[G_PLAN[unit][0]])
                    g_done(dve, l, unit)
                    q.add(marker(), x_mixed)

            def z_low(l, n):
                dve.wait_ge(high_ready, l * (NS + N_FFN) + n + 1)
                slot = (chunk0(l) + n) % RING
                TT(ring_low[:, slot, :], ring[:, slot, :], w_high[:, n % 2, :], ALU.subtract).then_inc(low_ready, 1)

            def split_h(n):
                for i in range(4):
                    dve.wait_ge(S["h_split_high"], 4 * n + i + 1)
                    two = slice(2 * i, 2 * i + 2)
                    TT(h_low[:, two, :], h[:, two, :], h_high[:, two, :], ALU.subtract).then_inc(S["h_split"], 1)

            def low(n, i=0):
                dve.wait_ge(high_ready, i * (2 * RING) + (NS + n + 1))
                slot = (FFN0 + n) % RING
                TT(ring_low[:, slot, :], ring[:, slot, :], w_high[:, n % 2, :], ALU.subtract).then_inc(low_ready, 1)

            def dense():
                with dve.Fori(0, FT // (2 * RING)) as i:
                    for s in range(2 * RING):
                        low(s + 1, i)
                        n = i * (2 * RING) + s
                        dve.wait_ge(silu_done, n + 1)
                        if s:
                            dve.wait_ge(ffn_drained, n)
                        TT(gu_tmp, gbank[gbanks[s % RING]][:, T:2 * T], sil[:, s % RING, :], ALU.mult).then_inc(S["gu_part"], 1)
                        dve.wait_ge(S["gu_part"], n * 2 + 1)
                        V.tensor_copy(gu_high[:, n, :], gu_tmp).then_inc(S["gu_part"], 1)
                        dve.wait_ge(S["gu_part"], n * 2 + 2)
                        TT(gu_low[:, n, :], gu_tmp, gu_high[:, n, :], ALU.subtract).then_inc(ffn_drained, 1)
                for n in range(FT + 1, N_FFN):
                    low(n)
                dve.wait_ge(chunks_used, FFN0 + N_FFN)
                for i in range(4):
                    x2 = x[:, 2 * i:2 * i + 2, :]
                    TT(x2, mbank[i][:, :].rearrange("p (j t) -> p j t", j=2), x2, ALU.add).then_inc(ffn_drained, 1)
                dve.wait_ge(ffn_drained, FT + 4)

            def overflowed(e):
                done = e * (2 * GROUPS + 4) + (FT + 4)
                for g in range(GROUPS):
                    dve.wait_ge(chunks_used, e * N_FFN + (N_CHUNKS + 4 * g + 4))
                    for i in range(2):
                        dve.wait_ge(silu_done, e * (2 * GROUPS) + (FT + 2 * g + i + 1))
                        TT(gu[:, 4 * g + 2 * i:4 * g + 2 * i + 2, :], gbank[2 + i][:, :].rearrange("p (j t) -> p j t", j=2),
                           sil2[:, i, :].rearrange("p (j t) -> p j t", j=2), ALU.mult).then_inc(ffn_drained, 1)
                dve.wait_ge(chunks_used, e * N_FFN + (N_CHUNKS + N_FFN))
                m2 = moe_tmp.rearrange("p (j t) -> p j t", j=2)
                for i in range(4):
                    x2 = x[:, 2 * i:2 * i + 2, :]
                    dve.wait_ge(S["b_done"], e * 4 + (i + 1))
                    TT(m2, mbank[i][:, :].rearrange("p (j t) -> p j t", j=2), over(crow[:, e, :], 2), ALU.mult).then_inc(ffn_drained, 1)
                    dve.wait_ge(ffn_drained, done + (2 * GROUPS + i + 1))
                    TT(x2, m2, x2, ALU.add).then_inc(S["b_done"], 1)

            place_tok = small[:, 100:118].rearrange("p (c e) -> p c e", c=NCH)

            def put_tokens(e):
                for c in range(NCH):
                    ins = V.tensor_scalar(put[:, c, :], const("slots", CAP), place_tok[:, c, e:e + 1] if isinstance(e, int)
                                          else place_tok[:, c, bass.ds(e, 1)], None, ALU.is_equal)
                    ins.then_inc(S["put_ready"], 1)

            def gathered():
                for i in range(2):
                    TT(hg_low[:, 4 * i:4 * i + 4, :], mbank[i][:, 0:4 * CAP].rearrange("p (j s) -> p j s", j=4),
                       hg_high[:, 4 * i:4 * i + 4, :], ALU.subtract).then_inc(S["hg_ready"], 1)

            def give_back(e, lo):
                for i in (lo, lo + 1):
                    dve.wait_ge(S["back_filled"], e * 4 + (i + 1))
                    x2 = x[:, 2 * i:2 * i + 2, :]
                    TT(x2, mbank[i % 2][:, :].rearrange("p (j t) -> p j t", j=2), x2, ALU.add).then_inc(S["back_drained"], 1)

            def experts():
                for i in range(2):
                    V.memset(mbank[2 + i][0:CAP, :], 0.0).then_inc(S["zeroed"], 1)
                V.memset(back, 0.0).then_inc(S["back_ready"], 1)
                dve.wait_ge(S["hg_high_ready"], 2)
                gathered()
                with dve.Fori(0, E) as e:
                    groups = e * GROUPS
                    for n in range(N_FFN):
                        dve.wait_ge(high_ready, e * N_FFN + (L * NS + N_FFN + n + 1))
                        slot = (MOE0 + n) % RING
                        TT(ring_low[:, slot, :], ring[:, slot, :], we_high[n % 3][:, :], ALU.subtract).then_inc(low_ready, 1)
                        if n == 0:
                            put_tokens(e + 1)
                        if n == 4:
                            give_back(e, 0)
                        if n == 6:
                            give_back(e, 2)
                            V.scalar_tensor_tensor(back, prow[0:CAP, e, :], cc[0:CAP, CC["slot"]:CC["slot"] + 1], crow[0:CAP, e, :],
                                                   ALU.is_equal, ALU.mult).then_inc(S["back_ready"], 1)
                        if n >= 6 and (n - 6) % 4 == 0 and n <= 30:
                            g = (n - 6) // 4
                            dve.wait_ge(chunks_used, e * N_FFN + (MOE0 + 4 * g + 4))
                            dve.wait_ge(S["silu_tok"], groups + (g + 1))
                            dve.wait_ge(S["hid_turned"], groups + max(g - 1, 0))
                            TT(hid_tok[:, g % 2, :], gbank[2 * (g % 2) + 1][0:CAP, :], sil_tok[:, g % 2, :], ALU.mult)\
                                .then_inc(S["hid_ready"], 1)
                        if n >= 10 and (n - 10) % 4 == 0 and n <= 34:
                            g = (n - 10) // 4
                            dve.wait_ge(S["eu_high_ready"], groups + (g + 1))
                            TT(eu_low[:, 4 * g:4 * g + 4, :], mbank[g % 2][:, 0:4 * CAP].rearrange("p (j s) -> p j s", j=4),
                               eu_high[:, 4 * g:4 * g + 4, :], ALU.subtract).then_inc(S["eu_ready"], 1)
                        if n == 40:
                            dve.wait_ge(S["hg_high_ready"], e * 2 + 4)
                            gathered()
                give_back(E, 0)
                give_back(E, 2)

            def router():
                dve.wait_ge(m_filled[1], L * M_TOTAL[1] + 1)
                r3 = lambda i: rt[:, 16 * i:16 * i + 16].rearrange("p (c e) -> p c e", c=NCH)
                comb, lg, eq, cum, first1, first2 = (r3(i) for i in range(6))
                v1, v2, dd = small[:, 32:34], small[:, 34:36], small[:, 36:38]
                p1, p2_ = small[:, 40:42], small[:, 42:44]
                q.step(V.tensor_copy(rt[:, 16:32], mbank[1][:, 0:16]))

                def pick(top, chosen):
                    q.step(V.tensor_reduce(top, lg, AX_X, ALU.max))
                    for c in range(NCH):
                        q.step(V.tensor_scalar(eq[:, c, :], lg[:, c, :], top[:, c:c + 1], None, ALU.is_equal))
                        q.step(V.tensor_tensor_scan(cum[:, c, :], const("ones", E), eq[:, c, :], 0.0, ALU.mult, ALU.add))
                    q.step(V.scalar_tensor_tensor(chosen, cum, 1.0, eq, ALU.is_equal, ALU.mult))

                pick(v1, first1)
                q.step(V.scalar_tensor_tensor(lg, first1, -3.0e38, lg, ALU.mult, ALU.add))
                pick(v2, first2)
                q.step(TT(dd, v1, v2, ALU.subtract), S["logits_top"])
                dve.wait_ge(S["probs"], 1)
                for c in range(NCH):
                    q.step(V.tensor_scalar(comb[:, c, :], first1[:, c, :], p1[:, c:c + 1], None, ALU.mult))
                    q.step(V.scalar_tensor_tensor(comb[:, c, :], first2[:, c, :], p2_[:, c:c + 1], comb[:, c, :], ALU.mult, ALU.add),
                           S["comb_ready"] if c else None)
                dve.wait_ge(m_filled[2], L * M_TOTAL[2] + 1)
                comb_t, chosen, count, place = (routeT[:, i, :] for i in range(4))
                q.step(V.tensor_copy(comb_t, mbank[2][0:E, 0:T]))
                q.step(V.tensor_scalar(chosen, comb_t, 0.0, None, ALU.is_gt))
                q.step(V.tensor_tensor_scan(count, cc[0:E, CC["ones"]:CC["ones"] + T], chosen, 0.0, ALU.mult, ALU.add))
                q.step(TT(count, count, chosen, ALU.mult))
                q.step(V.tensor_scalar(place, count, -1.0, None, ALU.add), S["places"])
                q.step(V.memset(small[:, 100:118], -1.0))
                dve.wait_ge(S["tok_done"], 1)
                q.step(V.tensor_copy(place_tok[:, :, 0:E], mbank[2][:, 256:256 + 2 * E].rearrange("p (c e) -> p c e", c=NCH)))
                put_tokens(0)
                dve.wait_ge(S["combs_done"], 1)
                for i in range(4):
                    ins = V.tensor_copy(crow[:, 2 * i:2 * i + 2, :], gbank[i][:, :].rearrange("p (j t) -> p j t", j=2))
                    (q.step(ins) if i < 3 else q.step(ins, S["crow_ready"]))
                dve.wait_ge(S["rows_done"], 1)
                for i in range(4):
                    q.step(V.tensor_copy(prow[:, 2 * i:2 * i + 2, :], gbank[i][:, :].rearrange("p (j t) -> p j t", j=2)))
                q.step(V.tensor_reduce(small[:, 80:81], prow.rearrange("p e t -> p (e t)"), AX_X, ALU.max))
                q.step(V.tensor_scalar(small[:, 80:81], small[:, 80:81], CAP - 0.5, None, ALU.is_gt))
                q.step(V.tensor_copy(flag[:, 0:1], small[:, 80:81]), S["flag_ready"])

            for l in range(L):
                z_low(l, 0)
                norm(lambda: m_done(dve, l, "norm1"), lambda k: par(l, "norm_mix", k), h_ready)
                dve.wait_ge(h_ready, 2 * DT * l + DT)
                split_h(2 * l)
                for n in range(1, 8):
                    z_low(l, n)
                dve.wait_ge(all_consts_in, 16)
                mixer_d_dt(l)
                mixer_d_conv(l)
                mixer_d_decay(l)
                mixer_d(l)
                mixer_a(l)
                mixer_c(l)
                merge(l)
                if l == 0:
                    low(0)
                norm(lambda: m_done(dve, l, "norm2"), lambda k: par(l, "norm_ffn", k), h_ready)
                if l == 0:
                    split_h(1)
                    dense()
                    for _ in range(4):
                        q.step(marker(), S["ffn_x"])
                else:
                    router()
                    experts()
                    overflow = dve.value_load(flag[0:1, 0:1], min_val=0, max_val=1)
                    dve.wait_ge(S["back_drained"], 4 * E + 4)
                    q.step(marker(), S["b_done"])
                    with dve.If(overflow > 0):
                        V.scalar_tensor_tensor(crow.rearrange("p e t -> p (e t)"), prow.rearrange("p e t -> p (e t)"), CAP - 0.5,
                                               crow.rearrange("p e t -> p (e t)"), ALU.is_gt, ALU.mult).then_inc(S["back_ready"], 1)
                        dve.wait_ge(S["back_ready"], E + 2)
                        with dve.Fori(0, E) as e:
                            overflowed(e)
                        dve.wait_ge(S["b_done"], 4 * E + 1)
                    for _ in range(4):
                        q.step(marker(), S["ffn_x"])
            dve.wait_ge(m_drained[0], L * M_TOTAL[0] + 1)
            q.step(V.reciprocal(rstd[:, :], rms[:, :]))
            for k in range(DT):
                q.add(V.scalar_tensor_tensor(h[:, k, :], x[:, k, :], par(0, "norm_final", k), rstd[:, :], ALU.mult, ALU.mult), S["out_ready"])


def kernel(x, norm_mix_g, w_in, a_ln_g, a_ln_b, a_w_s, a_b_s, b_w_pool, b_scale, c_mix, c_w0, c_w2, c_a0, c_a2, c_g2,
           c_k_k, c_k_a, c_r_k, c_ln_g, c_ln_b, d_conv_w, d_conv_b, d_dt_bias, d_a_log, d_skip, d_norm_g,
           w_branch, w_out, norm_ffn_g, ffn_w_gate, ffn_w_up, ffn_w_down, moe_router, moe_w_gate, moe_w_up, moe_w_down,
           norm_final_g):
    import numpy as np
    import concourse.bacc as bacc
    from concourse.bass_utils import run_bass_kernel_spmd

    f = lambda a: np.asarray(a)

    def col_tiles(w):
        k, n = w.shape
        return w.reshape(k // P, P, n // P, P).transpose(2, 1, 0, 3).reshape(n // P, P, k)

    def pairs(t):
        return t.reshape(-1, 2, P, D).transpose(0, 2, 1, 3).reshape(-1, P, CW)

    def swiglu_chunks(wg, wu, wd):
        g, up = col_tiles(wg), col_tiles(wu)
        hidden = np.stack([g, up], 1).transpose(0, 2, 1, 3).reshape(FT, P, CW)
        return [hidden, wd.reshape(N_DOWN, 2, P, D).transpose(0, 2, 1, 3).reshape(N_DOWN, P, CW)]

    def expert_chunks(wg, wu, wd):
        k_major = lambda w: w.reshape(2, 4, P, GROUPS, 512).transpose(3, 0, 2, 1, 4).reshape(GROUPS, 2, P, CW)
        hidden = np.concatenate([k_major(wg), k_major(wu)], 1).reshape(N_GU, P, CW)
        return [hidden, wd.reshape(N_DOWN, 2, P, D).transpose(0, 2, 1, 3).reshape(N_DOWN, P, CW)]

    def mixer_chunks(l):
        w = f(w_in)[l]
        v = w[:, 512:1024].reshape(2, 4, P, 512).transpose(0, 2, 1, 3).reshape(2, P, CW)
        gates = pairs(col_tiles(w[:, 4872:8968])).reshape(4, 2, 2, P, CW)[MERGE_ORDER].reshape(STEPS, 2, P, CW)
        branch = f(w_branch)[l].reshape(4, 4, P, 2, 4, P).transpose(0, 3, 2, 4, 1, 5)[MERGE_ORDER].reshape(STEPS, 1, P, CW)
        return [pairs(col_tiles(w[:, 3328:3840])), pairs(col_tiles(w[:, 3840:4864])), v, pairs(col_tiles(w[:, 0:512])),
                pairs(col_tiles(w[:, 1024:1536])), pairs(col_tiles(w[:, 1536:3328])),
                np.concatenate([gates, branch], 1).reshape(N_MERGE, P, CW)[[3 * s + u for s, u in MERGE_CHUNKS]], pairs(col_tiles(f(w_out)[l]))]

    parts = mixer_chunks(0) + swiglu_chunks(f(ffn_w_gate)[0], f(ffn_w_up)[0], f(ffn_w_down)[0]) + mixer_chunks(1)
    for e in range(E):
        parts += expert_chunks(f(moe_w_gate)[0, e], f(moe_w_up)[0, e], f(moe_w_down)[0, e])
    stream = np.concatenate(parts, 0)
    assert stream.shape == (N_CHUNKS, P, CW)

    def cols(a):
        return f(a).reshape(-1, P).T

    pp = np.zeros((P, L, NPP), np.float32)
    for l in range(L):
        put = {"norm_mix": cols(f(norm_mix_g)[l]), "norm_ffn": cols(f(norm_ffn_g)[l]), "mix": cols(f(c_mix)[l]), "w0": cols(f(c_w0)[l]),
               "a0": cols(f(c_a0)[l]), "k_k": cols(f(c_k_k)[l]), "k_a": cols(f(c_k_a)[l]), "r_k": cols(f(c_r_k)[l]),
               "ln_g": cols(f(c_ln_g)[l]), "ln_b": cols(f(c_ln_b)[l]), "conv_w": cols(f(d_conv_w)[l]), "conv_b": cols(f(d_conv_b)[l]),
               "norm_d": cols(f(d_norm_g)[l]), "skip": cols(np.repeat(f(d_skip)[l], 64)), "b_scale": cols(f(b_scale)[l]),
               "norm_final": cols(norm_final_g)}
        for name, a in put.items():
            pp[:, l, PP[name]:PP[name] + a.shape[1]] = a
        pp[0:H, l, PP["dt_bias"]] = f(d_dt_bias)[l]
        pp[0:H, l, PP["a_log"]] = f(d_a_log)[l]

    sw = np.zeros((L, P, NSW), np.float32)
    rep = np.zeros((L, P, NREP), np.float32)
    for l in range(L):
        put = {"w_s": f(a_w_s)[l].transpose(2, 0, 1).reshape(P, 512), "pool": f(b_w_pool)[l].transpose(1, 0, 2).reshape(P, 512),
               "w2a2": np.concatenate([f(c_w2)[l], f(c_a2)[l]], 0), "g2": f(c_g2)[l],
               "dt": f(w_in)[l][:, 4864:4872].reshape(DT, P, H).transpose(1, 0, 2).reshape(P, DT * H)}
        if l == 1:
            put["router"] = f(moe_router)[0].reshape(DT, P, E).transpose(1, 0, 2).reshape(P, DT * E)
        for name, a in put.items():
            sw[l, :, SW[name]:SW[name] + a.shape[1]] = a
        rep[l, :, 0:512] = f(a_ln_g)[l]
        rep[l, :, 512:1024] = f(a_ln_b)[l]
        rep[l, :, 1024:1536] = f(a_b_s)[l].reshape(512)

    i, j = np.arange(P)[:, None], np.arange(P)[None, :]
    t = np.arange(T)
    off = [((i // (2 * m) == j // (2 * m)) & (i // m != j // m)) for m in (2, 4, 8, 16, 32, 64)]
    put = {"ident": i == j, "ones": np.ones((P, T)), "heads": i // 64 == j // 64, "strict_up": i < j, "incl_up": i <= j,
           "low2": (i > j) & (i // 2 == j // 2), "up2": (i < j) & (i // 2 == j // 2), "off": np.concatenate(off, 1),
           "count": np.tile(np.concatenate([1.0 / np.minimum(t + 1, w) for w in (2, 4, 8, 16)]), (P, 1)),
           "reset": np.tile((np.arange(4 * T) % P != 0), (P, 1)),
           "sel": np.concatenate([np.repeat(i == hd, P, 1) for hd in range(H)], 1),
           "eps": np.full((P, 1), EPS), "gn_eps": np.full((P, 1), GN_EPS),
           "slots": np.tile(np.arange(CAP), (P, 1)), "slot": np.arange(P)[:, None]}
    cc = np.zeros((P, NCC), np.float32)
    for name, a in put.items():
        cc[:, CC[name]:CC[name] + a.shape[1]] = a

    xt = np.ascontiguousarray(f(x)[0].T.reshape(DT, P, T).transpose(1, 0, 2))
    nc = bacc.Bacc("TRN2", target_bir_lowering=False, num_devices=1,
                   dynamic_dma_scratch_size=3 * 1024)
    arrays, args = {}, []
    for name, a in (("x_in", xt), ("stream", stream), ("pp_in", pp), ("cc_in", cc), ("sw_in", sw), ("rep_in", rep)):
        arrays[name] = a
        args.append(nc.dram_tensor(name, a.shape, F32, kind="ExternalInput").ap())
    args.append(nc.dram_tensor("out", (P, DT, T), F32, kind="ExternalOutput").ap())
    trunk(nc, *args)
    r = run_bass_kernel_spmd(nc, [arrays], core_ids=[0])
    got = np.asarray(r.results[0]["out"])
    return np.ascontiguousarray(got.transpose(1, 0, 2).reshape(D, T).T)[None]
```
